# Optimizing a Trainium2 kernel written in Bass

```python
import jax, jax.numpy as jnp
from jax import lax
import numpy as np

D_MODEL = 1024
BATCH = 1
SEQ = 512
DEPTH = 2

HEAD_DIM = 64
D_FF = 2816
D_PLE = 256
ATTN_Q_HEADS = 8
ATTN_KV_HEADS = 2
ATTN_GROUP = ATTN_Q_HEADS // ATTN_KV_HEADS
WINDOW = 128
ROPE_THETA = 500000.0
ROPE_DIM = HEAD_DIM // 4
MLSTM_HEADS = 4
MLSTM_CHUNK = 64
MLSTM_CONV = 4
GATE_CAP = 15.0
RWKV_HEADS = 4
RWKV_W_RANK = 64
RWKV_A_RANK = 64
RWKV_G_RANK = 128
RWKV_GN_EPS = 64e-5
NORM_EPS = 1e-6
NEG_INF = -1e30

ATTN_W = ATTN_Q_HEADS * HEAD_DIM
KV_W = ATTN_KV_HEADS * HEAD_DIM
MLSTM_W = MLSTM_HEADS * HEAD_DIM
RWKV_W = RWKV_HEADS * HEAD_DIM
D_MIX = ATTN_W + MLSTM_W + RWKV_W
ATTN_COLS = ATTN_W + 2 * KV_W
MLSTM_COLS = 4 * MLSTM_W + 2 * MLSTM_HEADS
RWKV_COLS = 3 * RWKV_W + RWKV_W_RANK + RWKV_A_RANK + RWKV_G_RANK
D_IN = ATTN_COLS + MLSTM_COLS + RWKV_COLS


def rms_norm(x, gain):
    xf = x.astype(jnp.float32)
    y = xf * lax.rsqrt(jnp.mean(xf * xf, axis=-1, keepdims=True) + NORM_EPS)
    return (y * gain.astype(jnp.float32)).astype(x.dtype)

def swiglu(x, w_in, w_out):
    gate, up = jnp.split(x @ w_in, 2, axis=-1)
    return (jax.nn.silu(gate) * up) @ w_out

def rope_tables(positions):
    inv_freq = ROPE_THETA ** (-jnp.arange(0, ROPE_DIM, 2, dtype=jnp.float32) / ROPE_DIM)
    ang = positions.astype(jnp.float32)[..., None] * inv_freq
    return jnp.cos(ang)[:, :, None, :], jnp.sin(ang)[:, :, None, :]

def partial_rope(x, cos, sin):
    half = ROPE_DIM // 2
    x1 = x[..., :half].astype(jnp.float32)
    x2 = x[..., half:ROPE_DIM].astype(jnp.float32)
    rot = jnp.concatenate([x1 * cos - x2 * sin, x2 * cos + x1 * sin], axis=-1).astype(x.dtype)
    return jnp.concatenate([rot, x[..., ROPE_DIM:]], axis=-1)

def sliding_window_gqa(q, k, v, sinks):
    B, S = q.shape[:2]
    nb = S // WINDOW
    qb = q.reshape(B, nb, WINDOW, ATTN_KV_HEADS, ATTN_GROUP, HEAD_DIM)

    def band_keys(t):
        tb = t.reshape(B, nb, WINDOW, ATTN_KV_HEADS, HEAD_DIM)
        prev = jnp.pad(tb[:, :-1], ((0, 0), (1, 0), (0, 0), (0, 0), (0, 0)))
        return jnp.concatenate([prev, tb], axis=2)

    kb, vb = band_keys(k), band_keys(v)
    scores = jnp.einsum('bnqhgd,bnkhd->bnhgqk', qb, kb).astype(jnp.float32) * (HEAD_DIM ** -0.5)
    qi = jnp.arange(WINDOW)[:, None]
    kj = jnp.arange(2 * WINDOW)[None, :]
    lag = qi + WINDOW - kj
    in_band = (lag >= 0) & (lag < WINDOW)
    blk = jnp.arange(nb)[:, None, None]
    valid = in_band[None] & ((blk > 0) | (kj >= WINDOW)[None])
    scores = jnp.where(valid[None, :, None, None], scores, NEG_INF)
    sink = jnp.broadcast_to(
        sinks.astype(jnp.float32).reshape(1, 1, ATTN_KV_HEADS, ATTN_GROUP, 1, 1),
        scores.shape[:-1] + (1,))
    probs = jax.nn.softmax(jnp.concatenate([scores, sink], axis=-1), axis=-1)[..., :-1]
    out = jnp.einsum('bnhgqk,bnkhd->bnqhgd', probs.astype(v.dtype), vb)
    return out.reshape(B, S, ATTN_W)

def causal_depthwise_conv(x, w):
    return lax.conv_general_dilated(
        x, w[:, None, :].astype(x.dtype), window_strides=(1,),
        padding=((w.shape[0] - 1, 0),), dimension_numbers=('NWC', 'WIO', 'NWC'),
        feature_group_count=x.shape[-1])

def mlstm_chunkwise(q, k, v, i_pre, f_pre):
    B, S, H, D = q.shape
    L = MLSTM_CHUNK
    nc = S // L

    def chunks(t):
        return jnp.moveaxis(t.reshape((B, nc, L, H) + t.shape[3:]), 3, 1)

    q = chunks(q * (D ** -0.5))
    k = chunks(k)
    v = chunks(v)
    ig = chunks(i_pre)
    g = jnp.cumsum(chunks(jax.nn.log_sigmoid(f_pre)), axis=-1)
    g_tot = g[..., -1]

    a = g_tot[..., None] - g + ig
    m_loc = jnp.max(a, axis=-1)
    w_loc = jnp.exp(a - m_loc[..., None])
    c_loc = jnp.einsum('bhcl,bhclv,bhclk->bhcvk', w_loc, v, k)
    n_loc = jnp.einsum('bhcl,bhclk->bhck', w_loc, k)

    def carry_state(state, xs):
        c, n, m = state
        gt, ml, cl, nl = xs
        m_new = jnp.maximum(gt + m, ml)
        s_old = jnp.exp(gt + m - m_new)
        s_loc = jnp.exp(ml - m_new)
        c_new = s_old[..., None, None] * c + s_loc[..., None, None] * cl
        n_new = s_old[..., None] * n + s_loc[..., None] * nl
        return (c_new, n_new, m_new), (c, n, m)

    init = (jnp.zeros((B, H, D, D), jnp.float32), jnp.zeros((B, H, D), jnp.float32),
            jnp.full((B, H), NEG_INF, jnp.float32))
    xs = tuple(jnp.moveaxis(t, 2, 0) for t in (g_tot, m_loc, c_loc, n_loc))
    _, (c_prev, n_prev, m_prev) = lax.scan(carry_state, init, xs)
    c_prev = jnp.moveaxis(c_prev, 0, 2)
    n_prev = jnp.moveaxis(n_prev, 0, 2)
    m_prev = jnp.moveaxis(m_prev, 0, 2)

    causal = jnp.tril(jnp.ones((L, L), dtype=bool))
    d_intra = jnp.where(causal, g[..., :, None] - g[..., None, :] + ig[..., None, :], NEG_INF)
    inter = g + m_prev[..., None]
    m_row = jnp.maximum(inter, jnp.max(d_intra, axis=-1))
    w_intra = jnp.exp(d_intra - m_row[..., None])
    w_inter = jnp.exp(inter - m_row)
    s = jnp.einsum('bhcld,bhcsd->bhcls', q, k) * w_intra
    num = (jnp.einsum('bhcls,bhcsv->bhclv', s, v)
           + w_inter[..., None] * jnp.einsum('bhcvk,bhclk->bhclv', c_prev, q))
    den = jnp.sum(s, axis=-1) + w_inter * jnp.einsum('bhck,bhclk->bhcl', n_prev, q)
    h = num / jnp.maximum(jnp.abs(den), jnp.exp(-m_row))[..., None]
    return jnp.moveaxis(h, 1, 3).reshape(B, S, H, D)

def rwkv7_scan(r, decay, k, v, a_vec, b_vec):
    B, S, H, D = r.shape

    def step(state, xs):
        r_t, w_t, k_t, v_t, a_t, b_t = xs
        sa = jnp.einsum('bhvk,bhk->bhv', state, a_t)
        state = (state * w_t[:, :, None, :] + sa[..., None] * b_t[:, :, None, :]
                 + v_t[..., None] * k_t[:, :, None, :])
        return state, jnp.einsum('bhvk,bhk->bhv', state, r_t)

    xs = tuple(jnp.moveaxis(t, 1, 0) for t in (r, decay, k, v, a_vec, b_vec))
    _, y = lax.scan(step, jnp.zeros((B, H, D, D), jnp.float32), xs)
    return jnp.moveaxis(y, 0, 1)

def rwkv7_time_mix(u, mu, w0, w_up, a0, a_up, g_up, k_k, k_a, r_k, ln_w, ln_b):
    f32 = jnp.float32
    B, S, _ = u.shape
    u = u.astype(f32)
    prev = jnp.pad(u[:, :-1], ((0, 0), (1, 0), (0, 0)))
    u = u + (prev - u) * mu.astype(f32)
    r, k, v, xw, xa, xg = jnp.split(
        u, [RWKV_W, 2 * RWKV_W, 3 * RWKV_W, 3 * RWKV_W + RWKV_W_RANK,
            3 * RWKV_W + RWKV_W_RANK + RWKV_A_RANK], axis=-1)
    log_w = -jax.nn.softplus(-(w0.astype(f32) + jnp.tanh(xw) @ w_up.astype(f32))) - 0.5
    decay = jnp.exp(-jnp.exp(log_w))
    a = jax.nn.sigmoid(a0.astype(f32) + xa @ a_up.astype(f32))
    g = jax.nn.sigmoid(xg) @ g_up.astype(f32)

    def heads(t):
        return t.reshape(B, S, RWKV_HEADS, HEAD_DIM)

    kk = heads(k * k_k.astype(f32))
    kk = kk * lax.rsqrt(jnp.maximum(jnp.sum(kk * kk, axis=-1, keepdims=True), 1e-24))
    k = k * (1.0 + (a - 1.0) * k_a.astype(f32))
    r_h, k_h, v_h, a_h = heads(r), heads(k), heads(v), heads(a)
    y = rwkv7_scan(r_h, heads(decay), k_h, v_h, -kk, kk * a_h)
    mean = jnp.mean(y, axis=-1, keepdims=True)
    var = jnp.mean(jnp.square(y - mean), axis=-1, keepdims=True)
    y = ((y - mean) * lax.rsqrt(var + RWKV_GN_EPS) * ln_w.astype(f32).reshape(RWKV_HEADS, HEAD_DIM)
         + ln_b.astype(f32).reshape(RWKV_HEADS, HEAD_DIM))
    y = y + jnp.sum(r_h * k_h * r_k.astype(f32), axis=-1, keepdims=True) * v_h
    return y.reshape(B, S, RWKV_W) * g

def token_mixing(h, cos, sin, w_in, attn_sinks, mlstm_conv, mlstm_i_bias, mlstm_f_bias, mlstm_norm,
                 rwkv_mu, rwkv_w0, rwkv_w_up, rwkv_a0, rwkv_a_up, rwkv_g_up, rwkv_k_k, rwkv_k_a,
                 rwkv_r_k, rwkv_ln_w, rwkv_ln_b, w_out):
    f32 = jnp.float32
    B, S, _ = h.shape
    proj = h @ w_in
    attn_p, mlstm_p, rwkv_p = jnp.split(proj, [ATTN_COLS, ATTN_COLS + MLSTM_COLS], axis=-1)

    q_at, k_at, v_at = jnp.split(attn_p, [ATTN_W, ATTN_W + KV_W], axis=-1)
    q_at = partial_rope(q_at.reshape(B, S, ATTN_Q_HEADS, HEAD_DIM), cos, sin)
    k_at = partial_rope(k_at.reshape(B, S, ATTN_KV_HEADS, HEAD_DIM), cos, sin)
    v_at = v_at.reshape(B, S, ATTN_KV_HEADS, HEAD_DIM)
    y_attn = sliding_window_gqa(q_at, k_at, v_at, attn_sinks)

    qk_m, v_m, o_m, i_m, f_m = jnp.split(
        mlstm_p, [2 * MLSTM_W, 3 * MLSTM_W, 4 * MLSTM_W, 4 * MLSTM_W + MLSTM_HEADS], axis=-1)
    qk_m = jax.nn.silu(causal_depthwise_conv(qk_m, mlstm_conv))
    q_m, k_m = jnp.split(qk_m, 2, axis=-1)

    def m_heads(t):
        return t.astype(f32).reshape(B, S, MLSTM_HEADS, HEAD_DIM)

    i_pre = GATE_CAP * jnp.tanh((i_m.astype(f32) + mlstm_i_bias.astype(f32)) / GATE_CAP)
    f_pre = GATE_CAP * jnp.tanh((f_m.astype(f32) + mlstm_f_bias.astype(f32)) / GATE_CAP)
    h_m = mlstm_chunkwise(m_heads(q_m), m_heads(k_m), m_heads(v_m), i_pre, f_pre)
    h_m = (h_m * lax.rsqrt(jnp.mean(h_m * h_m, axis=-1, keepdims=True) + NORM_EPS)
           * mlstm_norm.astype(f32).reshape(MLSTM_HEADS, HEAD_DIM))
    y_mlstm = jax.nn.sigmoid(o_m.astype(f32)) * h_m.reshape(B, S, MLSTM_W)

    y_rwkv = rwkv7_time_mix(rwkv_p, rwkv_mu, rwkv_w0, rwkv_w_up, rwkv_a0, rwkv_a_up, rwkv_g_up,
                            rwkv_k_k, rwkv_k_a, rwkv_r_k, rwkv_ln_w, rwkv_ln_b)

    y = jnp.concatenate([y_attn, y_mlstm.astype(h.dtype), y_rwkv.astype(h.dtype)], axis=-1)
    return y @ w_out

def first_inputs(seed: int = 0) -> dict:
    key = jax.random.key(seed)
    ks = iter(jax.random.split(key, 48))
    f32 = jnp.float32

    def normal(shape, scale):
        return scale * jax.random.normal(next(ks), shape, f32)

    def uniform(shape, lo, hi):
        return jax.random.uniform(next(ks), shape, f32, lo, hi)

    def gain(width):
        return 1.0 + normal((DEPTH, width), 0.05)

    x = normal((BATCH, SEQ, D_MODEL), 1.0)
    p = normal((DEPTH, BATCH, SEQ, D_PLE), 1.0)
    start = jax.random.randint(next(ks), (BATCH, 1), 0, 4096, jnp.int32)
    positions = start + jnp.arange(SEQ, dtype=jnp.int32)[None, :]
    return {
        'x': x,
        'p': p,
        'positions': positions,
        'ln_ffn1_pre': gain(D_MODEL),
        'ln_ffn1_post': gain(D_MODEL),
        'w_ffn1_in': normal((DEPTH, D_MODEL, 2 * D_FF), D_MODEL ** -0.5),
        'w_ffn1_out': normal((DEPTH, D_FF, D_MODEL), D_FF ** -0.5),
        'ln_mix_pre': gain(D_MODEL),
        'w_in': normal((DEPTH, D_MODEL, D_IN), D_MODEL ** -0.5),
        'attn_sinks': normal((DEPTH, ATTN_Q_HEADS), 0.5),
        'mlstm_conv': normal((DEPTH, MLSTM_CONV, 2 * MLSTM_W), MLSTM_CONV ** -0.5),
        'mlstm_i_bias': normal((DEPTH, MLSTM_HEADS), 0.1),
        'mlstm_f_bias': uniform((DEPTH, MLSTM_HEADS), 3.0, 6.0),
        'mlstm_norm': gain(MLSTM_W),
        'rwkv_mu': uniform((DEPTH, RWKV_COLS), 0.0, 1.0),
        'rwkv_w0': uniform((DEPTH, RWKV_W), -1.5, 0.5),
        'rwkv_w_up': normal((DEPTH, RWKV_W_RANK, RWKV_W), 0.1),
        'rwkv_a0': normal((DEPTH, RWKV_W), 0.1),
        'rwkv_a_up': normal((DEPTH, RWKV_A_RANK, RWKV_W), 0.5 * RWKV_A_RANK ** -0.5),
        'rwkv_g_up': normal((DEPTH, RWKV_G_RANK, RWKV_W), RWKV_G_RANK ** -0.5),
        'rwkv_k_k': 0.85 + normal((DEPTH, RWKV_W), 0.05),
        'rwkv_k_a': 1.0 + normal((DEPTH, RWKV_W), 0.05),
        'rwkv_r_k': normal((DEPTH, RWKV_HEADS, HEAD_DIM), 0.1),
        'rwkv_ln_w': gain(RWKV_W),
        'rwkv_ln_b': normal((DEPTH, RWKV_W), 0.01),
        'w_out': normal((DEPTH, D_MIX, D_MODEL), D_MIX ** -0.5),
        'ln_mix_post': gain(D_MODEL),
        'ln_ffn2_pre': gain(D_MODEL),
        'ln_ffn2_post': gain(D_MODEL),
        'w_ffn2_in': normal((DEPTH, D_MODEL, 2 * D_FF), D_MODEL ** -0.5),
        'w_ffn2_out': normal((DEPTH, D_FF, D_MODEL), D_FF ** -0.5),
        'ln_ple_pre': gain(D_MODEL),
        'w_ple_gate': normal((DEPTH, D_MODEL, D_MODEL), D_MODEL ** -0.5),
        'w_ple_proj': normal((DEPTH, D_PLE, D_MODEL), D_PLE ** -0.5),
        'ln_ple_post': gain(D_MODEL),
    }

def first_block(x, p, positions, ln_ffn1_pre, ln_ffn1_post, w_ffn1_in, w_ffn1_out, ln_mix_pre, w_in,
              attn_sinks, mlstm_conv, mlstm_i_bias, mlstm_f_bias, mlstm_norm, rwkv_mu, rwkv_w0,
              rwkv_w_up, rwkv_a0, rwkv_a_up, rwkv_g_up, rwkv_k_k, rwkv_k_a, rwkv_r_k, rwkv_ln_w,
              rwkv_ln_b, w_out, ln_mix_post, ln_ffn2_pre, ln_ffn2_post, w_ffn2_in, w_ffn2_out,
              ln_ple_pre, w_ple_gate, w_ple_proj, ln_ple_post):
    cos, sin = rope_tables(positions)
    for l in range(DEPTH):
        x = x + 0.5 * rms_norm(swiglu(rms_norm(x, ln_ffn1_pre[l]), w_ffn1_in[l], w_ffn1_out[l]),
                               ln_ffn1_post[l])
        mix = token_mixing(rms_norm(x, ln_mix_pre[l]), cos, sin, w_in[l], attn_sinks[l],
                           mlstm_conv[l], mlstm_i_bias[l], mlstm_f_bias[l], mlstm_norm[l],
                           rwkv_mu[l], rwkv_w0[l], rwkv_w_up[l], rwkv_a0[l], rwkv_a_up[l],
                           rwkv_g_up[l], rwkv_k_k[l], rwkv_k_a[l], rwkv_r_k[l], rwkv_ln_w[l],
                           rwkv_ln_b[l], w_out[l])
        x = x + rms_norm(mix, ln_mix_post[l])
        x = x + 0.5 * rms_norm(swiglu(rms_norm(x, ln_ffn2_pre[l]), w_ffn2_in[l], w_ffn2_out[l]),
                               ln_ffn2_post[l])
        gate = jax.nn.sigmoid(rms_norm(x, ln_ple_pre[l]) @ w_ple_gate[l])
        x = x + rms_norm(gate * (p[l] @ w_ple_proj[l]), ln_ple_post[l])
    return x


DEPTH_2 = 1

CHUNK = 64
MEM_LEN = 256
EPS = 1e-6
CONV_W = 4

GDN_HEADS = 4
GDN_DK = 128
GDN_DV = 128
GDN_QK = GDN_HEADS * GDN_DK
GDN_VD = GDN_HEADS * GDN_DV
LRU_DIM = D_MODEL // 2
LRU_BLOCKS = 8
LRU_BW = LRU_DIM // LRU_BLOCKS
LRU_C = 8.0
MIX_DIM = GDN_VD + LRU_DIM
IN_SPLITS = (3 * GDN_QK, GDN_VD, GDN_HEADS, GDN_HEADS, LRU_DIM, LRU_DIM)
IN_COLS = 3 * GDN_QK + GDN_VD + 2 * GDN_HEADS + 2 * LRU_DIM

XA_HEADS = 4
XA_DH = D_MODEL // XA_HEADS

PEER_HEADS = 8
PEER_NKEYS = 128
PEER_N = PEER_NKEYS * PEER_NKEYS
PEER_DQ = 256
PEER_DH = PEER_DQ // 2
PEER_TOPK = 16
PEER_BLOCK = 128


def rmsnorm(x, w):
    xf = x.astype(jnp.float32)
    y = xf * lax.rsqrt(jnp.mean(xf * xf, axis=-1, keepdims=True) + EPS)
    return (y * w.astype(jnp.float32)).astype(x.dtype)

def l2norm(x):
    return x * lax.rsqrt(jnp.sum(x * x, axis=-1, keepdims=True) + EPS)

def causal_dwconv(x, w, b=None):
    s = x.shape[1]
    xp = jnp.pad(x, ((0, 0), (CONV_W - 1, 0), (0, 0)))
    y = sum(xp[:, j:j + s] * w[j] for j in range(CONV_W))
    return y if b is None else y + b

def gated_delta_rule(q, k, v, g, beta):
    bsz, s, h, dk = q.shape
    dv = v.shape[-1]
    n = s // CHUNK
    f32 = jnp.float32
    q = l2norm(q.astype(f32)) * (dk ** -0.5)
    k = l2norm(k.astype(f32))
    v = v.astype(f32)

    def chunks(t):
        return t.reshape(bsz, n, CHUNK, h, -1).transpose(0, 3, 1, 2, 4)

    qc, kc, vc = chunks(q), chunks(k), chunks(v)
    gc = g.astype(f32).reshape(bsz, n, CHUNK, h).transpose(0, 3, 1, 2)
    bc = beta.astype(f32).reshape(bsz, n, CHUNK, h).transpose(0, 3, 1, 2)
    gcum = jnp.cumsum(gc, axis=-1)
    pos = jnp.arange(CHUNK)
    causal = pos[:, None] >= pos[None, :]
    strict = pos[:, None] > pos[None, :]
    decay = jnp.exp(jnp.where(causal, gcum[..., :, None] - gcum[..., None, :], -jnp.inf))
    kb = kc * bc[..., None]
    vb = vc * bc[..., None]
    a_mat = jnp.where(strict, jnp.einsum('bhncd,bhnsd->bhncs', kb, kc) * decay, 0.0)
    t_mat = a_mat + jnp.eye(CHUNK, dtype=f32)
    rhs = jnp.concatenate([vb, kb * jnp.exp(gcum)[..., None]], axis=-1)
    sol = lax.linalg.triangular_solve(t_mat, rhs, left_side=True, lower=True, unit_diagonal=True)
    u, w = sol[..., :dv], sol[..., dv:]
    attn = jnp.where(causal, jnp.einsum('bhncd,bhnsd->bhncs', qc, kc) * decay, 0.0)
    q_dec = qc * jnp.exp(gcum)[..., None]
    k_dec = kc * jnp.exp(gcum[..., -1:] - gcum)[..., None]
    chunk_decay = jnp.exp(gcum[..., -1])

    def step(state, xs):
        q_i, w_i, u_i, a_i, k_i, d_i = xs
        v_new = u_i - jnp.einsum('bhcd,bhdv->bhcv', w_i, state)
        o = jnp.einsum('bhcd,bhdv->bhcv', q_i, state) + jnp.einsum('bhcs,bhsv->bhcv', a_i, v_new)
        state = state * d_i[..., None, None] + jnp.einsum('bhcd,bhcv->bhdv', k_i, v_new)
        return state, o

    xs = tuple(jnp.moveaxis(t, 2, 0) for t in (q_dec, w, u, attn, k_dec, chunk_decay))
    state0 = jnp.zeros((bsz, h, dk, dv), f32)
    _, o = lax.scan(step, state0, xs)
    return o.transpose(1, 0, 3, 2, 4).reshape(bsz, s, h, dv)

def rg_lru(xr, w_a, b_a, w_x, b_x, lam):
    bsz, s, c = xr.shape
    f32 = jnp.float32
    xf = xr.astype(f32)
    xb = xf.reshape(bsz, s, LRU_BLOCKS, LRU_BW)
    r = jax.nn.sigmoid(jnp.einsum('bsgi,gij->bsgj', xb, w_a.astype(f32)).reshape(bsz, s, c) + b_a.astype(f32))
    i = jax.nn.sigmoid(jnp.einsum('bsgi,gij->bsgj', xb, w_x.astype(f32)).reshape(bsz, s, c) + b_x.astype(f32))
    log_a = -LRU_C * r * jax.nn.softplus(-lam.astype(f32))
    a = jnp.exp(log_a)
    b_term = jnp.sqrt(-jnp.expm1(2.0 * log_a)) * (i * xf)

    def combine(c1, c2):
        a1, b1 = c1
        a2, b2 = c2
        return a1 * a2, a2 * b1 + b2

    _, hs = lax.associative_scan(combine, (a, b_term), axis=1)
    return hs

def hybrid_mixer(h, w_in, conv_qkv_w, gdn_a_log, gdn_dt_bias, gdn_norm_w,
                 lru_conv_w, lru_conv_b, lru_wa, lru_ba, lru_wx, lru_bx, lru_lambda, w_out):
    bsz, s, _ = h.shape
    f32 = jnp.float32
    proj = h @ w_in
    offs = np.cumsum(IN_SPLITS)[:-1].tolist()
    qkv, z, a_in, b_in, xr, gate = jnp.split(proj, offs, axis=-1)
    qkv = jax.nn.silu(causal_dwconv(qkv, conv_qkv_w))
    q, k, v = jnp.split(qkv, [GDN_QK, 2 * GDN_QK], axis=-1)
    g = -jnp.exp(gdn_a_log.astype(f32)) * jax.nn.softplus(a_in.astype(f32) + gdn_dt_bias.astype(f32))
    beta = jax.nn.sigmoid(b_in.astype(f32))
    o = gated_delta_rule(q.reshape(bsz, s, GDN_HEADS, GDN_DK), k.reshape(bsz, s, GDN_HEADS, GDN_DK),
                         v.reshape(bsz, s, GDN_HEADS, GDN_DV), g, beta)
    o = rmsnorm(o, gdn_norm_w) * jax.nn.silu(z.reshape(bsz, s, GDN_HEADS, GDN_DV).astype(f32))
    y_gdn = o.reshape(bsz, s, GDN_VD).astype(h.dtype)
    xr = causal_dwconv(xr, lru_conv_w, lru_conv_b)
    y_lru = (rg_lru(xr, lru_wa, lru_ba, lru_wx, lru_bx, lru_lambda) * jax.nn.gelu(gate.astype(f32))).astype(h.dtype)
    return jnp.concatenate([y_gdn, y_lru], axis=-1) @ w_out

def memory_cross_attention(h, mem_n, wq, wkv, wo):
    bsz, s, _ = h.shape
    m = mem_n.shape[1]
    f32 = jnp.float32
    q = (h @ wq).reshape(bsz, s, XA_HEADS, XA_DH)
    kv = (mem_n @ wkv).reshape(bsz, m, 2, XA_HEADS, XA_DH)
    k, v = kv[:, :, 0], kv[:, :, 1]
    scores = jnp.einsum('bshd,bmhd->bhsm', q.astype(f32), k.astype(f32)) * (XA_DH ** -0.5)
    p = jax.nn.softmax(scores, axis=-1)
    o = jnp.einsum('bhsm,bmhd->bshd', p, v.astype(f32)).reshape(bsz, s, XA_HEADS * XA_DH).astype(h.dtype)
    return o @ wo

def peer_ffn(h, wq, subkeys, u_tab, v_tab):
    bsz, s, d = h.shape
    t = h.reshape(bsz * s, d)
    ntok = t.shape[0]
    f32 = jnp.float32
    q = (t @ wq).reshape(ntok, PEER_HEADS, 2, PEER_DH).astype(f32)
    sc = jnp.einsum('thpd,hpkd->thpk', q, subkeys.astype(f32))
    s1, i1 = lax.top_k(sc[:, :, 0], PEER_TOPK)
    s2, i2 = lax.top_k(sc[:, :, 1], PEER_TOPK)
    cand = (s1[..., :, None] + s2[..., None, :]).reshape(ntok, PEER_HEADS, PEER_TOPK * PEER_TOPK)
    best, pos = lax.top_k(cand, PEER_TOPK)
    e1 = jnp.take_along_axis(i1, pos // PEER_TOPK, axis=-1)
    e2 = jnp.take_along_axis(i2, pos % PEER_TOPK, axis=-1)
    idx = e1 * PEER_NKEYS + e2
    gate = jax.nn.softmax(best, axis=-1).astype(h.dtype)
    nb = ntok // PEER_BLOCK

    def block(args):
        tb, ib, gb = args
        act = jax.nn.gelu(jnp.einsum('phkd,pd->phk', u_tab[ib], tb)) * gb
        return jnp.einsum('phk,phkd->pd', act, v_tab[ib])

    out = lax.map(block, (t.reshape(nb, PEER_BLOCK, d),
                          idx.reshape(nb, PEER_BLOCK, PEER_HEADS, PEER_TOPK),
                          gate.reshape(nb, PEER_BLOCK, PEER_HEADS, PEER_TOPK)))
    return out.reshape(bsz, s, d)

def second_inputs(seed: int = 0) -> dict:
    key = jax.random.key(seed)
    ks = jax.random.split(key, 32)
    f32 = jnp.float32
    L = DEPTH_2

    def nrm(k, shape, scale):
        return jax.random.normal(k, shape, f32) * scale

    def gain(k, shape):
        return 1.0 + 0.05 * jax.random.normal(k, shape, f32)

    x = nrm(ks[0], (BATCH, SEQ, D_MODEL), 1.0)
    mem = nrm(ks[1], (BATCH, MEM_LEN, D_MODEL), 1.0)
    norm_mix_w = gain(ks[2], (L, D_MODEL))
    w_in = nrm(ks[3], (L, D_MODEL, IN_COLS), D_MODEL ** -0.5)
    conv_qkv_w = nrm(ks[4], (L, CONV_W, 3 * GDN_QK), 0.5)
    gdn_a_log = jnp.log(jax.random.uniform(ks[5], (L, GDN_HEADS), f32, 1.0, 16.0))
    dt = jnp.exp(jax.random.uniform(ks[6], (L, GDN_HEADS), f32, np.log(1e-3), np.log(1e-1)))
    gdn_dt_bias = dt + jnp.log(-jnp.expm1(-dt))
    gdn_norm_w = gain(ks[7], (L, GDN_DV))
    lru_conv_w = nrm(ks[8], (L, CONV_W, LRU_DIM), 0.5)
    lru_conv_b = nrm(ks[9], (L, LRU_DIM), 0.01)
    lru_wa = nrm(ks[10], (L, LRU_BLOCKS, LRU_BW, LRU_BW), LRU_BW ** -0.5)
    lru_ba = nrm(ks[11], (L, LRU_DIM), 0.01)
    lru_wx = nrm(ks[12], (L, LRU_BLOCKS, LRU_BW, LRU_BW), LRU_BW ** -0.5)
    lru_bx = nrm(ks[13], (L, LRU_DIM), 0.01)
    a0 = jax.random.uniform(ks[14], (L, LRU_DIM), f32, 0.9, 0.999)
    a_base = a0 ** (1.0 / LRU_C)
    lru_lambda = jnp.log(a_base) - jnp.log1p(-a_base)
    w_out = nrm(ks[15], (L, MIX_DIM, D_MODEL), MIX_DIM ** -0.5)
    norm_xattn_w = gain(ks[16], (L, D_MODEL))
    norm_mem_w = gain(ks[17], (L, D_MODEL))
    xattn_wq = nrm(ks[18], (L, D_MODEL, XA_HEADS * XA_DH), D_MODEL ** -0.5)
    xattn_wkv = nrm(ks[19], (L, D_MODEL, 2 * XA_HEADS * XA_DH), D_MODEL ** -0.5)
    xattn_wo = nrm(ks[20], (L, XA_HEADS * XA_DH, D_MODEL), (XA_HEADS * XA_DH) ** -0.5)
    norm_ffn_w = gain(ks[21], (L, D_MODEL))
    peer_wq = nrm(ks[22], (L, D_MODEL, PEER_HEADS * PEER_DQ), D_MODEL ** -0.5)
    peer_subkeys = nrm(ks[23], (L, PEER_HEADS, 2, PEER_NKEYS, PEER_DH), PEER_DH ** -0.5)
    peer_u = nrm(ks[24], (L, PEER_N, D_MODEL), D_MODEL ** -0.5)
    peer_v = nrm(ks[25], (L, PEER_N, D_MODEL), PEER_HEADS ** -0.5)
    norm_final_w = gain(ks[26], (D_MODEL,))
    return {'x': x, 'mem': mem, 'norm_mix_w': norm_mix_w, 'w_in': w_in, 'conv_qkv_w': conv_qkv_w,
            'gdn_a_log': gdn_a_log, 'gdn_dt_bias': gdn_dt_bias, 'gdn_norm_w': gdn_norm_w,
            'lru_conv_w': lru_conv_w, 'lru_conv_b': lru_conv_b, 'lru_wa': lru_wa, 'lru_ba': lru_ba,
            'lru_wx': lru_wx, 'lru_bx': lru_bx, 'lru_lambda': lru_lambda, 'w_out': w_out,
            'norm_xattn_w': norm_xattn_w, 'norm_mem_w': norm_mem_w, 'xattn_wq': xattn_wq,
            'xattn_wkv': xattn_wkv, 'xattn_wo': xattn_wo, 'norm_ffn_w': norm_ffn_w,
            'peer_wq': peer_wq, 'peer_subkeys': peer_subkeys, 'peer_u': peer_u, 'peer_v': peer_v,
            'norm_final_w': norm_final_w}

def second_block(x, mem, norm_mix_w, w_in, conv_qkv_w, gdn_a_log, gdn_dt_bias, gdn_norm_w,
              lru_conv_w, lru_conv_b, lru_wa, lru_ba, lru_wx, lru_bx, lru_lambda, w_out,
              norm_xattn_w, norm_mem_w, xattn_wq, xattn_wkv, xattn_wo, norm_ffn_w,
              peer_wq, peer_subkeys, peer_u, peer_v, norm_final_w):
    for l in range(DEPTH_2):
        x = x + hybrid_mixer(rmsnorm(x, norm_mix_w[l]), w_in[l], conv_qkv_w[l], gdn_a_log[l],
                             gdn_dt_bias[l], gdn_norm_w[l], lru_conv_w[l], lru_conv_b[l],
                             lru_wa[l], lru_ba[l], lru_wx[l], lru_bx[l], lru_lambda[l], w_out[l])
        x = x + memory_cross_attention(rmsnorm(x, norm_xattn_w[l]), rmsnorm(mem, norm_mem_w[l]),
                                       xattn_wq[l], xattn_wkv[l], xattn_wo[l])
        x = x + peer_ffn(rmsnorm(x, norm_ffn_w[l]), peer_wq[l], peer_subkeys[l], peer_u[l], peer_v[l])
    return rmsnorm(x, norm_final_w)


def setup_inputs(seed=0):
    out = dict(first_inputs(seed))
    for name, value in second_inputs(seed + 1).items():
        if name != "x":
            out[name + "_2"] = value
    return out


def reference(
    x, p, positions, ln_ffn1_pre, ln_ffn1_post, w_ffn1_in, w_ffn1_out, ln_mix_pre, w_in,
    attn_sinks, mlstm_conv, mlstm_i_bias, mlstm_f_bias, mlstm_norm, rwkv_mu, rwkv_w0, rwkv_w_up,
    rwkv_a0, rwkv_a_up, rwkv_g_up, rwkv_k_k, rwkv_k_a, rwkv_r_k, rwkv_ln_w, rwkv_ln_b, w_out,
    ln_mix_post, ln_ffn2_pre, ln_ffn2_post, w_ffn2_in, w_ffn2_out, ln_ple_pre, w_ple_gate,
    w_ple_proj, ln_ple_post, mem_2, norm_mix_w_2, w_in_2, conv_qkv_w_2, gdn_a_log_2,
    gdn_dt_bias_2, gdn_norm_w_2, lru_conv_w_2, lru_conv_b_2, lru_wa_2, lru_ba_2, lru_wx_2,
    lru_bx_2, lru_lambda_2, w_out_2, norm_xattn_w_2, norm_mem_w_2, xattn_wq_2, xattn_wkv_2,
    xattn_wo_2, norm_ffn_w_2, peer_wq_2, peer_subkeys_2, peer_u_2, peer_v_2, norm_final_w_2,
):
    x = first_block(
        x, p, positions, ln_ffn1_pre, ln_ffn1_post, w_ffn1_in, w_ffn1_out, ln_mix_pre, w_in,
        attn_sinks, mlstm_conv, mlstm_i_bias, mlstm_f_bias, mlstm_norm, rwkv_mu, rwkv_w0,
        rwkv_w_up, rwkv_a0, rwkv_a_up, rwkv_g_up, rwkv_k_k, rwkv_k_a, rwkv_r_k, rwkv_ln_w,
        rwkv_ln_b, w_out, ln_mix_post, ln_ffn2_pre, ln_ffn2_post, w_ffn2_in, w_ffn2_out,
        ln_ple_pre, w_ple_gate, w_ple_proj, ln_ple_post,
    )
    return second_block(
        x, mem_2, norm_mix_w_2, w_in_2, conv_qkv_w_2, gdn_a_log_2, gdn_dt_bias_2, gdn_norm_w_2,
        lru_conv_w_2, lru_conv_b_2, lru_wa_2, lru_ba_2, lru_wx_2, lru_bx_2, lru_lambda_2,
        w_out_2, norm_xattn_w_2, norm_mem_w_2, xattn_wq_2, xattn_wkv_2, xattn_wo_2,
        norm_ffn_w_2, peer_wq_2, peer_subkeys_2, peer_u_2, peer_v_2, norm_final_w_2,
    )


_drawn_inputs = setup_inputs


def setup_inputs(seed=0):
    import zlib

    import numpy as np

    out = dict(_drawn_inputs(seed))
    spreads = {}
    factors = {'attn_sinks': 5.179,
     'mlstm_i_bias': 8.0,
     'rwkv_k_k': 5.809,
     'rwkv_ln_b': 5.309,
     'ln_ple_pre': 3.303,
     'gdn_norm_w_2': 6.051,
     'lru_conv_b_2': 5.606,
     'lru_ba_2': 8.0,
     'lru_bx_2': 8.0,
     'norm_xattn_w_2': 8.0,
     'norm_mem_w_2': 8.0,
     'norm_ffn_w_2': 10.406}
    for name, (base, spread) in spreads.items():
        noise = np.random.default_rng([zlib.crc32(name.encode()), seed]).standard_normal(out[name].shape)
        drawn = base * np.exp(spread * noise) if base else spread * noise
        out[name] = __import__('jax').numpy.asarray(drawn.astype(out[name].dtype))
    for name, factor in factors.items():
        out[name] = (out[name] * factor).astype(out[name].dtype)
    return out
```

```python
import math
from contextlib import ExitStack, contextmanager

import concourse.bass as bass
from concourse import mybir

F32 = mybir.dt.float32
I32 = mybir.dt.int32
U32 = mybir.dt.uint32
ACT = mybir.ActivationFunctionType
ALU = mybir.AluOpType
AX = mybir.AxisListType

P = 128
D = 1024
DK = D // P
SEQ = 512
TT = SEQ // P
DEPTH = 2
EPS = 1e-6
NEG = -1e30

HD = 64
D_FF = 2816
FK = D_FF // P
D_PLE = 256
QH, KVH = 8, 2
ATTN_COLS = QH * HD + 2 * KVH * HD
MH, RH = 4, 4
ML_V = ATTN_COLS + 2 * MH * HD
ML_O = ML_V + MH * HD
ML_I = ML_O + MH * HD
ML_F = ML_I + MH
RW = ML_F + MH
D_IN = RW + 3 * RH * HD + 64 + 64 + 128
GATE_CAP = 15.0

COLS = {}
ROWS = {}


def lay(table, names):
    at = 0
    for name, width in names:
        table[name] = (at, at + width)
        at += width
    return at


NCOL = lay(COLS, [("ffn1_pre", 8), ("mix_pre", 8), ("ffn2_pre", 8), ("ple_pre", 8), ("conv", 16), ("mu", 8), ("w0", 2),
                  ("a0", 2), ("k_k", 2), ("k_a", 2), ("r_k", 2), ("i_bias", 1), ("f_bias", 1)])
NROW = lay(ROWS, [("ffn1_post", D), ("mix_post", D), ("ffn2_post", D), ("ple_post", D), ("mlstm_norm", 256),
                  ("ln_w", 256), ("ln_b", 256), ("sinks", 8)])

GH = 4
GQK = GH * P
G_Z = 3 * GQK
G_A = G_Z + GQK
G_B = G_A + GH
G_XR = G_B + GH
G_GATE = G_XR + 512
IN2 = G_GATE + 512
MEM = 256
XH = 4
PH = 8
NKEY = 128
TOPK = 16
COLS2 = {}
ROWS2 = {}
NCOL2 = lay(COLS2, [("mix", 8), ("xattn", 8), ("mem", 8), ("ffn", 8), ("conv_qkv", 48), ("conv_lru", 16), ("conv_b", 4),
                    ("ba", 4), ("bx", 4), ("lam", 4)])
NROW2 = lay(ROWS2, [("a_log", GH), ("dt_bias", GH), ("gdn_norm", P), ("ffn_row", D), ("final", D)])


def chain(engine, sem):
    done = [0]

    def link(instruction):
        done[0] += 1
        instruction.then_inc(sem, 1)
        engine.wait_ge(sem, done[0])

    return link


@contextmanager
def stage(nc, name, signals):
    with ExitStack() as s:
        sems = [s.enter_context(nc.semaphore(f"{name}_{x}")) for x in signals.split()]
        yield sems
        numbers = sorted(x.num for x in sems)
        first = numbers[0]
        for n, following in zip(numbers, numbers[1:] + [None]):
            if following != n + 1:
                nc.multi_engine_barrier(list(nc.engines), range(first, n + 1))
                first = following


class Arena:

    def __init__(self, region):
        self.region, self.at = region, 0

    def take(self, *shape, parts=P, dtype=F32):
        n = math.prod(shape)
        n += n % 2
        assert self.at + n <= self.region.shape[1], (self.at, n, self.region.shape)
        flat = self.region[0:parts, self.at:self.at + math.prod(shape)]
        self.at += n
        if dtype != F32:
            flat = flat.bitcast(dtype)
        if len(shape) == 1:
            return flat
        names = "abcde"[:len(shape)]
        return flat.rearrange(f"p ({' '.join(names)}) -> p {' '.join(names)}", **dict(zip(names, shape)))


def spread(ap, axis, n):
    v = ap.unsqueeze(axis)
    shape = list(v.shape)
    shape[axis] = n
    return v.broadcast_to(shape)


class Memory:
    pass



def constants(nc, m):
    def block_view(ap, b):
        return ap.rearrange("p (n b) -> p n b", b=b)

    with stage(nc, "const", "pool dve") as (pool_chain, dve_chain), nc.Block() as block:
        @block.gpsimd
        def _(pool):
            link = chain(pool, pool_chain)
            for ap in (m.ident, m.upper, m.strict_upper, m.strict_lower, *m.same.values(), m.ones):
                nc.gpsimd.memset(ap, 1.0)
            link(nc.gpsimd.memset(m.window, 0.0))

            def keep(ap, pattern, base, mult, fill=0.0, op=ALU.is_ge):
                link(nc.gpsimd.affine_select(out=ap, in_=ap, compare_op=op, fill=fill, base=base,
                                             pattern=pattern, channel_multiplier=mult))

            keep(m.ident, [[-1, P]], 0, 1, op=ALU.is_equal)
            keep(m.upper, [[1, P]], 0, -1)
            keep(m.strict_upper, [[1, P]], -1, -1)
            keep(m.strict_lower, [[-1, P]], -1, 1)
            for b, ap in m.same.items():
                keep(block_view(ap, b), [[-b, P // b], [0, b]], 0, 1)
                keep(block_view(ap, b), [[b, P // b], [0, b]], b - 1, -1)
            for n in range(2):
                keep(m.window[:, n, :], [[-1, 2 * P]], P, 1, fill=NEG)
                keep(m.window[:, n, :], [[1, 2 * P]], -1, -1, fill=NEG)
            keep(m.window[:, 0, :], [[1, 2 * P]], -P, 0, fill=NEG)
            link(nc.gpsimd.memset(m.pick, 1.0))
            keep(m.pick, [[-1, 4], [0, P]], 0, 1, op=ALU.is_equal)

        @block.vector
        def _(dve):
            dve.wait_ge(pool_chain, 6 + 2 * len(m.same) + 5 + 1)
            link = chain(dve, dve_chain)
            V = nc.vector
            for b, ap in m.merge.items():
                if 2 * b < P:
                    link(V.tensor_tensor(ap, m.same[2 * b], m.same[b], ALU.subtract))
                else:
                    link(V.tensor_scalar(ap, m.same[b], -1.0, 1.0, ALU.mult, ALU.add))
                link(V.tensor_tensor(ap, ap, m.strict_upper, ALU.mult))
            V.tensor_tensor(m.upper8, m.same[8], m.strict_upper, ALU.mult)
            V.tensor_tensor(m.lower8, m.same[8], m.strict_lower, ALU.mult)
            V.tensor_tensor(m.strict_upper64, m.same[64], m.strict_upper, ALU.mult)
            link(V.tensor_tensor(m.upper64, m.same[64], m.upper, ALU.mult))


def rope_tables(nc, m, positions):
    turn = [6.28125, 0.0019350051879882812, 3.019915981956753e-07]
    magic = 1.5 * 2.0 ** 23
    A = Arena(m.R)
    pos_i = A.take(TT, dtype=I32)
    pos, ang, k, mag = A.take(TT), A.take(TT, 8), A.take(TT, 8), A.take(TT, 8)
    with stage(nc, "rope", "loaded reduced dve") as (loaded, reduced, dve_chain), nc.Block() as block:
        @block.sync
        def _(sp):
            with nc.allow_non_contiguous_dma(reason="512 positions"):
                sp.dma_start(pos_i, positions).then_inc(loaded, 16)

        @block.vector
        def _(dve):
            link = chain(dve, dve_chain)
            V = nc.vector
            dve.wait_ge(loaded, 16)
            link(V.tensor_copy(pos, pos_i))
            for j in range(8):
                last = V.tensor_scalar(ang[:, :, j], pos, float(bass.np.float32(500000.0 ** (-j / 8))), None, ALU.mult)
            link(last)
            link(V.tensor_scalar(k, ang, 1.0 / (2 * math.pi), magic, ALU.mult, ALU.add))
            link(V.tensor_scalar(k, k, magic, None, ALU.subtract))
            for part in turn:
                link(V.scalar_tensor_tensor(ang, k, -part, ang, ALU.mult, ALU.add))
            link(V.tensor_scalar(ang, ang, 3.1415925, -3.1415925, ALU.min, ALU.max))
            link(V.scalar_tensor_tensor(mag, ang, -1.0, ang, ALU.mult, ALU.max))
            V.tensor_scalar(mag, mag, -1.0, math.pi / 2, ALU.mult, ALU.add).then_inc(reduced, 1)

        @block.scalar
        def _(act):
            act.wait_ge(reduced, 1)
            nc.scalar.activation(m.sin, ang, ACT.Sin)
            nc.scalar.activation(m.cos, mag, ACT.Sin)



def load_layer(nc, m, cols, rows, ncol, nrow):
    with stage(nc, "vectors", "loaded") as (loaded,), nc.Block() as block:
        @block.sync
        def _(sp):
            sp.dma_start(m.cols[:, 0:ncol], cols).then_inc(loaded, 16)
            sp.dma_start(m.rows[:, 0:nrow], rows.broadcast_to([P, nrow])).then_inc(loaded, 16)
            sp.wait_ge(loaded, 32)


def norm_transpose(nc, m, name, src, T, gain, dst, A):
    ssq, rstd = A.take(T), A.take(T)
    xn = A.take(T, D)
    junk = dst.rearrange("p a b -> p (a b)")
    with stage(nc, name, "squares mean root scaled turned dve") as (squares, mean, root, scaled, turned, dve_chain), \
            nc.Block() as block:
        @block.scalar
        def _(act):
            for t in range(T):
                nc.scalar.activation(junk[:, t * D:t * D + D], src[:, t, :], ACT.Square, accum_out=ssq[:, t:t + 1]).then_inc(squares, 1)
            act.wait_ge(mean, 1)
            nc.scalar.activation(rstd, ssq, ACT.Sqrt).then_inc(root, 1)
            for k in range(1, DK, 2):
                act.wait_ge(turned, k + 1)
                nc.scalar.activation(dst[:, k, :], m.PS[:, k, 0:P * T], ACT.Copy, scale=gain[:, k:k + 1])

        @block.vector
        def _(dve):
            link = chain(dve, dve_chain)
            V = nc.vector
            dve.wait_ge(squares, T)
            V.tensor_scalar(ssq, ssq, 1.0 / D, EPS, ALU.mult, ALU.add).then_inc(mean, 1)
            dve.wait_ge(root, 1)
            link(V.reciprocal(rstd, rstd))
            for t in range(T):
                V.tensor_scalar(xn[:, t, :], src[:, t, :], rstd[:, t:t + 1], None, ALU.mult).then_inc(scaled, 1)
            for k in range(0, DK, 2):
                dve.wait_ge(turned, k + 1)
                V.tensor_scalar(dst[:, k, :], m.PS[:, k, 0:P * T], gain[:, k:k + 1], None, ALU.mult)

        @block.tensor
        def _(pe):
            for k in range(DK):
                for t in range(T):
                    if k == 0:
                        pe.wait_ge(scaled, t + 1)
                    last = nc.tensor.transpose(m.PS[:, k, t * P:t * P + P], xn[:, t, k * P:k * P + P], m.ident)
                last.then_inc(turned, 1)


def post_norm_add(nc, m, name, y, gain, factor, A):
    ssq, rstd, junk = A.take(TT), A.take(TT), A.take(TT, D)
    with stage(nc, name, "squares mean root dve") as (squares, mean, root, dve_chain), nc.Block() as block:
        @block.scalar
        def _(act):
            for t in range(TT):
                nc.scalar.activation(junk[:, t], y[:, t, :], ACT.Square, accum_out=ssq[:, t:t + 1]).then_inc(squares, 1)
            act.wait_ge(mean, 1)
            nc.scalar.activation(rstd, ssq, ACT.Sqrt).then_inc(root, 1)

        @block.vector
        def _(dve):
            link = chain(dve, dve_chain)
            V = nc.vector
            dve.wait_ge(squares, TT)
            V.tensor_scalar(ssq, ssq, 1.0 / D, EPS, ALU.mult, ALU.add).then_inc(mean, 1)
            dve.wait_ge(root, 1)
            link(V.reciprocal(rstd, rstd))
            for t in range(TT):
                last = V.scalar_tensor_tensor(y[:, t, :], y[:, t, :], rstd[:, t:t + 1], gain, ALU.mult, ALU.mult)
            link(last)
            for t in range(TT):
                V.scalar_tensor_tensor(m.x[:, t, :], y[:, t, :], factor, m.x[:, t, :], ALU.mult, ALU.add)


def project_tokens(nc, m, name, acts, K, weight, N, out, ring, T=TT, func=ACT.Copy):
    chunks = [(c, min(512, N - c)) for c in range(0, N, 512)]
    slot = K * 512

    def w_slot(c, w):
        return ring[:, (c % 2) * slot:(c % 2) * slot + K * w].rearrange("p (k n) -> p k n", k=K)

    with stage(nc, name, "loaded_even loaded_odd product out_dve out_act") as \
            (loaded_even, loaded_odd, product, out_dve, out_act), nc.Block() as block:
        loaded = (loaded_even, loaded_odd)

        @block.sync
        def _(sp):
            for c, (at, w) in enumerate(chunks):
                if c >= 2:
                    sp.wait_ge(product, T * (c - 1))
                sp.dma_start(w_slot(c, w), weight[:, at:at + w].rearrange("(k p) n -> p k n", p=P)).then_inc(loaded[c % 2], 16)

        @block.tensor
        def _(pe):
            for c, (at, w) in enumerate(chunks):
                pe.wait_ge(loaded[c % 2], 16 * (c // 2 + 1))
                for t in range(T):
                    n = c * T + t
                    if n >= 8:
                        pe.wait_ge((out_dve, out_act)[n % 2], (n - 8) // 2 + 1)
                    for k in range(K):
                        last = nc.tensor.matmul(m.PS[:, n % 8, 0:w], acts[:, k, t * P:t * P + P], w_slot(c, w)[:, k, :],
                                                start=(k == 0), stop=(k == K - 1))
                    last.then_inc(product, 1)

        def tiles(parity):
            for c, (at, w) in enumerate(chunks):
                for t in range(T):
                    if (c * T + t) % 2 == parity:
                        yield c * T + t, out[:, t, at:at + w], m.PS[:, (c * T + t) % 8, 0:w]

        @block.vector
        def _(dve):
            for n, to, of in tiles(0):
                dve.wait_ge(product, n + 1)
                nc.vector.tensor_copy(to, of).then_inc(out_dve, 1)

        @block.scalar
        def _(act):
            for n, to, of in tiles(1):
                act.wait_ge(product, n + 1)
                nc.scalar.activation(to, of, ACT.Copy).then_inc(out_act, 1)


def project_features(nc, m, name, acts, K, weight, N, out, ring, n_tok):
    chunks = N // 512
    slot = K * 512

    def w_slot(c):
        return ring[:, (c % 2) * slot:(c % 2) * slot + slot].rearrange("p (k n) -> p k n", k=K)

    with stage(nc, name, "loaded_even loaded_odd product out_dve out_act") as \
            (loaded_even, loaded_odd, product, out_dve, out_act), nc.Block() as block:
        loaded = (loaded_even, loaded_odd)

        @block.sync
        def _(sp):
            for c in range(chunks):
                if c >= 2:
                    sp.wait_ge(product, 4 * (c - 1))
                sp.dma_start(w_slot(c), weight[:, c * 512:c * 512 + 512].rearrange("(k p) n -> p k n", p=P))\
                    .then_inc(loaded[c % 2], 16)

        @block.tensor
        def _(pe):
            for c in range(chunks):
                pe.wait_ge(loaded[c % 2], 16 * (c // 2 + 1))
                for j in range(4):
                    n = 4 * c + j
                    if n >= 8:
                        pe.wait_ge((out_dve, out_act)[n % 2], (n - 8) // 2 + 1)
                    for k in range(K):
                        last = nc.tensor.matmul(m.PS[:, n % 8, 0:n_tok], w_slot(c)[:, k, j * P:j * P + P], acts[:, k, 0:n_tok],
                                                start=(k == 0), stop=(k == K - 1))
                    last.then_inc(product, 1)

        @block.vector
        def _(dve):
            for n in range(0, 4 * chunks, 2):
                dve.wait_ge(product, n + 1)
                nc.vector.tensor_copy(out[:, n, :], m.PS[:, n % 8, 0:n_tok]).then_inc(out_dve, 1)

        @block.scalar
        def _(act):
            for n in range(1, 4 * chunks, 2):
                act.wait_ge(product, n + 1)
                nc.scalar.activation(out[:, n, :], m.PS[:, n % 8, 0:n_tok], ACT.Copy).then_inc(out_act, 1)


def turn_tiles(nc, m, name, src_of, K, dst):
    with stage(nc, name, "turned") as (turned,), nc.Block() as block:
        @block.tensor
        def _(pe):
            for k in range(K):
                for t in range(TT):
                    last = nc.tensor.transpose(m.PS[:, k, t * P:t * P + P], src_of(t, k), m.ident)
                last.then_inc(turned, 1)

        @block.vector
        def _(dve):
            for k in range(0, K, 2):
                dve.wait_ge(turned, k + 1)
                nc.vector.tensor_copy(dst[:, k, :], m.PS[:, k, :])

        @block.scalar
        def _(act):
            for k in range(1, K, 2):
                act.wait_ge(turned, k + 1)
                nc.scalar.activation(dst[:, k, :], m.PS[:, k, :], ACT.Copy)


def swiglu_up(nc, m, name, weight):
    acts = m.A[:, 0:FK * SEQ].rearrange("p (j n) -> p j n", j=FK)
    cols = weight.rearrange("(k p) (g n) -> p k g n", p=P, g=2)
    slots = [m.R[:, s * 2048:(s + 1) * 2048].rearrange("p (k g c) -> p k g c", k=DK, g=2) for s in range(2)]
    silus = [m.R[:, 4096 + s * SEQ:4096 + (s + 1) * SEQ] for s in range(2)]
    with stage(nc, name, "loaded_even loaded_odd product silu gated") as \
            (loaded_even, loaded_odd, product, silu, gated), nc.Block() as block:
        loaded = (loaded_even, loaded_odd)

        @block.sync
        def _(sp):
            def load(j, s):
                for g in range(2):
                    sp.dma_start(slots[s][:, :, g, :], cols[:, :, g, bass.ds(j * P, P)]).then_inc(loaded[s], 16)

            load(0, 0)
            load(1, 1)
            with sp.Fori(0, FK // 2 - 1) as i:
                for s in range(2):
                    sp.wait_ge(product, i * 2 + s + 1)
                    load(i * 2 + s + 2, s)

        @block.tensor
        def _(pe):
            def pair(i, first):
                for s in range(2):
                    pe.wait_ge(loaded[s], (i + 1) * 32)
                    if not first:
                        pe.wait_ge(gated, i * 2 + s - 1)
                    for g in range(2):
                        for k in range(DK):
                            last = nc.tensor.matmul(m.PS[:, 2 * s + g, :], slots[s][:, k, g, :], m.hT[:, k, :],
                                                    start=(k == 0), stop=(k == DK - 1))
                    last.then_inc(product, 1)

            pair(0, True)
            with pe.Fori(1, FK // 2) as i:
                pair(i, False)

        @block.scalar
        def _(act):
            def pair(i, first):
                for s in range(2):
                    act.wait_ge(product, i * 2 + s + 1)
                    if not first:
                        act.wait_ge(gated, i * 2 + s - 1)
                    nc.scalar.activation(silus[s], m.PS[:, 2 * s, :], ACT.Silu).then_inc(silu, 1)

            pair(0, True)
            with act.Fori(1, FK // 2) as i:
                pair(i, False)

        @block.vector
        def _(dve):
            with dve.Fori(0, FK // 2) as i:
                for s in range(2):
                    dve.wait_ge(silu, i * 2 + s + 1)
                    to = acts[:, bass.ds(i * 2 + s, 1), :].rearrange("p a n -> p (a n)")
                    nc.vector.tensor_tensor(to, silus[s], m.PS[:, 2 * s + 1, :], ALU.mult).then_inc(gated, 1)


def feed_forward(nc, m, name, w_in, w_out, pre, post):
    norm_transpose(nc, m, name + "_pre", m.x, TT, pre, m.hT, Arena(m.R))
    swiglu_up(nc, m, name + "_up", w_in)
    acts = m.A[:, 0:FK * SEQ].rearrange("p (j n) -> p j n", j=FK)
    project_tokens(nc, m, name + "_down", acts, FK, w_out, D, m.y, m.R)
    post_norm_add(nc, m, name + "_post", m.y, post, 0.5, Arena(m.R))



def attention(nc, m, proj, y, A):
    qT = A.take(QH // 2, SEQ)
    kT = A.take(KVH, P + SEQ)
    vp = A.take(TT + 1, KVH * HD)
    kdup = A.take(TT, KVH, 2, HD)
    S = A.take(QH, 2 * P)
    pT = A.take(2 * QH, P)
    tmp = A.take(4, TT, 10, 8)
    mx, es, den = A.take(QH), A.take(QH), A.take(QH)
    kq = ATTN_COLS - 2 * KVH * HD
    with stage(nc, "attn", "keys_dup turned_q turned_k dve scored shifted probs_act probs_turned turned_act turned_dve summed stored ready") as \
            (keys_dup, turned_q, turned_k, dve_chain, scored, shifted, probs, probs_turned, turned_act, turned_dve, summed,
             stored, ready), nc.Block() as block:
        by_parity = lambda ap: ap.rearrange("p (j a) -> p a j", a=2)
        in_order = lambda ap: ap.rearrange("p (a j) -> p a j", a=2)
        sinks = by_parity(m.row("sinks"))
        place = lambda h: (h % 2) * (QH // 2) + h // 2

        @block.vector
        def _(dve):
            link = chain(dve, dve_chain)
            V = nc.vector
            for t in range(TT):
                heads = proj[:, t, 0:10 * HD].rearrange("p (h d) -> p h d", d=HD)
                x1, x2 = heads[:, :, 0:8], heads[:, :, 8:16]
                cos, sin = spread(m.cos[:, t, :], 1, 10), spread(m.sin[:, t, :], 1, 10)
                V.tensor_tensor(tmp[:, 0, t], x1, cos, ALU.mult)
                V.tensor_tensor(tmp[:, 1, t], x2, sin, ALU.mult)
                V.tensor_tensor(tmp[:, 2, t], x2, cos, ALU.mult)
                link(V.tensor_tensor(tmp[:, 3, t], x1, sin, ALU.mult))
                V.tensor_tensor(x1, tmp[:, 0, t], tmp[:, 1, t], ALU.subtract)
                link(V.tensor_tensor(x2, tmp[:, 2, t], tmp[:, 3, t], ALU.add))
                for twice in range(2):
                    last = V.tensor_copy(kdup[:, t, :, twice, :],
                                         proj[:, t, kq:kq + KVH * HD].rearrange("p (h d) -> p h d", d=HD))
            last.then_inc(keys_dup, 1)
            V.memset(kT[:, :, 0:P], 0.0)
            V.memset(vp[:, 0, :], 0.0)
            V.tensor_copy(vp[:, 1:TT + 1, :], proj[:, :, kq + KVH * HD:ATTN_COLS])
            dve.wait_ge(turned_q, 1)
            V.tensor_scalar(qT, m.PS[:, 0:4, :], HD ** -0.5, None, ALU.mult)
            dve.wait_ge(turned_k, 1)
            V.tensor_copy(kT[:, :, P:P + SEQ], m.PS[:, 4:6, :]).then_inc(ready, 1)
            for n in range(TT):
                dve.wait_ge(scored, n + 1)
                if n:
                    dve.wait_ge(probs_turned, n)
                scores = m.PS[:, 0:4, :].rearrange("p b (h k) -> p (b h) k", h=2)
                link(V.tensor_tensor(S, scores, spread(m.window[:, min(n, 1), :], 1, QH), ALU.add))
                link(V.tensor_reduce(mx, S, AX.X, ALU.max))
                link(V.tensor_tensor(in_order(mx), in_order(mx), sinks, ALU.max))
                V.tensor_tensor(S, S, spread(mx, 2, 2 * P), ALU.subtract)
                V.tensor_tensor(in_order(es), sinks, in_order(mx), ALU.subtract).then_inc(shifted, 1)
                dve.wait_ge(probs, n + 1)
                link(V.tensor_reduce(den, S, AX.X, ALU.add))
                link(V.tensor_tensor(den, den, es, ALU.add))
                link(V.reciprocal(den, den))
                dve.wait_ge(probs_turned, n + 1)
                V.tensor_copy(pT[:, 0:QH, :], m.PS[:, 4:6, :].rearrange("p b (h k) -> p (b h) k", h=4)).then_inc(turned_dve, 1)
                dve.wait_ge(summed, n + 1)
                for a in range(2):
                    last = V.tensor_tensor(y[:, n, 0:QH * HD].rearrange("p (j a d) -> p a j d", a=2, d=HD)[:, a],
                                           m.PS[:, 0, :].rearrange("p (j a d) -> p a j d", a=2, d=HD)[:, a],
                                           spread(in_order(den)[:, a], 2, HD), ALU.mult)
                last.then_inc(stored, 1)

        @block.scalar
        def _(act):
            for n in range(TT):
                act.wait_ge(shifted, n + 1)
                nc.scalar.activation(es, es, ACT.Exp)
                nc.scalar.activation(S, S, ACT.Exp).then_inc(probs, 1)
                act.wait_ge(probs_turned, n + 1)
                nc.scalar.activation(pT[:, QH:2 * QH, :], m.PS[:, 6:8, :].rearrange("p b (h k) -> p (b h) k", h=4),
                                     ACT.Copy).then_inc(turned_act, 1)

        @block.tensor
        def _(pe):
            pe.wait_ge(keys_dup, 1)
            for j in range(QH // 2):
                for t in range(TT):
                    last = nc.tensor.transpose(m.PS[:, j, t * P:t * P + P], proj[:, t, j * P:j * P + P], m.ident)
            last.then_inc(turned_q, 1)
            for j in range(KVH):
                for t in range(TT):
                    last = nc.tensor.transpose(m.PS[:, 4 + j, t * P:t * P + P],
                                               kdup[:, t, j].rearrange("p a d -> p (a d)"), m.ident)
            last.then_inc(turned_k, 1)
            pe.wait_ge(ready, 1)
            for n in range(TT):
                if n:
                    pe.wait_ge(stored, n)
                for h in range(QH):
                    at = (h % 2) * HD
                    last = nc.tensor.matmul(m.PS[:, place(h) // 2, (place(h) % 2) * 2 * P:(place(h) % 2 + 1) * 2 * P],
                                            qT[at:at + HD, h // 2, n * P:n * P + P],
                                            kT[at:at + HD, h // (QH // KVH), n * P:n * P + 2 * P], start=True, stop=True)
                last.then_inc(scored, 1)
                pe.wait_ge(probs, n + 1)
                for h in range(QH):
                    for b in range(2):
                        i = 2 * h + b
                        last = nc.tensor.transpose(m.PS[:, 4 + i // 4, (i % 4) * P:(i % 4 + 1) * P],
                                                   S[:, place(h), b * P:b * P + P], m.ident)
                last.then_inc(probs_turned, 1)
                pe.wait_ge(turned_dve, n + 1)
                pe.wait_ge(turned_act, n + 1)
                for h in range(QH):
                    kv = h // (QH // KVH)
                    for b in range(2):
                        last = nc.tensor.matmul(m.PS[:, 0, h * HD:h * HD + HD], pT[:, 2 * h + b, :],
                                                vp[:, n + b, kv * HD:kv * HD + HD], start=(b == 0), stop=(b == 1))
                last.then_inc(summed, 1)



def log1p_series(link, V, e, z, z2, out):
    link(V.tensor_scalar(z2, e, 2.0, None, ALU.add))
    link(V.reciprocal(z2, z2))
    link(V.tensor_tensor(z, e, z2, ALU.mult))
    link(V.tensor_tensor(z2, z, z, ALU.mult))
    link(V.tensor_scalar(out, z2, 1.0 / 17, None, ALU.mult))
    for n in (15, 13, 11, 9, 7, 5, 3):
        link(V.scalar_tensor_tensor(out, out, 1.0 / n, z2, ALU.add, ALU.mult))
    link(V.tensor_scalar(out, out, 1.0, 2.0, ALU.add, ALU.mult))
    link(V.tensor_tensor(out, out, z, ALU.mult))


def mlstm(nc, m, proj, y, A):
    xc = A.take(4, 3 + SEQ)
    qk = A.take(4, SEQ)
    gates = A.take(11, SEQ, parts=4)
    I, F, E, Z, Z2, L, G, C, M, EM, ONE = (gates[:, j, :] for j in range(11))
    ccol, ecol = A.take(TT, MH), A.take(TT, MH)
    pairs = [(j, i) for j in range(TT) for i in range(j, TT)]
    start = [pairs.index((j, j)) for j in range(TT)]
    W = A.take(MH, len(pairs), P)
    va = A.take(TT, MH, HD + 1)
    num = A.take(TT, MH, HD)
    den, ms = A.take(TT, MH), A.take(TT, MH)
    og = A.take(TT, MH, HD)
    iT, fT = m.PS[0:4, 4, :], m.PS[0:4, 5, :]

    with stage(nc, "mlstm1", "turned tanh_in tanh_out abs_in exp_out dve conv rows cols bcast dist weights") as \
            (turned, tanh_in, tanh_out, abs_in, exp_out, dve_chain, conv_done, rows_done, cols_done, bcast, dist, weights), \
            nc.Block() as block:
        @block.tensor
        def _(pe):
            for t in range(TT):
                nc.tensor.transpose(m.PS[0:4, 4, t * P:t * P + P], proj[:, t, ML_I:ML_I + MH], m.ident)
            for t in range(TT):
                last = nc.tensor.transpose(m.PS[0:4, 5, t * P:t * P + P], proj[:, t, ML_F:ML_F + MH], m.ident)
            last.then_inc(turned, 1)
            for j in range(4):
                for t in range(TT):
                    last = nc.tensor.transpose(m.PS[:, j, t * P:t * P + P],
                                               proj[:, t, ATTN_COLS + j * P:ATTN_COLS + j * P + P], m.ident)
            last.then_inc(turned, 1)
            pe.wait_ge(rows_done, 1)
            for t in range(TT):
                nc.tensor.transpose(m.PS[:, 6, t * 4:t * 4 + 4], C[:, t * P:t * P + P], m.ident[0:4, 0:4])
            for t in range(TT):
                last = nc.tensor.transpose(m.PS[:, 7, t * 4:t * 4 + 4], EM[:, t * P:t * P + P], m.ident[0:4, 0:4])
            last.then_inc(cols_done, 1)
            pe.wait_ge(conv_done, 1)
            for h in range(MH):
                last = nc.tensor.matmul(m.PS[:, h, :], m.pick[:, h, :], M, start=True, stop=True)
            last.then_inc(bcast, 1)

        @block.scalar
        def _(act):
            act.wait_ge(tanh_in, 1)
            nc.scalar.activation(I, I, ACT.Tanh)
            nc.scalar.activation(F, F, ACT.Tanh).then_inc(tanh_out, 1)
            act.wait_ge(abs_in, 1)
            nc.scalar.activation(E, E, ACT.Exp, scale=-1.0).then_inc(exp_out, 1)
            act.wait_ge(abs_in, 2)
            nc.scalar.activation(EM, EM, ACT.Exp, scale=-1.0).then_inc(rows_done, 1)
            act.wait_ge(dist, 1)
            nc.scalar.activation(W, W, ACT.Exp, scale=-1.0).then_inc(weights, 1)
            act.wait_ge(conv_done, 2)
            nc.scalar.activation(qk, qk, ACT.Silu)
            nc.scalar.activation(og, proj[:, :, ML_O:ML_O + MH * HD].rearrange("p t (h d) -> p t h d", d=HD), ACT.Sigmoid)

        @block.vector
        def _(dve):
            link = chain(dve, dve_chain)
            V = nc.vector
            dve.wait_ge(turned, 1)
            V.tensor_scalar(I, iT, m.col("i_bias")[0:4], 1 / GATE_CAP, ALU.add, ALU.mult)
            V.tensor_scalar(F, fT, m.col("f_bias")[0:4], 1 / GATE_CAP, ALU.add, ALU.mult).then_inc(tanh_in, 1)
            V.memset(ONE, 1.0)
            V.memset(xc[:, :, 0:3], 0.0)
            V.memset(va[:, :, :, HD:HD + 1], 1.0)
            V.tensor_copy(va[:, :, :, 0:HD], proj[:, :, ML_V:ML_V + MH * HD].rearrange("p t (h d) -> p t h d", d=HD))
            dve.wait_ge(turned, 2)
            V.tensor_copy(xc[:, :, 3:3 + SEQ], m.PS[:, 0:4, :]).then_inc(conv_done, 1)
            dve.wait_ge(tanh_out, 1)
            V.tensor_scalar(I, I, GATE_CAP, None, ALU.mult)
            link(V.tensor_scalar(F, F, GATE_CAP, None, ALU.mult))
            V.scalar_tensor_tensor(E, F, -1.0, F, ALU.mult, ALU.max).then_inc(abs_in, 1)
            dve.wait_ge(exp_out, 1)
            log1p_series(link, V, E, Z, Z2, L)
            link(V.scalar_tensor_tensor(L, F, 0.0, L, ALU.min, ALU.subtract))
            link(V.tensor_tensor_scan(G, ONE, L, 0.0, ALU.mult, ALU.add))
            link(V.tensor_tensor(C, I, G, ALU.subtract))
            link(V.tensor_tensor_scan(M, ONE, C, NEG, ALU.mult, ALU.max))
            V.tensor_tensor(EM, G, M, ALU.add).then_inc(abs_in, 1)
            dve.wait_ge(cols_done, 1)
            V.tensor_copy(ecol, m.PS[:, 7, 0:TT * MH].rearrange("p (t h) -> p t h", h=MH))
            link(V.tensor_copy(ccol, m.PS[:, 6, 0:TT * MH].rearrange("p (t h) -> p t h", h=MH)))
            dve.wait_ge(bcast, 1)
            for h in range(MH):
                for j in range(TT):
                    n = TT - j
                    last = V.tensor_scalar(W[:, h, start[j]:start[j] + n, :],
                                           m.PS[:, h, j * P:].rearrange("p (n k) -> p n k", k=P),
                                           ccol[:, j, h:h + 1], 0.0, ALU.subtract, ALU.max)
            last.then_inc(dist, 1)
            taps = m.col("conv").rearrange("p (j w) -> p j w", w=4)
            for j in range(4):
                last = V.tensor_scalar(qk[:, j, :], xc[:, j, 0:SEQ], taps[:, j, 0:1], None, ALU.mult)
            link(last)
            for w in range(1, 4):
                for j in range(4):
                    last = V.scalar_tensor_tensor(qk[:, j, :], xc[:, j, w:w + SEQ], taps[:, j, w:w + 1], qk[:, j, :],
                                                  ALU.mult, ALU.add)
                if w < 3:
                    link(last)
            last.then_inc(conv_done, 1)
            dve.wait_ge(weights, 1)
            for j in range(TT):
                V.tensor_tensor(W[:, :, start[j], :], W[:, :, start[j], :], spread(m.upper, 1, MH), ALU.mult)

    with stage(nc, "mlstm2", "scored weighted summed squares root dve") as (scored, weighted, summed, squares, root, dve_chain), \
            nc.Block() as block:
        @block.tensor
        def _(pe):
            for j in range(TT):
                if j >= 2:
                    pe.wait_ge(weighted, j - 1)
                for h in range(MH):
                    at = (h % 2) * HD
                    last = nc.tensor.matmul(m.PS[:, 4 * (j % 2) + h, 0:SEQ - j * P],
                                            qk[at:at + HD, 2 + h // 2, j * P:j * P + P],
                                            qk[at:at + HD, h // 2, j * P:SEQ], start=True, stop=True)
                last.then_inc(scored, 1)
            pe.wait_ge(weighted, TT)
            for i in range(TT):
                for h in range(MH):
                    for j in range(i + 1):
                        last = nc.tensor.matmul(m.PS[:, i, h * (HD + 1):(h + 1) * (HD + 1)], W[:, h, start[j] + i - j, :],
                                                va[:, j, h, :], start=(j == 0), stop=(j == i))
            last.then_inc(summed, 1)

        @block.vector
        def _(dve):
            link = chain(dve, dve_chain)
            V = nc.vector
            for j in range(TT):
                dve.wait_ge(scored, j + 1)
                for h in range(MH):
                    part = W[:, h, start[j]:start[j] + TT - j, :].rearrange("p n k -> p (n k)")
                    last = V.scalar_tensor_tensor(part, m.PS[:, 4 * (j % 2) + h, 0:SEQ - j * P], HD ** -0.5, part,
                                                  ALU.mult, ALU.mult)
                last.then_inc(weighted, 1)
            dve.wait_ge(summed, 1)
            sums = m.PS[:, 0:TT, 0:MH * (HD + 1)].rearrange("p t (h d) -> p t h d", d=HD + 1)
            link(V.tensor_copy(den, sums[:, :, :, HD]))
            link(V.scalar_tensor_tensor(den, den, -1.0, den, ALU.mult, ALU.max))
            link(V.tensor_tensor(den, den, ecol, ALU.max))
            link(V.reciprocal(den, den))
            for t in range(TT):
                last = V.tensor_tensor(num[:, t], sums[:, t, :, 0:HD], spread(den[:, t], 2, HD), ALU.mult)
            link(last)
            link(V.tensor_tensor(va[:, :, :, 0:HD], num, num, ALU.mult))
            link(V.tensor_reduce(ms, va[:, :, :, 0:HD], AX.X, ALU.add))
            V.tensor_scalar(ms, ms, 1.0 / HD, EPS, ALU.mult, ALU.add).then_inc(squares, 1)
            norm = m.row("mlstm_norm").rearrange("p (h d) -> p h d", d=HD)
            link(V.tensor_tensor(og, og, spread(norm, 1, TT), ALU.mult))
            dve.wait_ge(root, 1)
            link(V.reciprocal(ms, ms))
            for t in range(TT):
                last = V.tensor_tensor(num[:, t], num[:, t], spread(ms[:, t], 2, HD), ALU.mult)
            link(last)
            V.tensor_tensor(y[:, :, QH * HD:(QH + MH) * HD].rearrange("p t (h d) -> p t h d", d=HD), num, og, ALU.mult)

        @block.scalar
        def _(act):
            act.wait_ge(squares, 1)
            nc.scalar.activation(ms, ms, ACT.Sqrt).then_inc(root, 1)



def invert(nc, m, name, AT, A0, levels, A):
    N = 4 * TT
    XT, X, A0T, A2, A2T = (A.take(N, P) for _ in range(5))
    IA, IAT = X, XT
    with stage(nc, name, "product dve") as (product, dve_chain), nc.Block() as block:
        lo, hi = (m.PS[:, 4 * s:4 * s + 4, :].rearrange("p b (h k) -> p (b h) k", h=4) for s in range(2))
        eye = spread(m.ident, 1, N)
        C, T1 = A0, A0T

        @block.vector
        def _(dve):
            link = chain(dve, dve_chain)
            V = nc.vector
            link(V.tensor_tensor(A0T, AT, spread(m.upper8, 1, N), ALU.mult))
            V.tensor_tensor(IAT, A0T, eye, ALU.add)
            link(V.tensor_tensor(IA, A0, eye, ALU.add))
            dve.wait_ge(product, 1)
            V.tensor_copy(A2, lo)
            link(V.tensor_copy(A2T, hi))
            dve.wait_ge(product, 2)
            V.tensor_tensor(X, lo, IA, ALU.add)
            link(V.tensor_tensor(XT, hi, IAT, ALU.add))
            dve.wait_ge(product, 3)
            V.tensor_copy(A0, lo)
            link(V.tensor_copy(A0T, hi))
            dve.wait_ge(product, 4)
            V.tensor_tensor(X, lo, X, ALU.add)
            link(V.tensor_tensor(XT, hi, XT, ALU.add))
            for n, b in enumerate(levels):
                link(V.tensor_tensor(C, AT, spread(m.merge[b], 1, N), ALU.mult))
                dve.wait_ge(product, 5 + 2 * n)
                link(V.tensor_copy(T1, lo))
                dve.wait_ge(product, 6 + 2 * n)
                V.tensor_tensor(X, lo, X, ALU.add)
                link(V.tensor_tensor(XT, hi, XT, ALU.add))

        @block.tensor
        def _(pe):
            def products(after, low, high):
                pe.wait_ge(dve_chain, after)
                for to, pair in ((lo, low), (hi, high)):
                    if pair:
                        for i in range(N):
                            last = nc.tensor.matmul(to[:, i, :], pair[0][:, i, :], pair[1][:, i, :], start=True, stop=True)
                last.then_inc(product, 1)

            products(2, (A0T, A0), (A0, A0T))
            products(3, (A2T, IA), (A2, IAT))
            products(4, (A2T, A2), (A2, A2T))
            products(5, (A0T, X), (A0, XT))
            for n in range(len(levels)):
                products(7 + 3 * n, (C, X), None)
                products(8 + 3 * n, (XT, T1), (T1, XT))
    return XT



def rwkv(nc, m, proj, y, A, w_up, a_up, g_up):
    LC = 64
    NC = SEQ // LC
    N = 4 * TT
    place = lambda t, h: (h % 2) * 8 + t * 2 + h // 2
    g = A.take(TT, 256)
    bonus = A.take(TT, RH)
    vtok = A.take(TT, 256)
    rt, at_, bt, kt, bh, kh = (A.take(2, SEQ) for _ in range(6))
    pend = A.take(2, NC)
    stay = A.at
    fm = A.take(DK, SEQ)
    r, k, v, lora, gx = fm[:, 0:2], fm[:, 2:4], fm[:, 4:6], fm[:, 6], fm[:, 7]
    upw, gw = A.take(256), A.take(256)
    raw = A.take(DK, 1 + SEQ)
    B = Arena(m.A)
    lw, a, kk, t1, t2, reset = (B.take(2, SEQ) for _ in range(6))

    with stage(nc, "rwkv1", "loaded turned moved mixed lora_in lora_out gates gate_out squares root norm_sum dve expd exp_in bonus_out heads_out") as \
            (loaded, turned, moved, mixed, lora_in, lora_out, gates, gate_out, squares, root, norm_sum, dve_chain, expd, exp_in,
             bonus_out, heads_out), nc.Block() as block:
        @block.sync
        def _(sp):
            sp.dma_start(upw[0:64], w_up).then_inc(loaded, 16)
            sp.dma_start(upw[64:128], a_up).then_inc(loaded, 16)
            sp.dma_start(gw, g_up).then_inc(loaded, 16)

        @block.tensor
        def _(pe):
            for j in range(DK):
                for t in range(TT):
                    last = nc.tensor.transpose(m.PS[:, j, t * P:t * P + P], proj[:, t, RW + j * P:RW + j * P + P], m.ident)
            last.then_inc(turned, 1)
            pe.wait_ge(moved, 1)
            pe.wait_ge(loaded, 48)
            pe.wait_ge(lora_in, 1)
            for j in range(2):
                nc.tensor.matmul(m.PS[:, j, :], upw[0:64, j * P:j * P + P], lora[0:64], start=True, stop=True)
                last = nc.tensor.matmul(m.PS[:, 2 + j, :], upw[64:128, j * P:j * P + P], lora[64:128], start=True, stop=True)
            last.then_inc(lora_out, 1)
            for t in range(TT):
                last = nc.tensor.matmul(m.PS[:, 4 + t // 2, (t % 2) * 256:(t % 2 + 1) * 256], gx[:, t * P:t * P + P], gw,
                                        start=True, stop=True)
            last.then_inc(gate_out, 1)
            pe.wait_ge(squares, 1)
            for j in range(2):
                last = nc.tensor.matmul(m.PS[:, 6 + j, :], m.same[64], t1[:, j], start=True, stop=True)
            last.then_inc(norm_sum, 1)
            pe.wait_ge(squares, 2)
            for t in range(TT):
                for j in range(2):
                    last = nc.tensor.matmul(m.PS[:, 4, t * 4 + 2 * j:t * 4 + 2 * j + 2], t1[:, j, t * P:t * P + P],
                                            m.same[64][:, 0:P:64], start=True, stop=True)
            for t in range(TT):
                for j in range(2):
                    last = nc.tensor.transpose(m.PS[:, t // 2, (t % 2) * 256 + j * P:(t % 2) * 256 + j * P + P],
                                               v[:, j, t * P:t * P + P], m.ident)
            last.then_inc(bonus_out, 1)

        @block.scalar
        def _(act):
            act.wait_ge(mixed, 1)
            nc.scalar.activation(lora[0:64], lora[0:64], ACT.Tanh)
            nc.scalar.activation(gx, gx, ACT.Sigmoid).then_inc(lora_in, 1)
            act.wait_ge(lora_out, 1)
            for j in range(2):
                nc.scalar.activation(lw[:, j], m.PS[:, j, :], ACT.Sigmoid, bias=m.col("w0")[:, j:j + 1])
                nc.scalar.activation(a[:, j], m.PS[:, 2 + j, :], ACT.Sigmoid, bias=m.col("a0")[:, j:j + 1])\
                    .then_inc(gates, 1)
            act.wait_ge(norm_sum, 2)
            nc.scalar.activation(t2, t2, ACT.Sqrt).then_inc(root, 1)
            for i in range(3):
                act.wait_ge(exp_in, i + 1)
                src, dst, sign = ((t1, rt, 1.0), (t2, at_, 1.0), (t1, bt, -1.0))[i]
                nc.scalar.activation(dst, src, ACT.Exp, scale=sign).then_inc(expd, 1)
            act.wait_ge(exp_in, 4)
            nc.scalar.activation(bh, bh, ACT.Exp)
            nc.scalar.activation(pend, t1.rearrange("p a (c l) -> p a c l", l=LC)[:, :, :, LC - 1], ACT.Exp).then_inc(expd, 1)

        @block.vector
        def _(dve):
            link = chain(dve, dve_chain)
            V = nc.vector
            link(V.memset(raw[:, :, 0:1], 0.0))
            dve.wait_ge(turned, 1)
            V.memset(reset, 1.0)
            link(V.tensor_copy(raw[:, :, 1:1 + SEQ], m.PS[:, :, :]))
            V.memset(reset.rearrange("p a (c l) -> p a c l", l=LC)[:, :, :, 0:1], 0.0)
            link(V.tensor_tensor(fm, raw[:, :, 0:SEQ], raw[:, :, 1:1 + SEQ], ALU.subtract))
            for j in (6, 7, 0, 1, 2, 3, 4, 5):
                last = V.scalar_tensor_tensor(fm[:, j], fm[:, j], m.col("mu")[:, j:j + 1], raw[:, j, 1:1 + SEQ],
                                              ALU.mult, ALU.add)
                if j == 7:
                    last.then_inc(mixed, 1)
            last.then_inc(moved, 1)
            dve.wait_ge(moved, 1)
            for j in range(2):
                last = V.tensor_scalar(kk[:, j], k[:, j], m.col("k_k")[:, j:j + 1], None, ALU.mult)
            link(last)
            V.tensor_tensor(t1, kk, kk, ALU.mult).then_inc(squares, 1)
            dve.wait_ge(norm_sum, 1)
            V.tensor_scalar(t2, m.PS[:, 6:8, :], 1e-24, None, ALU.max).then_inc(norm_sum, 1)
            dve.wait_ge(root, 1)
            link(V.reciprocal(t2, t2))
            link(V.tensor_tensor(kk, kk, t2, ALU.mult))
            dve.wait_ge(gates, 2)
            link(V.tensor_scalar(t2, a, 1.0, None, ALU.subtract))
            for j in range(2):
                last = V.tensor_scalar(t2[:, j], t2[:, j], m.col("k_a")[:, j:j + 1], 1.0, ALU.mult, ALU.add)
            link(last)
            link(V.tensor_tensor(k, k, t2, ALU.mult))
            dve.wait_ge(gate_out, 1)
            link(V.tensor_copy(g, m.PS[:, 4:6, :].rearrange("p b (t n) -> p (b t) n", t=2)))
            link(V.tensor_tensor(t1, r, k, ALU.mult))
            for j in range(2):
                last = V.tensor_scalar(t1[:, j], t1[:, j], m.col("r_k")[:, j:j + 1], None, ALU.mult)
            last.then_inc(squares, 1)
            dve.wait_ge(bonus_out, 1)
            V.tensor_copy(vtok, m.PS[:, 0:2, :].rearrange("p b (t n) -> p (b t) n", t=2))
            link(V.tensor_copy(bonus, m.PS[:, 4, 0:16].rearrange("p (t h) -> p t h", h=RH)))
            link(V.tensor_scalar(lw, lw, -math.exp(-0.5), None, ALU.mult))
            for j in range(2):
                last = V.tensor_tensor_scan(t1[:, j], reset[:, j], lw[:, j], 0.0, ALU.mult, ALU.add)
            last.then_inc(exp_in, 1)
            dve.wait_ge(exp_in, 1)
            V.tensor_tensor(t2, t1, lw, ALU.subtract).then_inc(exp_in, 2)
            cum = t1.rearrange("p a (c l) -> p a c l", l=LC)
            V.tensor_tensor(bh.rearrange("p a (c l) -> p a c l", l=LC), spread(cum[:, :, :, LC - 1], 3, LC), cum,
                            ALU.subtract).then_inc(exp_in, 1)
            dve.wait_ge(expd, 4)
            link(V.tensor_tensor(a, a, kk, ALU.mult))
            V.tensor_tensor(rt, rt, r, ALU.mult)
            V.scalar_tensor_tensor(at_, at_, -1.0, kk, ALU.mult, ALU.mult)
            V.tensor_tensor(kt, bt, k, ALU.mult)
            V.tensor_tensor(kh, bh, k, ALU.mult)
            dve.wait_ge(dve_chain, 1)
            link(V.tensor_tensor(bt, bt, a, ALU.mult))
            V.tensor_tensor(bh, bh, a, ALU.mult)

    A.at = stay
    AbT, A0, AkT, RbT, RkT = (A.take(N, P) for _ in range(5))
    abk = A.take(TT, 3, 256)
    with stage(nc, "rwkv2", "turned scored dve act") as (turned, scored, dve_chain, act_chain), nc.Block() as block:
        @block.tensor
        def _(pe):
            for i in range(3):
                src = (at_, bh, kh)[i]
                for t in range(TT):
                    for j in range(2):
                        last = nc.tensor.transpose(m.PS[:, 2 * i + t // 2, (t % 2) * 256 + j * P:(t % 2) * 256 + j * P + P],
                                                   src[:, j, t * P:t * P + P], m.ident)
            last.then_inc(turned, 1)
            n = 0
            for left, right in ((bt, at_), (at_, bt), (kt, at_), (bt, rt), (kt, rt)):
                pe.wait_ge(dve_chain, n + 1)
                for t in range(TT):
                    for h in range(RH):
                        po, j = (h % 2) * HD, h // 2
                        last = nc.tensor.matmul(m.PS[:, place(t, h) // 4, (place(t, h) % 4) * P:(place(t, h) % 4 + 1) * P], left[po:po + HD, j, t * P:t * P + P],
                                                right[po:po + HD, j, t * P:t * P + P], start=True, stop=True)
                last.then_inc(scored, 1)
                n += 1

        @block.vector
        def _(dve):
            V = nc.vector
            dve.wait_ge(turned, 1)
            for i in range(3):
                last = V.tensor_copy(abk[:, :, i, :], m.PS[:, 2 * i:2 * i + 2, :].rearrange("p b (t n) -> p (b t) n", t=2))
            last.then_inc(dve_chain, 1)
            for n, (to, mask) in enumerate(((AbT, m.strict_upper64), (A0, m.lower8), (AkT, m.strict_upper64),
                                            (RbT, m.upper64), (RkT, m.upper64))):
                dve.wait_ge(scored, n + 1)
                V.tensor_tensor(to, m.PS[:, 0:4, :].rearrange("p b (h k) -> p (b h) k", h=4), spread(mask, 1, N), ALU.mult)\
                    .then_inc(dve_chain, 1)

    B = Arena(m.A)
    XT = invert(nc, m, "rwkv_inv", AbT, A0, (8, 16, 32), B)
    B.at = N * P

    zin = A0
    WU = AbT
    TTm, Hm = B.take(2, 2, NC // 2, HD), B.take(2, 2, NC // 2, HD)
    QT = B.take(2, SEQ)
    Nst = B.take(2, NC + 1, HD)
    y0 = B.take(TT, 256)
    with stage(nc, "rwkv3", "product dve act") as (product, dve_chain, act_chain), nc.Block() as block:
        flat = lambda ap: ap.rearrange("p b (h k) -> p (b h) k", h=4)
        diag = m.ident

        @block.tensor
        def _(pe):
            for t in range(TT):
                for h in range(RH):
                    last = nc.tensor.matmul(m.PS[:, place(t, h) // 8, (place(t, h) % 8) * HD:(place(t, h) % 8 + 1) * HD], AkT[:, place(t, h), :], vtok[:, t, h * HD:h * HD + HD],
                                            start=True, stop=True)
            last.then_inc(product, 1)
            pe.wait_ge(dve_chain, 1)
            for t in range(TT):
                for h in range(RH):
                    last = nc.tensor.matmul(m.PS[:, 4 + place(t, h) // 4, (place(t, h) % 4) * P:(place(t, h) % 4 + 1) * P], XT[:, place(t, h), :], zin[:, place(t, h), :],
                                            start=True, stop=True)
            last.then_inc(product, 1)
            pe.wait_ge(dve_chain, 2)
            for t in range(TT):
                for h in range(RH):
                    po, j = (h % 2) * HD, h // 2
                    last = nc.tensor.matmul(m.PS[po:po + HD, j, t * P:t * P + P], WU[:, place(t, h), 0:HD], RbT[:, place(t, h), :],
                                            start=True, stop=True)
            for c in range(NC):
                t, q = c // 2, (c % 2) * LC
                for h in range(RH):
                    po, j = (h % 2) * HD, h // 2
                    wu = WU[q:q + LC, place(t, h), :]
                    bt_, kt_ = abk[q:q + LC, t, 1, h * HD:h * HD + HD], abk[q:q + LC, t, 2, h * HD:h * HD + HD]
                    at = (4 * j + c // 2) * HD
                    nc.tensor.matmul(m.PS[po:po + HD, 2 + c % 2, at:at + HD], wu[:, 0:HD], bt_, start=True, stop=True)
                    nc.tensor.matmul(m.PS[po:po + HD, 4 + c % 2, at:at + HD], bt_, wu[:, HD:P], start=True, stop=False)
                    last = nc.tensor.matmul(m.PS[po:po + HD, 4 + c % 2, at:at + HD], kt_,
                                            vtok[q:q + LC, t, h * HD:h * HD + HD], start=False, stop=True)
            for t in range(TT):
                for h in range(RH):
                    to = m.PS[:, 6 + t // 2, (t % 2) * 256 + h * HD:(t % 2) * 256 + h * HD + HD]
                    nc.tensor.matmul(to, RbT[:, place(t, h), :], WU[:, place(t, h), HD:P], start=True, stop=False)
                    last = nc.tensor.matmul(to, RkT[:, place(t, h), :], vtok[:, t, h * HD:h * HD + HD], start=False, stop=True)
            last.then_inc(product, 1)
            for c in range(NC - 1):
                pe.wait_ge(dve_chain, 3 + c)
                for h in range(RH):
                    po, j = (h % 2) * HD, h // 2
                    last = nc.tensor.matmul(m.PS[po:po + HD, 0, j * HD:j * HD + HD], TTm[po:po + HD, c % 2, j, c // 2, :],
                                            Nst[po:po + HD, j, c, :], start=True, stop=True)
                last.then_inc(product, 1)
            pe.wait_ge(dve_chain, 3 + NC - 1)
            for c in range(NC):
                t, q = c // 2, (c % 2) * LC
                for h in range(RH):
                    po, j = (h % 2) * HD, h // 2
                    last = nc.tensor.matmul(m.PS[q:q + LC, 4 + h % 2, (t * 2 + j) * HD:(t * 2 + j) * HD + HD],
                                            QT[po:po + HD, j, c * LC:c * LC + LC], Nst[po:po + HD, j, c, :],
                                            start=True, stop=True)
            last.then_inc(product, 1)

        @block.vector
        def _(dve):
            V = nc.vector
            for a in range(2):
                V.tensor_copy(zin.rearrange("p (a t j) n -> p a t j n", a=2, j=2)[:, a, :, :, 0:HD],
                              abk[:, :, 0, :].rearrange("p t (j a d) -> p a t j d", a=2, d=HD)[:, a])
            V.memset(Nst[:, :, 0, :], 0.0)
            dve.wait_ge(product, 1)
            V.tensor_copy(zin[:, :, HD:P], m.PS[:, 0:2, :].rearrange("p b (n d) -> p (b n) d", d=HD)).then_inc(dve_chain, 1)
            dve.wait_ge(product, 2)
            V.tensor_copy(WU, flat(m.PS[:, 4:8, :])).then_inc(dve_chain, 1)
            dve.wait_ge(product, 3)
            V.tensor_tensor(QT, m.PS[:, 0:2, :], rt, ALU.add)
            V.tensor_copy(Hm.rearrange("p a j c n -> p a (j c n)"), m.PS[:, 4:6, :])
            V.tensor_copy(y0, m.PS[:, 6:8, :].rearrange("p b (t n) -> p (b t) n", t=2))
            for po in (0, HD):
                for j in range(2):
                    for c in range(NC):
                        last = V.scalar_tensor_tensor(TTm[po:po + HD, c % 2, j, c // 2, :], diag[po:po + HD, po:po + HD],
                                                      pend[po:po + HD, j, c:c + 1], m.PS[po:po + HD, 2 + c % 2, (4 * j + c // 2) * HD:(4 * j + c // 2 + 1) * HD],
                                                      ALU.mult, ALU.add)
            last.then_inc(dve_chain, 1)
            for c in range(NC - 1):
                dve.wait_ge(product, 4 + c)
                V.tensor_tensor(Nst[:, :, c + 1, :], m.PS[:, 0, 0:2 * HD].rearrange("p (j n) -> p j n", j=2), Hm[:, c % 2, :, c // 2, :],
                                ALU.add).then_inc(dve_chain, 1)
            dve.wait_ge(product, 4 + NC - 1)
            for a in range(2):
                part = y0.rearrange("p t (j a d) -> p a t j d", a=2, d=HD)[:, a]
                V.tensor_tensor(part, part, m.PS[:, 4 + a, :].rearrange("p (t j d) -> p t j d", t=TT, d=HD), ALU.add)

    yv, sq = y0, B.take(TT, RH, HD)
    mean, var = B.take(TT, RH), B.take(TT, RH)
    with stage(nc, "rwkv4", "squares root dve") as (squares, root, dve_chain), nc.Block() as block:
        y4 = yv.rearrange("p t (h d) -> p t h d", d=HD)
        v4 = vtok.rearrange("p t (h d) -> p t h d", d=HD)

        @block.vector
        def _(dve):
            link = chain(dve, dve_chain)
            V = nc.vector
            link(V.tensor_reduce(mean, y4, AX.X, ALU.add))
            link(V.tensor_scalar(mean, mean, 1.0 / HD, None, ALU.mult))
            for t in range(TT):
                last = V.tensor_tensor(y4[:, t], y4[:, t], spread(mean[:, t], 2, HD), ALU.subtract)
            link(last)
            link(V.tensor_tensor(sq, y4, y4, ALU.mult))
            link(V.tensor_reduce(var, sq, AX.X, ALU.add))
            V.tensor_scalar(var, var, 1.0 / HD, 64e-5, ALU.mult, ALU.add).then_inc(squares, 1)
            for t in range(TT):
                last = V.tensor_tensor(v4[:, t], v4[:, t], spread(bonus[:, t], 2, HD), ALU.mult)
            link(last)
            link(V.tensor_tensor(vtok, vtok, spread(m.row("ln_b"), 1, TT), ALU.add))
            dve.wait_ge(root, 1)
            link(V.reciprocal(var, var))
            for t in range(TT):
                last = V.tensor_tensor(y4[:, t], y4[:, t], spread(var[:, t], 2, HD), ALU.mult)
            link(last)
            link(V.tensor_tensor(yv, yv, spread(m.row("ln_w"), 1, TT), ALU.mult))
            link(V.tensor_tensor(yv, yv, vtok, ALU.add))
            V.tensor_tensor(y[:, :, (QH + MH) * HD:D], yv, g, ALU.mult)

        @block.scalar
        def _(act):
            act.wait_ge(squares, 1)
            nc.scalar.activation(var, var, ACT.Sqrt).then_inc(root, 1)



def gated_embedding(nc, m, p, w_gate, w_proj):
    norm_transpose(nc, m, "ple_pre", m.x, TT, m.col("ple_pre"), m.hT, Arena(m.R))
    A = Arena(m.A)
    gate = A.take(TT, D)
    pt = A.take(TT, D_PLE)
    pT = A.take(D_PLE // P, SEQ)
    project_tokens(nc, m, "ple_gate", m.hT, DK, w_gate, D, gate, m.R)
    with stage(nc, "ple_load", "loaded") as (loaded,), nc.Block() as block:
        @block.sync
        def _(sp):
            sp.dma_start(pt, p.rearrange("(t p) n -> p t n", p=P)).then_inc(loaded, 16)
            sp.wait_ge(loaded, 16)

        @block.scalar
        def _(act):
            nc.scalar.activation(gate, gate, ACT.Sigmoid)
    turn_tiles(nc, m, "ple_turn", lambda t, k: pt[:, t, k * P:k * P + P], D_PLE // P, pT)
    project_tokens(nc, m, "ple_proj", pT, D_PLE // P, w_proj, D, m.y, m.R)
    with stage(nc, "ple_mul", "done") as (done,), nc.Block() as block:
        @block.vector
        def _(dve):
            nc.vector.tensor_tensor(m.y, m.y, gate, ALU.mult).then_inc(done, 1)
    post_norm_add(nc, m, "ple_post", m.y, m.row("ple_post"), 1.0, Arena(m.R))


def first_layer(nc, m, w, l):
    def at(name):
        ap = w[name]
        names = "abc"[:len(ap.shape) - 1]
        sub = ap[bass.ds(l, 1)]
        return sub.rearrange(f"z {' '.join(names)} -> (z {names[0]}) {' '.join(names[1:])}")

    load_layer(nc, m, at("cols"), w["rows"][bass.ds(l, 1)], NCOL, NROW)
    m.table = (COLS, ROWS)
    feed_forward(nc, m, "ffn1", at("w_ffn1_in"), at("w_ffn1_out"), m.col("ffn1_pre"), m.row("ffn1_post"))
    norm_transpose(nc, m, "mix_pre", m.x, TT, m.col("mix_pre"), m.hT, Arena(m.R))
    proj = m.A[:, 0:TT * D_IN].rearrange("p (t n) -> p t n", t=TT)
    project_tokens(nc, m, "mix_in", m.hT, DK, at("w_in"), D_IN, proj, m.R)
    attention(nc, m, proj, m.y, Arena(m.R))
    mlstm(nc, m, proj, m.y, Arena(m.R))
    rwkv(nc, m, proj, m.y, Arena(m.R), at("rwkv_w_up"), at("rwkv_a_up"), at("rwkv_g_up"))
    A = Arena(m.A)
    yT = A.take(DK, SEQ)
    turn_tiles(nc, m, "mix_turn", lambda t, k: m.y[:, t, k * P:k * P + P], DK, yT)
    project_tokens(nc, m, "mix_out", yT, DK, at("w_out"), D, m.y, m.R)
    post_norm_add(nc, m, "mix_post", m.y, m.row("mix_post"), 1.0, Arena(m.R))
    feed_forward(nc, m, "ffn2", at("w_ffn2_in"), at("w_ffn2_out"), m.col("ffn2_pre"), m.row("ffn2_post"))
    gated_embedding(nc, m, at("p"), at("w_ple_gate"), at("w_ple_proj"))



def convolve(V, link, tiles, taps, src, dst, bias=None):
    for j in tiles:
        if bias is None:
            last = V.tensor_scalar(dst[:, j, :], src[:, j, :], taps[:, j, 3:4], None, ALU.mult)
        else:
            last = V.tensor_scalar(dst[:, j, :], src[:, j, :], taps[:, j, 3:4], bias[:, j:j + 1], ALU.mult, ALU.add)
    link(last)
    for back in range(1, 4):
        for j in tiles:
            last = V.scalar_tensor_tensor(dst[:, j, back:], src[:, j, 0:SEQ - back], taps[:, j, 3 - back:4 - back],
                                          dst[:, j, back:], ALU.mult, ALU.add)
        link(last)


def rg_lru(nc, m, feats, yT, A, weights):
    gw = A.take(2, 4, HD)
    c, r, i, a, sq = (A.take(4, SEQ) for _ in range(5))
    lam = m.col("lam")
    la, e, z, z2, sp = (A.take(4) for _ in range(5))
    xr, gate = feats[:, 0:4], feats[:, 4:8]
    with stage(nc, "lru", "loaded dve lam_in lam_out mixed product gates la_in act squares root gelu") as \
            (loaded, dve_chain, lam_in, lam_out, mixed, product, gates, la_in, act_out, squares, root, gelu), \
            nc.Block() as block:
        @block.sync
        def _(sp_):
            for which in range(2):
                sp_.dma_start(gw[:, which], weights[which].rearrange("j p n -> p j n")).then_inc(loaded, 16)

        @block.tensor
        def _(pe):
            pe.wait_ge(loaded, 32)
            pe.wait_ge(mixed, 1)
            for which in range(2):
                for j in range(4):
                    for po in (0, HD):
                        last = nc.tensor.matmul(m.PS[po:po + HD, 4 * which + j, :], gw[po:po + HD, which, j, :],
                                                c[po:po + HD, j, :], start=True, stop=True)
                last.then_inc(product, 1)

        @block.scalar
        def _(act):
            act.wait_ge(lam_in, 1)
            nc.scalar.activation(e, la, ACT.Exp, scale=-1.0).then_inc(lam_out, 1)
            for which, (to, bias) in enumerate(((r, "ba"), (i, "bx"))):
                act.wait_ge(product, which + 1)
                for j in range(4):
                    last = nc.scalar.activation(to[:, j], m.PS[:, 4 * which + j, :], ACT.Sigmoid, bias=m.col(bias)[:, j:j + 1])
                last.then_inc(gates, 1)
            act.wait_ge(la_in, 1)
            nc.scalar.activation(a, r, ACT.Exp)
            nc.scalar.activation(sq, r, ACT.Tanh, scale=-1.0).then_inc(act_out, 1)
            nc.scalar.activation(gate, gate, ACT.Gelu_apprx_tanh).then_inc(gelu, 1)
            act.wait_ge(squares, 1)
            nc.scalar.activation(sq, sq, ACT.Sqrt).then_inc(root, 1)

        @block.vector
        def _(dve):
            link = chain(dve, dve_chain)
            V = nc.vector
            V.scalar_tensor_tensor(la, lam, -1.0, lam, ALU.mult, ALU.max).then_inc(lam_in, 1)
            convolve(V, link, range(4), m.col("conv_lru").rearrange("p (j w) -> p j w", w=4), xr, c, m.col("conv_b"))
            V.memset(z, 0.0).then_inc(mixed, 1)
            dve.wait_ge(lam_out, 1)
            dve.wait_ge(mixed, 1)
            log1p_series(link, V, e, z, z2, sp)
            link(V.tensor_scalar(la, lam, -1.0, 0.0, ALU.mult, ALU.max))
            link(V.tensor_tensor(sp, sp, la, ALU.add))
            link(V.tensor_scalar(sp, sp, -8.0, None, ALU.mult))
            dve.wait_ge(gates, 2)
            for j in range(4):
                last = V.tensor_scalar(r[:, j], r[:, j], sp[:, j:j + 1], None, ALU.mult)
            last.then_inc(la_in, 1)
            link(V.tensor_tensor(i, i, c, ALU.mult))
            dve.wait_ge(act_out, 1)
            link(V.tensor_tensor(r, a, a, ALU.mult))
            V.scalar_tensor_tensor(sq, r, 1.0, sq, ALU.add, ALU.mult).then_inc(squares, 1)
            dve.wait_ge(root, 1)
            link(V.tensor_tensor(i, i, sq, ALU.mult))
            for j in range(4):
                last = V.tensor_tensor_scan(c[:, j], a[:, j], i[:, j], 0.0, ALU.mult, ALU.add)
            link(last)
            dve.wait_ge(gelu, 1)
            V.tensor_tensor(yT, c, gate, ALU.mult)


def delta_net(nc, m, f, zab, yT, A):
    N = 4 * TT
    araw, beta, g, e, z, z2, gcol, eg, kds, egl = (A.take(N) for _ in range(10))
    start = A.at
    cv, sq = A.take(12, SEQ), A.take(8, SEQ)
    taps = m.col("conv_qkv").rearrange("p (j w) -> p j w", w=4)
    th = lambda ap: ap.rearrange("p (t h) -> p t h", h=4)

    with stage(nc, "gdn1", "dve conv silu squared summed shifted root") as (dve_chain, conv, silu, squared, summed, shifted, root), \
            nc.Block() as block:
        @block.vector
        def _(dve):
            link = chain(dve, dve_chain)
            V = nc.vector
            for part in range(3):
                convolve(V, link, range(4 * part, 4 * part + 4), taps, f, cv)
                V.memset(e, 0.0).then_inc(conv, 1)
            for half in range(2):
                dve.wait_ge(summed, half + 1)
                V.tensor_scalar(sq[:, 4 * half:4 * half + 4], m.PS[:, 4 * half:4 * half + 4, :], EPS, None, ALU.add)\
                    .then_inc(shifted, 1)
            for half in range(2):
                dve.wait_ge(root, half + 1)
                part = slice(4 * half, 4 * half + 4)
                link(V.reciprocal(sq[:, part], sq[:, part]))
                V.scalar_tensor_tensor(f[:, part].rearrange("p a b -> p (a b)"), cv[:, part].rearrange("p a b -> p (a b)"),
                                       (P ** -0.5, 1.0)[half], sq[:, part].rearrange("p a b -> p (a b)"), ALU.mult, ALU.mult)

        @block.scalar
        def _(act):
            for part in range(3):
                act.wait_ge(conv, part + 1)
                tiles = slice(4 * part, 4 * part + 4)
                to = cv[:, tiles] if part < 2 else f[:, tiles]
                nc.scalar.activation(to, cv[:, tiles], ACT.Silu).then_inc(silu, 1)
                if part < 2:
                    act.wait_ge(silu, part + 1)
                    nc.scalar.activation(sq[:, tiles], cv[:, tiles], ACT.Square).then_inc(squared, 1)
            for half in range(2):
                act.wait_ge(shifted, half + 1)
                tiles = slice(4 * half, 4 * half + 4)
                nc.scalar.activation(sq[:, tiles], sq[:, tiles], ACT.Sqrt).then_inc(root, 1)

        @block.tensor
        def _(pe):
            for half in range(2):
                pe.wait_ge(squared, half + 1)
                for j in range(4 * half, 4 * half + 4):
                    last = nc.tensor.matmul(m.PS[:, j, :], m.ones, sq[:, j, :], start=True, stop=True)
                last.then_inc(summed, 1)

    A.at = start
    DT, D_, attnT, AT, QT = (A.take(N, P) for _ in range(5))
    zin = A.take(N, 2 * P)
    kd = A.take(N, P)
    kbT = A.take(N, P)
    bb, gb, A0 = AT, attnT, D_
    four = lambda ap, h0: ap[:, h0:h0 + 4, :].rearrange("p h (t k) -> p t h k", t=TT)
    banks = lambda b: m.PS[:, b:b + 4, :].rearrange("p b (h k) -> p (b h) k", h=4)
    banks4 = lambda b: m.PS[:, b:b + 4, :].rearrange("p b (h k) -> p b h k", h=4)
    view4 = lambda ap: ap.rearrange("p (t h) k -> p t h k", h=4)
    with stage(nc, "gdn2", "dve abs_in exp_out product copies dist act_out") as (dve_chain, abs_in, exp_out, product, copies, dist, act_out), \
            nc.Block() as block:
        @block.vector
        def _(dve):
            link = chain(dve, dve_chain)
            V = nc.vector
            link(V.tensor_tensor(th(araw), zab[:, :, 512:516], spread(m.row("dt_bias"), 1, TT), ALU.add))
            link(V.scalar_tensor_tensor(e, araw, -1.0, araw, ALU.mult, ALU.max))
            V.tensor_copy(th(beta), zab[:, :, 516:520]).then_inc(abs_in, 1)
            dve.wait_ge(exp_out, 1)
            log1p_series(link, V, e, z, z2, g)
            link(V.scalar_tensor_tensor(g, araw, 0.0, g, ALU.max, ALU.add))
            link(V.scalar_tensor_tensor(th(g), th(g), -1.0, spread(m.row("a_log"), 1, TT), ALU.mult, ALU.mult))
            V.tensor_copy(gb, spread(g, 2, P))
            V.tensor_copy(bb, spread(beta, 2, P)).then_inc(copies, 1)
            dve.wait_ge(product, 1)
            link(V.tensor_copy(gcol, m.PS[:, 4, 0:N]))
            V.tensor_copy(egl, banks(0)[:, :, P - 1])
            link(V.tensor_tensor(DT, banks(0), spread(gcol, 2, P), ALU.subtract))
            V.tensor_tensor(kds, egl, gcol, ALU.subtract)
            V.tensor_scalar(D_, DT, -1.0, 0.0, ALU.mult, ALU.min)
            link(V.tensor_scalar(DT, DT, 0.0, None, ALU.min))
            V.memset(z, 0.0).then_inc(dist, 1)
            dve.wait_ge(product, 2)
            V.tensor_tensor(view4(kbT), four(f, 4), banks4(4), ALU.mult)
            dve.wait_ge(act_out, 1)
            V.tensor_tensor(DT, DT, spread(m.upper, 1, N), ALU.mult)
            V.tensor_tensor(D_, D_, spread(m.lower8, 1, N), ALU.mult)
            V.tensor_tensor(view4(QT), four(f, 0), view4(QT), ALU.mult)

        @block.scalar
        def _(act):
            act.wait_ge(abs_in, 1)
            nc.scalar.activation(e, e, ACT.Exp, scale=-1.0)
            nc.scalar.activation(m.row("a_log"), m.row("a_log"), ACT.Exp)
            nc.scalar.activation(beta, beta, ACT.Sigmoid).then_inc(exp_out, 1)
            act.wait_ge(dist, 1)
            nc.scalar.activation(QT, banks(0), ACT.Exp)
            nc.scalar.activation(DT, DT, ACT.Exp)
            nc.scalar.activation(D_, D_, ACT.Exp)
            nc.scalar.activation(eg, gcol, ACT.Exp)
            nc.scalar.activation(kds, kds, ACT.Exp)
            nc.scalar.activation(egl, egl, ACT.Exp).then_inc(act_out, 1)

        @block.tensor
        def _(pe):
            pe.wait_ge(copies, 1)
            nc.tensor.matmul(m.PS[:, 4, 0:N], m.upper, g, start=True, stop=True)
            for n in range(N):
                last = nc.tensor.matmul(banks(0)[:, n, :], gb[:, n, :], m.upper, start=True, stop=True)
            last.then_inc(product, 1)
            pe.wait_ge(dist, 1)
            for n in range(N):
                last = nc.tensor.matmul(banks(4)[:, n, :], bb[:, n, :], m.ident, start=True, stop=True)
            last.then_inc(product, 1)

    with stage(nc, "gdn3", "product dve turned") as (product, dve_chain, turned), nc.Block() as block:
        @block.vector
        def _(dve):
            V = nc.vector
            link = chain(dve, dve_chain)
            dve.wait_ge(product, 1)
            link(V.scalar_tensor_tensor(AT, banks(0), -1.0, DT, ALU.mult, ALU.mult))
            V.tensor_tensor(AT, AT, spread(m.strict_upper, 1, N), ALU.mult)
            dve.wait_ge(product, 2)
            link(V.scalar_tensor_tensor(A0, banks(4), -1.0, D_, ALU.mult, ALU.mult))
            dve.wait_ge(product, 3)
            link(V.tensor_tensor(attnT, banks(0), DT, ALU.mult))
            dve.wait_ge(turned, 1)
            V.tensor_tensor(zin[:, :, 0:P], banks(4), spread(beta, 2, P), ALU.mult)
            link(V.tensor_tensor(eg, eg, beta, ALU.mult))
            dve.wait_ge(turned, 2)
            V.tensor_tensor(kd, banks(0), spread(kds, 2, P), ALU.mult)
            V.tensor_tensor(zin[:, :, P:2 * P], banks(0), spread(eg, 2, P), ALU.mult)

        @block.tensor
        def _(pe):
            def scores(b, left, right, lk, rk):
                for t in range(TT):
                    for h in range(4):
                        lo = left[:, t * 4 + h, :] if lk is None else left[:, lk + h, t * P:t * P + P]
                        hi = right[:, t * 4 + h, :] if rk is None else right[:, rk + h, t * P:t * P + P]
                        last = nc.tensor.matmul(banks(b)[:, t * 4 + h, :], lo, hi, start=True, stop=True)
                last.then_inc(product, 1)

            scores(0, f, kbT, 4, None)
            scores(4, kbT, f, None, 4)
            pe.wait_ge(dve_chain, 1)
            scores(0, f, f, 4, 0)
            pe.wait_ge(dve_chain, 2)
            for b, head0, after in ((4, 8, None), (0, 4, 3)):
                if after:
                    pe.wait_ge(dve_chain, after)
                for t in range(TT):
                    for h in range(4):
                        last = nc.tensor.transpose(banks(b)[:, t * 4 + h, :], f[:, head0 + h, t * P:t * P + P], m.ident)
                last.then_inc(turned, 1)

    B = Arena(m.A)
    XT = invert(nc, m, "gdn_inv", AT, A0, (8, 16, 32, 64), B)
    B.at = N * P
    UW = B.take(N, 2 * P)
    Nst = B.take(TT + 1, GH, P)
    TTm, Hm, y0 = AT, A0, DT
    with stage(nc, "gdn4", "product dve") as (product, dve_chain), nc.Block() as block:
        @block.tensor
        def _(pe):
            for n in range(N):
                last = nc.tensor.matmul(m.PS[:, n // 2, (n % 2) * 256:(n % 2 + 1) * 256], XT[:, n, :], zin[:, n, :],
                                        start=True, stop=True)
            last.then_inc(product, 1)
            pe.wait_ge(dve_chain, 1)
            for n in range(N):
                nc.tensor.matmul(banks(0)[:, n, :], UW[:, n, P:2 * P], attnT[:, n, :], start=True, stop=True)
            for n in range(N):
                last = nc.tensor.matmul(banks(4)[:, n, :], UW[:, n, P:2 * P], kd[:, n, :], start=True, stop=True)
            last.then_inc(product, 1)
            pe.wait_ge(dve_chain, 2)
            for n in range(N):
                nc.tensor.matmul(banks(0)[:, n, :], kd[:, n, :], UW[:, n, 0:P], start=True, stop=True)
            for n in range(N):
                last = nc.tensor.matmul(banks(4)[:, n, :], attnT[:, n, :], UW[:, n, 0:P], start=True, stop=True)
            last.then_inc(product, 1)
            for t in range(TT - 1):
                pe.wait_ge(dve_chain, 3 + t)
                for h in range(GH):
                    last = nc.tensor.matmul(m.PS[:, 0, h * P:h * P + P], TTm[:, t * 4 + h, :], Nst[:, t, h, :],
                                            start=True, stop=True)
                last.then_inc(product, 1)
            pe.wait_ge(dve_chain, 3 + TT - 1)
            for n in range(N):
                last = nc.tensor.matmul(banks(4)[:, n, :], QT[:, n, :], Nst[:, n // 4, n % 4, :], start=True, stop=True)
            last.then_inc(product, 1)

        @block.vector
        def _(dve):
            V = nc.vector
            V.memset(Nst[:, 0], 0.0)
            dve.wait_ge(product, 1)
            V.tensor_copy(UW, m.PS[:, :, :].rearrange("p b (n k) -> p (b n) k", n=2)).then_inc(dve_chain, 1)
            dve.wait_ge(product, 2)
            V.tensor_tensor(QT, QT, banks(0), ALU.subtract)
            for n in range(N):
                last = V.scalar_tensor_tensor(TTm[:, n, :], m.ident, egl[:, n:n + 1], banks(4)[:, n, :], ALU.mult, ALU.subtract)
            last.then_inc(dve_chain, 1)
            dve.wait_ge(product, 3)
            V.tensor_copy(y0, banks(4))
            V.tensor_copy(Hm, banks(0)).then_inc(dve_chain, 1)
            for t in range(TT - 1):
                dve.wait_ge(product, 4 + t)
                if t == 0:
                    dve.wait_ge(dve_chain, 3)
                V.tensor_tensor(Nst[:, t + 1], m.PS[:, 0, :].rearrange("p (h k) -> p h k", h=GH),
                                Hm[:, 4 * t:4 * t + 4, :], ALU.add).then_inc(dve_chain, 1)
            dve.wait_ge(product, 4 + TT - 1)
            V.tensor_tensor(y0, y0, banks(4), ALU.add)

    ms, o2 = z, QT
    with stage(nc, "gdn5", "squares root dve silu gated turned") as (squares, root, dve_chain, silu, gated, turned), \
            nc.Block() as block:
        zz = zab[:, :, 0:512].rearrange("p t (h k) -> p t h k", h=4)

        @block.vector
        def _(dve):
            link = chain(dve, dve_chain)
            V = nc.vector
            link(V.tensor_tensor(o2, y0, y0, ALU.mult))
            link(V.tensor_reduce(ms, o2, AX.X, ALU.add))
            V.tensor_scalar(ms, ms, 1.0 / P, EPS, ALU.mult, ALU.add).then_inc(squares, 1)
            dve.wait_ge(root, 1)
            link(V.reciprocal(ms, ms))
            link(V.tensor_tensor(y0, y0, spread(ms, 2, P), ALU.mult))
            link(V.tensor_tensor(y0, y0, spread(m.row("gdn_norm"), 1, N), ALU.mult))
            dve.wait_ge(silu, 1)
            V.tensor_tensor(view4(y0), view4(y0), zz, ALU.mult).then_inc(gated, 1)
            dve.wait_ge(turned, 1)
            V.tensor_copy(yT, m.PS[:, 0:4, :])

        @block.scalar
        def _(act):
            nc.scalar.activation(zz, zz, ACT.Silu).then_inc(silu, 1)
            act.wait_ge(squares, 1)
            nc.scalar.activation(ms, ms, ACT.Sqrt).then_inc(root, 1)

        @block.tensor
        def _(pe):
            pe.wait_ge(gated, 1)
            for h in range(4):
                for t in range(TT):
                    last = nc.tensor.transpose(m.PS[:, h, t * P:t * P + P], y0[:, t * 4 + h, :], m.ident)
            last.then_inc(turned, 1)


def add_to_x(nc, m, name, y):
    with stage(nc, name, "added") as (added,), nc.Block() as block:
        @block.vector
        def _(dve):
            nc.vector.tensor_tensor(m.x, m.x, y, ALU.add).then_inc(added, 1)


def hybrid_mixer(nc, m, w):
    norm_transpose(nc, m, "hyb_pre", m.x, TT, m.col("mix"), m.hT, Arena(m.R))
    A = Arena(m.A)
    qkv = A.take(12, SEQ)
    lru_f = A.take(8, SEQ)
    zab = m.R[:, m.R.shape[1] - TT * 520:].rearrange("p (t n) -> p t n", t=TT)
    w_in = w["w_in_2"]
    project_features(nc, m, "hyb_qkv", m.hT, DK, w_in[:, 0:G_Z], 3 * GQK, qkv, m.R, SEQ)
    project_features(nc, m, "hyb_lru", m.hT, DK, w_in[:, G_XR:IN2], 1024, lru_f, m.R, SEQ)
    project_tokens(nc, m, "hyb_z", m.hT, DK, w_in[:, G_Z:G_XR], 520, zab, m.R)
    rg_lru(nc, m, lru_f, m.hT[:, 4:8], Arena(m.R), w["lru_w_2"])
    delta_net(nc, m, qkv, zab, m.hT[:, 0:4], Arena(m.R[:, 0:m.R.shape[1] - TT * 520]))
    y = Arena(m.A).take(TT, D)
    project_tokens(nc, m, "hyb_out", m.hT, DK, w["w_out_2"], D, y, m.R)
    add_to_x(nc, m, "hyb_add", y)



def cross_attention(nc, m, w):
    ring = 2 * DK * 512
    R = Arena(m.R)
    R.at = ring
    mem = R.take(2, D)
    memT = R.take(DK, MEM)
    kT = R.take(DK, MEM)
    v = R.take(2, XH * 256)
    B = Arena(m.A)
    qT = B.take(DK, SEQ)
    keep = B.at
    with stage(nc, "mem_in", "loaded") as (loaded,), nc.Block() as block:
        @block.sync
        def _(sp):
            sp.dma_start(mem, w["mem_2"].rearrange("(t p) n -> p t n", p=P)).then_inc(loaded, 16)
            sp.wait_ge(loaded, 16)
    norm_transpose(nc, m, "xa_pre", m.x, TT, m.col("xattn"), m.hT, Arena(m.R[:, 0:ring]))
    norm_transpose(nc, m, "xa_mem", mem, 2, m.col("mem"), memT, Arena(m.R[:, 0:ring]))
    project_features(nc, m, "xa_q", m.hT, DK, w["xattn_wq_2"], D, qT, m.R, SEQ)
    project_features(nc, m, "xa_k", memT, DK, w["xattn_wkv_2"][:, 0:D], D, kT, m.R, MEM)
    project_tokens(nc, m, "xa_v", memT, DK, w["xattn_wkv_2"][:, D:2 * D], D, v, m.R, T=2)
    N = TT * XH
    S = B.take(N, MEM)
    pT = Arena(m.R).take(2 * XH, SEQ)
    mx, den = B.take(N), B.take(N)
    with stage(nc, "xa", "scored dve act probs turned copied product copied_act") as \
            (scored, dve_chain, act_out, probs, turned, copied, product, copied_act), nc.Block() as block:
        @block.tensor
        def _(pe):
            for t in range(TT):
                for h in range(XH):
                    for b in range(2):
                        last = nc.tensor.matmul(m.PS[:, 2 * t + h // 2, (h % 2) * MEM:(h % 2 + 1) * MEM],
                                                qT[:, 2 * h + b, t * P:t * P + P], kT[:, 2 * h + b, :],
                                                start=(b == 0), stop=(b == 1))
            last.then_inc(scored, 1)
            pe.wait_ge(probs, 1)
            for h in range(XH):
                for b in range(2):
                    for t in range(TT):
                        last = nc.tensor.transpose(m.PS[:, 2 * h + b, t * P:t * P + P], S[:, t * XH + h, b * P:b * P + P], m.ident)
            last.then_inc(turned, 1)
            pe.wait_ge(copied, 1)
            pe.wait_ge(copied_act, 1)
            for h in range(XH):
                for half in range(2):
                    for b in range(2):
                        last = nc.tensor.matmul(m.PS[:, 2 * h + half, :], v[:, b, h * 256 + half * P:h * 256 + half * P + P],
                                                pT[:, 2 * h + b, :], start=(b == 0), stop=(b == 1))
            last.then_inc(product, 1)

        @block.vector
        def _(dve):
            link = chain(dve, dve_chain)
            V = nc.vector
            dve.wait_ge(scored, 1)
            scores = m.PS[:, :, :].rearrange("p b (h k) -> p (b h) k", h=2)
            link(V.tensor_reduce(mx, scores, AX.X, ALU.max))
            link(V.tensor_tensor(S, scores, spread(mx, 2, MEM), ALU.subtract))
            dve.wait_ge(act_out, 1)
            link(V.tensor_reduce(den, S, AX.X, ALU.add))
            link(V.reciprocal(den, den))
            V.tensor_tensor(S, S, spread(den, 2, MEM), ALU.mult).then_inc(probs, 1)
            dve.wait_ge(turned, 1)
            V.tensor_copy(pT[:, 0:4], m.PS[:, 0:4, :]).then_inc(copied, 1)
            dve.wait_ge(product, 1)
            V.tensor_copy(m.hT[:, 0:4], m.PS[:, 0:4, :])

        @block.scalar
        def _(act):
            act.wait_ge(dve_chain, 2)
            nc.scalar.activation(S, S, ACT.Exp, scale=256 ** -0.5).then_inc(act_out, 1)
            act.wait_ge(turned, 1)
            nc.scalar.activation(pT[:, 4:8], m.PS[:, 4:8, :], ACT.Copy).then_inc(copied_act, 1)
            act.wait_ge(product, 1)
            nc.scalar.activation(m.hT[:, 4:8], m.PS[:, 4:8, :], ACT.Copy)
    y = Arena(m.A).take(TT, D)
    project_tokens(nc, m, "xa_out", m.hT, DK, w["xattn_wo_2"], D, y, m.R)
    add_to_x(nc, m, "xa_add", y)



def peer(nc, m, w):
    ring = 2 * DK * 512
    B = Arena(m.A)
    norm_transpose(nc, m, "peer_pre", m.x, TT, m.col("ffn"), m.hT, B)
    xn = m.A[:, 8:8 + TT * D].rearrange("p (t n) -> p t n", t=TT)
    R = Arena(m.R)
    R.at = ring
    qT = R.take(2 * PH, SEQ)
    sub = R.take(2 * PH, NKEY)
    project_features(nc, m, "peer_q", m.hT, DK, w["peer_wq_2"], 2 * PH * P, qT, m.R, SEQ)

    NE = PH * TOPK
    idx = B.take(TT, NE, dtype=U32)
    gate = B.take(TT, NE)
    dots = B.take(TT, NE)
    iota = B.take(TOPK)
    iota_i = B.take(TOPK, dtype=I32)
    R2 = Arena(m.R)
    sc = R2.take(2 * PH, NKEY)
    vals, ids_f = R2.take(2 * PH, TOPK), R2.take(2 * PH, TOPK)
    ids = R2.take(2 * PH, TOPK, dtype=U32)
    cand = R2.take(PH, TOPK, TOPK)
    best, pos = R2.take(PH, TOPK), R2.take(PH, TOPK, dtype=U32)
    half_u = R2.take(PH, TOPK, dtype=U32)
    half_f, e12 = R2.take(PH, TOPK), R2.take(2, NE)
    den = R2.take(PH)
    flatc = cand.rearrange("p h i j -> p h (i j)")
    assert R2.at <= ring
    with stage(nc, "peer_top", "loaded scored taken dve iota_done exp_in exp_out") as \
            (loaded, scored, taken, dve_chain, iota_done, exp_in, exp_out), nc.Block() as block:
        @block.sync
        def _(sp):
            sp.dma_start(sub, w["subkeys_2"]).then_inc(loaded, 16)

        @block.gpsimd
        def _(pool):
            nc.gpsimd.iota(iota_i, pattern=[[1, TOPK]], base=0, channel_multiplier=0).then_inc(iota_done, 1)

        @block.tensor
        def _(pe):
            pe.wait_ge(loaded, 16)
            for t in range(TT):
                if t >= 2:
                    pe.wait_ge(taken, t - 1)
                for n in range(2 * PH):
                    last = nc.tensor.matmul(m.PS[:, 4 * (t % 2) + n // 4, (n % 4) * P:(n % 4 + 1) * P],
                                            qT[:, n, t * P:t * P + P], sub[:, n, :], start=True, stop=True)
                last.then_inc(scored, 1)

        @block.scalar
        def _(act):
            for t in range(TT):
                act.wait_ge(exp_in, t + 1)
                nc.scalar.activation(best, best, ACT.Exp).then_inc(exp_out, 1)

        @block.vector
        def _(dve):
            link = chain(dve, dve_chain)
            V = nc.vector
            dve.wait_ge(iota_done, 1)
            link(V.tensor_copy(iota, iota_i))
            V.tensor_tensor(xn, xn, spread(m.row("ffn_row"), 1, TT), ALU.mult)

            def top16(values, indices, table, n):
                for part in (slice(0, 8), slice(8, 16)):
                    for r in range(n):
                        last = V.max(values[:, r, part], table[:, r, :])
                    link(last)
                    for r in range(n):
                        last = V.max_index(indices[:, r, part], values[:, r, part], table[:, r, :])
                    if part.start == 0:
                        link(last)
                        for r in range(n):
                            last = V.match_replace(table[:, r, :], values[:, r, part], table[:, r, :], -3.0e38)
                    link(last)

            for t in range(TT):
                dve.wait_ge(scored, t + 1)
                last = V.tensor_copy(sc, m.PS[:, 4 * (t % 2):4 * (t % 2) + 4, :].rearrange("p b (n k) -> p (b n) k", n=4))
                last.then_inc(taken, 1)
                dve.wait_ge(taken, t + 1)
                top16(vals, ids, sc, 2 * PH)
                link(V.tensor_copy(ids_f, ids))
                pairs = vals.rearrange("p (h s) k -> p h s k", s=2)
                ipairs = ids_f.rearrange("p (h s) k -> p h s k", s=2)
                link(V.tensor_tensor(cand, spread(pairs[:, :, 0, :], 3, TOPK), spread(pairs[:, :, 1, :], 2, TOPK), ALU.add))
                top16(best, pos, flatc, PH)
                for s in range(2):
                    if s == 0:
                        link(V.tensor_scalar(half_u, pos, 4, None, ALU.logical_shift_right))
                    else:
                        link(V.tensor_scalar(half_u, pos, 15, None, ALU.bitwise_and))
                    link(V.tensor_copy(half_f, half_u))
                    link(V.tensor_tensor(cand.rearrange("p h i j -> p (h i) j"),
                                         spread(half_f.rearrange("p h k -> p (h k)"), 2, TOPK), spread(iota, 1, NE), ALU.is_equal))
                    link(V.tensor_tensor(cand, cand, spread(ipairs[:, :, s, :], 2, TOPK), ALU.mult))
                    link(V.tensor_reduce(e12[:, s, :], cand.rearrange("p h i j -> p (h i) j"), AX.X, ALU.add))
                link(V.scalar_tensor_tensor(e12[:, 0, :], e12[:, 0, :], float(NKEY), e12[:, 1, :], ALU.mult, ALU.add))
                V.tensor_copy(idx[:, t, :], e12[:, 0, :])
                link(V.tensor_copy(den, best[:, :, 0]))
                V.tensor_tensor(best, best, spread(den, 2, TOPK), ALU.subtract).then_inc(exp_in, 1)
                dve.wait_ge(exp_out, t + 1)
                link(V.tensor_reduce(den, best, AX.X, ALU.add))
                link(V.reciprocal(den, den))
                last = V.tensor_tensor(gate[:, t, :].rearrange("p (h k) -> p h k", h=PH), best, spread(den, 2, TOPK), ALU.mult)
                link(last)

    gather(nc, m, "peer_u", w["peer_u_2"], idx, xn, dots, None)
    with stage(nc, "peer_act", "gelu done") as (gelu, done), nc.Block() as block:
        @block.scalar
        def _(act):
            nc.scalar.activation(dots, dots, ACT.Gelu_apprx_tanh).then_inc(gelu, 1)

        @block.vector
        def _(dve):
            dve.wait_ge(gelu, 1)
            nc.vector.tensor_tensor(dots, dots, gate, ALU.mult).then_inc(done, 1)
    gather(nc, m, "peer_v", w["peer_v_2"], idx, None, dots, m.x)


def gather(nc, m, name, table, idx, tokens, dots, acc):
    SLOTS = 8
    turns = TT * PH * TOPK // SLOTS
    A = Arena(m.R)
    rows = [A.take(D) for _ in range(2 * SLOTS)]
    junk = A.take(2, D)
    flat_idx = idx.rearrange("p t n -> p (t n)")
    flat_dots = dots.rearrange("p t n -> p (t n)")
    now = [A.take(SLOTS, dtype=U32) for _ in range(2)]
    zero, spare = A.take(2), A.take(2)
    with stage(nc, name, "zeroed copied used " + " ".join(f"row{s}" for s in range(2 * SLOTS))) as (zeroed, copied, used, *row_in), \
            nc.Block() as block:
        @block.gpsimd
        def _(pool):
            def turn(i, parity, first):
                if not first:
                    pool.wait_ge(used, i * SLOTS - SLOTS)
                    pool.wait_ge(copied, 1)
                nc.gpsimd.tensor_copy(now[parity], flat_idx[:, bass.ds(i * SLOTS, SLOTS)]).then_inc(copied, 1)
                pool.wait_ge(copied, i * 2 + 1)
                nc.gpsimd.tensor_tensor(spare, zero, zero, ALU.add).then_inc(copied, 1)
                for s in range(SLOTS):
                    slot = parity * SLOTS + s
                    nc.gpsimd.indirect_dma_start(out=rows[slot], out_offset=None, in_=table,
                                                 in_offset=bass.IndirectOffsetOnAxis(ap=now[parity][:, s:s + 1], axis=0))\
                        .then_inc(row_in[slot], 16)

            nc.gpsimd.memset(zero, 0.0).then_inc(zeroed, 1)
            pool.wait_ge(zeroed, 1)
            turn(0, 0, True)
            turn(1, 1, True)
            with pool.Fori(1, turns // 2) as i:
                turn(i * 2, 0, False)
                turn(i * 2 + 1, 1, False)

        @block.vector
        def _(dve):
            per = turns // TT // 2
            V = nc.vector

            def turn(i, parity, t):
                for s in range(SLOTS):
                    slot = parity * SLOTS + s
                    n = i * 2 * SLOTS + slot
                    dve.wait_ge(row_in[slot], (i + 1) * 16)
                    one = flat_dots[:, bass.ds(n, 1)]
                    tile = (tokens if acc is None else acc)[:, t, :]
                    if acc is None:
                        V.scalar_tensor_tensor(junk[:, s % 2], rows[slot], 1.0, tile, ALU.mult, ALU.mult, accum_out=one)\
                            .then_inc(used, 1)
                    else:
                        V.scalar_tensor_tensor(tile, rows[slot], one, tile, ALU.mult, ALU.add).then_inc(used, 1)
                    dve.wait_ge(used, n + 1)

            for t in range(TT):
                with dve.Fori(t * per, (t + 1) * per) as i:
                    for parity in range(2):
                        turn(i, parity, t)


def final_norm(nc, m):
    ssq = Arena(m.R).take(TT)
    with stage(nc, "final", "squares mean root dve") as (squares, mean, root, dve_chain), nc.Block() as block:
        @block.scalar
        def _(act):
            for t in range(TT):
                nc.scalar.activation(m.y[:, t, :], m.x[:, t, :], ACT.Square, accum_out=ssq[:, t:t + 1]).then_inc(squares, 1)
            act.wait_ge(mean, 1)
            nc.scalar.activation(ssq, ssq, ACT.Sqrt).then_inc(root, 1)

        @block.vector
        def _(dve):
            link = chain(dve, dve_chain)
            V = nc.vector
            dve.wait_ge(squares, TT)
            V.tensor_scalar(ssq, ssq, 1.0 / D, EPS, ALU.mult, ALU.add).then_inc(mean, 1)
            dve.wait_ge(root, 1)
            link(V.reciprocal(ssq, ssq))
            for t in range(TT):
                V.scalar_tensor_tensor(m.x[:, t, :], m.x[:, t, :], ssq[:, t:t + 1], m.row("final"), ALU.mult, ALU.mult)


def second_block(nc, m, w):
    load_layer(nc, m, w["cols_2"], w["rows_2"], NCOL2, NROW2)
    m.table = (COLS2, ROWS2)
    hybrid_mixer(nc, m, w)
    cross_attention(nc, m, w)
    peer(nc, m, w)
    final_norm(nc, m)


def build(nc, w, out):
    ctx = ExitStack()
    with ctx:
        def sb(name, n, parts=P):
            return ctx.enter_context(nc.sbuf_tensor(name, [parts, n], F32))[:, :]

        m = Memory()
        m.PS = ctx.enter_context(nc.psum_tensor("PS", [P, 8, 512], F32))[:, :, :]
        m.x = sb("x", TT * D).rearrange("p (t n) -> p t n", t=TT)
        m.H = sb("H", DK * SEQ)
        m.hT = m.H.rearrange("p (k n) -> p k n", k=DK)
        m.y = m.H.rearrange("p (t n) -> p t n", t=TT)
        m.A = sb("A", TT * D_IN)
        m.R = sb("R", 2 * FK * 512)
        m.cols = sb("cols", max(NCOL, NCOL2))
        m.rows = sb("rows", max(NROW, NROW2))
        m.ident, m.ones = sb("ident", P), sb("ones", P)
        m.upper, m.strict_upper, m.strict_lower = (sb(n, P) for n in ("upper", "strict_upper", "strict_lower"))
        m.upper8, m.lower8 = sb("upper8", P), sb("lower8", P)
        m.upper64, m.strict_upper64 = sb("upper64", P), sb("strict_upper64", P)
        m.same = {b: sb(f"same{b}", P) for b in (8, 16, 32, 64)}
        m.merge = {b: sb(f"merge{b}", P) for b in (8, 16, 32, 64)}
        m.window = sb("window", 4 * P).rearrange("p (n k) -> p n k", n=2)
        m.pick = sb("pick", 4 * P, parts=4).rearrange("p (h n) -> p h n", h=4)
        m.cos, m.sin = (sb(n, TT * 8).rearrange("p (t j) -> p t j", t=TT) for n in ("cos", "sin"))
        m.table = (COLS, ROWS)
        m.col = lambda name: m.cols[:, m.table[0][name][0]:m.table[0][name][1]]
        m.row = lambda name: m.rows[:, m.table[1][name][0]:m.table[1][name][1]]

        constants(nc, m)
        with stage(nc, "x_in", "loaded") as (loaded,), nc.Block() as block:
            @block.sync
            def _(sp):
                sp.dma_start(m.x, w["x"].rearrange("z (t p) n -> p (z t) n", p=P)).then_inc(loaded, 16)
                sp.wait_ge(loaded, 16)
        rope_tables(nc, m, w["positions"].rearrange("z (t p) -> p (z t)", p=P))
        with nc.Fori(0, DEPTH) as l:
            first_layer(nc, m, w, l)
        second_block(nc, m, w)
        with stage(nc, "x_out", "stored") as (stored,), nc.Block() as block:
            @block.sync
            def _(sp):
                sp.dma_start(out.rearrange("z (t p) n -> p (z t) n", p=P), m.x).then_inc(stored, 16)
                sp.wait_ge(stored, 16)



def columns(parts):
    import numpy as np
    out = []
    for a in parts:
        L = a.shape[0]
        out.append(a.reshape(L, -1, P).transpose(0, 2, 1) if a.shape[-1] >= P
                   else np.pad(a.reshape(L, -1, 1), ((0, 0), (0, P - a.shape[-1]), (0, 0))))
    return np.ascontiguousarray(np.concatenate(out, axis=2))


def taps_last(a):
    L, W, C = a.shape
    return a.reshape(L, W, C // P, P).transpose(0, 2, 1, 3).reshape(L, -1)


def layout(i):
    import numpy as np
    w = {n: i[n] for n in ("x", "positions", "w_ffn1_in", "w_ffn1_out", "w_in", "rwkv_w_up", "rwkv_a_up", "rwkv_g_up",
                           "w_out", "w_ffn2_in", "w_ffn2_out", "w_ple_gate", "w_ple_proj")}
    w["p"] = i["p"].reshape(DEPTH, SEQ, D_PLE)
    w["cols"] = columns([i["ln_ffn1_pre"], i["ln_mix_pre"], i["ln_ffn2_pre"], i["ln_ple_pre"], taps_last(i["mlstm_conv"]),
                         i["rwkv_mu"], i["rwkv_w0"], i["rwkv_a0"], i["rwkv_k_k"], i["rwkv_k_a"],
                         i["rwkv_r_k"].reshape(DEPTH, -1), i["mlstm_i_bias"], i["mlstm_f_bias"]])
    w["rows"] = np.concatenate([i["ln_ffn1_post"], i["ln_mix_post"], i["ln_ffn2_post"], i["ln_ple_post"], i["mlstm_norm"],
                                i["rwkv_ln_w"], i["rwkv_ln_b"], i["attn_sinks"]], axis=1)
    for n in ("w_in", "w_out", "xattn_wq", "xattn_wkv", "xattn_wo", "peer_wq", "peer_u", "peer_v"):
        w[n + "_2"] = i[n + "_2"][0]
    w["mem_2"] = i["mem_2"][0]
    w["lru_w_2"] = np.stack([i["lru_wa_2"][0], i["lru_wx_2"][0]]).reshape(2, 4, 2 * HD, HD)
    w["subkeys_2"] = np.ascontiguousarray(i["peer_subkeys_2"][0].reshape(16, NKEY, P).transpose(2, 0, 1))
    w["cols_2"] = columns([i["norm_mix_w_2"], i["norm_xattn_w_2"], i["norm_mem_w_2"], i["norm_ffn_w_2"],
                           taps_last(i["conv_qkv_w_2"]), taps_last(i["lru_conv_w_2"]), i["lru_conv_b_2"], i["lru_ba_2"],
                           i["lru_bx_2"], i["lru_lambda_2"]])[0]
    w["rows_2"] = np.concatenate([i["gdn_a_log_2"], i["gdn_dt_bias_2"], i["gdn_norm_w_2"], i["norm_ffn_w_2"], i["norm_final_w_2"].reshape(1, -1)],
                                 axis=1)
    return w


def kernel(**inputs):
    import numpy as np
    import concourse.bacc as bacc
    from concourse.bass_utils import run_bass_kernel_spmd

    nc = bacc.Bacc("TRN2", target_bir_lowering=False, num_devices=1)
    arrays, w = {}, {}
    for name, a in layout({n: np.asarray(a) for n, a in inputs.items()}).items():
        a = np.ascontiguousarray(a)
        arrays[f"in_{name}"] = a
        w[name] = nc.dram_tensor(f"in_{name}", a.shape, mybir.dt.from_np(a.dtype), kind="ExternalInput").ap()
    out = nc.dram_tensor("out_x", (1, SEQ, D), F32, kind="ExternalOutput").ap()
    build(nc, w, out)
    got = run_bass_kernel_spmd(nc, [arrays], core_ids=[0])
    return got.results[0]["out_x"]
```

```python
import math
from contextlib import ExitStack, contextmanager

import concourse.bass as bass
from concourse import mybir

F32 = mybir.dt.float32
F32R = mybir.dt.float32r
I32 = mybir.dt.int32
U32 = mybir.dt.uint32
ACT = mybir.ActivationFunctionType
ALU = mybir.AluOpType
AX = mybir.AxisListType

P = 128
D = 1024
DK = D // P
SEQ = 512
TT = SEQ // P
DEPTH = 2
EPS = 1e-6
NEG = -1e30

HD = 64
D_FF = 2816
FK = D_FF // P
D_PLE = 256
QH, KVH = 8, 2
ATTN_COLS = QH * HD + 2 * KVH * HD
MH, RH = 4, 4
ML_V = ATTN_COLS + 2 * MH * HD
ML_O = ML_V + MH * HD
ML_I = ML_O + MH * HD
ML_F = ML_I + MH
RW = ML_F + MH
D_IN = RW + 3 * RH * HD + 64 + 64 + 128
GATE_CAP = 15.0

COLS = {}
ROWS = {}


def lay(table, names):
    at = 0
    for name, width in names:
        table[name] = (at, at + width)
        at += width
    return at


NCOL = lay(COLS, [("ffn1_pre", 8), ("mix_pre", 8), ("ffn2_pre", 8), ("ple_pre", 8), ("conv", 16), ("mu", 8), ("w0", 2),
                  ("a0", 2), ("k_k", 2), ("k_a", 2), ("r_k", 2), ("i_bias", 1), ("f_bias", 1)])
NROW = lay(ROWS, [("ffn1_post", D), ("mix_post", D), ("ffn2_post", D), ("ple_post", D), ("mlstm_norm", 256),
                  ("ln_w", 256), ("ln_b", 256), ("sinks", 8)])

GH = 4
GQK = GH * P
G_Z = 3 * GQK
G_A = G_Z + GQK
G_B = G_A + GH
G_XR = G_B + GH
G_GATE = G_XR + 512
IN2 = G_GATE + 512
MEM = 256
XH = 4
PH = 8
NKEY = 128
TOPK = 16
COLS2 = {}
ROWS2 = {}
NCOL2 = lay(COLS2, [("mix", 8), ("xattn", 8), ("mem", 8), ("ffn", 8), ("conv_qkv", 48), ("conv_lru", 16), ("conv_b", 4),
                    ("ba", 4), ("bx", 4), ("lam", 4)])
NROW2 = lay(ROWS2, [("a_log", GH), ("dt_bias", GH), ("gdn_norm", P), ("ffn_row", D), ("final", D)])


def chain(engine, sem):
    done = [0]

    def link(instruction):
        done[0] += 1
        instruction.then_inc(sem, 1)
        engine.wait_ge(sem, done[0])

    return link


@contextmanager
def stage(nc, name, signals):
    with ExitStack() as s:
        sems = [s.enter_context(nc.semaphore(f"{name}_{x}")) for x in signals.split()]
        yield sems
        numbers = sorted(x.num for x in sems)
        first = numbers[0]
        for n, following in zip(numbers, numbers[1:] + [None]):
            if following != n + 1:
                nc.multi_engine_barrier(list(nc.engines), range(first, n + 1))
                first = following


class Arena:

    def __init__(self, region):
        self.region, self.at = region, 0

    def take(self, *shape, parts=P, dtype=F32):
        n = math.prod(shape)
        n += n % 2
        assert self.at + n <= self.region.shape[1], (self.at, n, self.region.shape)
        flat = self.region[0:parts, self.at:self.at + math.prod(shape)]
        self.at += n
        if dtype != F32:
            flat = flat.bitcast(dtype)
        if len(shape) == 1:
            return flat
        names = "abcde"[:len(shape)]
        return flat.rearrange(f"p ({' '.join(names)}) -> p {' '.join(names)}", **dict(zip(names, shape)))


def spread(ap, axis, n):
    v = ap.unsqueeze(axis)
    shape = list(v.shape)
    shape[axis] = n
    return v.broadcast_to(shape)


class Memory:
    pass



def constants(nc, m):
    def block_view(ap, b):
        return ap.rearrange("p (n b) -> p n b", b=b)

    with stage(nc, "const", "pool dve") as (pool_chain, dve_chain), nc.Block() as block:
        @block.gpsimd
        def _(pool):
            link = chain(pool, pool_chain)
            for ap in (m.ident, m.upper, m.strict_upper, m.strict_lower, *m.same.values(), m.ones):
                nc.gpsimd.memset(ap, 1.0)
            link(nc.gpsimd.memset(m.window, 0.0))

            def keep(ap, pattern, base, mult, fill=0.0, op=ALU.is_ge):
                link(nc.gpsimd.affine_select(out=ap, in_=ap, compare_op=op, fill=fill, base=base,
                                             pattern=pattern, channel_multiplier=mult))

            keep(m.ident, [[-1, P]], 0, 1, op=ALU.is_equal)
            keep(m.upper, [[1, P]], 0, -1)
            keep(m.strict_upper, [[1, P]], -1, -1)
            keep(m.strict_lower, [[-1, P]], -1, 1)
            for b, ap in m.same.items():
                keep(block_view(ap, b), [[-b, P // b], [0, b]], 0, 1)
                keep(block_view(ap, b), [[b, P // b], [0, b]], b - 1, -1)
            for n in range(2):
                keep(m.window[:, n, :], [[-1, 2 * P]], P, 1, fill=NEG)
                keep(m.window[:, n, :], [[1, 2 * P]], -1, -1, fill=NEG)
            keep(m.window[:, 0, :], [[1, 2 * P]], -P, 0, fill=NEG)
            link(nc.gpsimd.memset(m.pick, 1.0))
            keep(m.pick, [[-1, 4], [0, P]], 0, 1, op=ALU.is_equal)

        @block.vector
        def _(dve):
            dve.wait_ge(pool_chain, 6 + 2 * len(m.same) + 5 + 1)
            link = chain(dve, dve_chain)
            V = nc.vector
            for b, ap in m.merge.items():
                if 2 * b < P:
                    link(V.tensor_tensor(ap, m.same[2 * b], m.same[b], ALU.subtract))
                else:
                    link(V.tensor_scalar(ap, m.same[b], -1.0, 1.0, ALU.mult, ALU.add))
                link(V.tensor_tensor(ap, ap, m.strict_upper, ALU.mult))
            V.tensor_tensor(m.upper8, m.same[8], m.strict_upper, ALU.mult)
            V.tensor_tensor(m.lower8, m.same[8], m.strict_lower, ALU.mult)
            V.tensor_tensor(m.strict_upper64, m.same[64], m.strict_upper, ALU.mult)
            link(V.tensor_tensor(m.upper64, m.same[64], m.upper, ALU.mult))


def rope_tables(nc, m, positions, A):
    turn = [6.28125, 0.0019350051879882812, 3.019915981956753e-07]
    magic = 1.5 * 2.0 ** 23
    pos_i = A.take(TT, dtype=I32)
    pos, ang, k, mag = A.take(TT), A.take(TT, 8), A.take(TT, 8), A.take(TT, 8)
    with stage(nc, "rope", "loaded reduced dve") as (loaded, reduced, dve_chain), nc.Block() as block:
        @block.sync
        def _(sp):
            with nc.allow_non_contiguous_dma(reason="512 positions"):
                sp.dma_start(pos_i, positions).then_inc(loaded, 16)

        @block.vector
        def _(dve):
            link = chain(dve, dve_chain)
            V = nc.vector
            dve.wait_ge(loaded, 16)
            link(V.tensor_copy(pos, pos_i))
            for j in range(8):
                last = V.tensor_scalar(ang[:, :, j], pos, float(bass.np.float32(500000.0 ** (-j / 8))), None, ALU.mult)
            link(last)
            link(V.tensor_scalar(k, ang, 1.0 / (2 * math.pi), magic, ALU.mult, ALU.add))
            link(V.tensor_scalar(k, k, magic, None, ALU.subtract))
            for part in turn:
                link(V.scalar_tensor_tensor(ang, k, -part, ang, ALU.mult, ALU.add))
            link(V.tensor_scalar(ang, ang, 3.1415925, -3.1415925, ALU.min, ALU.max))
            link(V.scalar_tensor_tensor(mag, ang, -1.0, ang, ALU.mult, ALU.max))
            V.tensor_scalar(mag, mag, -1.0, math.pi / 2, ALU.mult, ALU.add).then_inc(reduced, 1)

        @block.scalar
        def _(act):
            act.wait_ge(reduced, 1)
            nc.scalar.activation(m.sin, ang, ACT.Sin)
            nc.scalar.activation(m.cos, mag, ACT.Sin)



def load_layer(nc, m, cols, rows, ncol, nrow):
    with stage(nc, "vectors", "loaded") as (loaded,), nc.Block() as block:
        @block.sync
        def _(sp):
            sp.dma_start(m.cols[:, 0:ncol], cols).then_inc(loaded, 16)
            sp.dma_start(m.rows[:, 0:nrow], rows.broadcast_to([P, nrow])).then_inc(loaded, 16)
            sp.wait_ge(loaded, 32)


@contextmanager
def region(nc, name, *shape, dtype=F32):
    USES[name] = USES.get(name, 0) + 1
    with nc.sbuf_tensor(f"{name}_{USES[name]}", [P, math.prod(shape)], dtype) as t:
        if len(shape) == 1:
            yield t[:, :]
        else:
            names = "abcde"[:len(shape)]
            yield t[:, :].rearrange(f"p ({' '.join(names)}) -> p {' '.join(names)}", **dict(zip(names, shape)))


USES = {}


@contextmanager
def split_acts(nc, name, K, n):
    with region(nc, name + "_high", K, n, dtype=F32R) as high, region(nc, name + "_low", K, n, dtype=F32R) as low:
        yield high, low


@contextmanager
def weight_ring(nc, K=2, wide=512, raw=3, split=2):
    with ExitStack() as s:
        yield ([s.enter_context(region(nc, "w_raw", K, wide)) for _ in range(raw)],
               [s.enter_context(split_acts(nc, "w", K, wide)) for _ in range(split)])


def norm_transpose(nc, m, name, src, T, gain, dst, A):
    ssq, rstd = A.take(T), A.take(T)
    xn = A.take(T, D)
    high, low = dst
    with stage(nc, name, "squares mean root scaled turned rounded dve") as \
            (squares, mean, root, scaled, turned, rounded, dve_chain), nc.Block() as block:
        @block.scalar
        def _(act):
            for t in range(T):
                nc.scalar.activation(m.y[:, t, :], src[:, t, :], ACT.Square, accum_out=ssq[:, t:t + 1]).then_inc(squares, 1)
            act.wait_ge(mean, 1)
            nc.scalar.activation(rstd, ssq, ACT.Sqrt).then_inc(root, 1)
            for k in range(DK):
                act.wait_ge(turned, k + 1)
                nc.scalar.activation(high[:, k, :], m.PS[:, k, 0:P * T], ACT.Copy, scale=gain[:, k:k + 1]).then_inc(rounded, 1)

        @block.vector
        def _(dve):
            link = chain(dve, dve_chain)
            V = nc.vector
            dve.wait_ge(squares, T)
            V.tensor_scalar(ssq, ssq, 1.0 / D, EPS, ALU.mult, ALU.add).then_inc(mean, 1)
            dve.wait_ge(root, 1)
            link(V.reciprocal(rstd, rstd))
            for t in range(T):
                V.tensor_scalar(xn[:, t, :], src[:, t, :], rstd[:, t:t + 1], None, ALU.mult).then_inc(scaled, 1)
            for k in range(DK):
                dve.wait_ge(rounded, k + 1)
                V.scalar_tensor_tensor(low[:, k, :], m.PS[:, k, 0:P * T], gain[:, k:k + 1], high[:, k, :].bitcast(F32),
                                       ALU.mult, ALU.subtract)

        @block.tensor
        def _(pe):
            for k in range(DK):
                for t in range(T):
                    if k == 0:
                        pe.wait_ge(scaled, t + 1)
                    last = nc.tensor.transpose(m.PS[:, k, t * P:t * P + P], xn[:, t, k * P:k * P + P], m.ident)
                last.then_inc(turned, 1)


def post_norm_add(nc, m, name, y, gain, factor, A):
    ssq, rstd, junk = A.take(TT), A.take(TT), A.take(TT, D)
    with stage(nc, name, "squares mean root dve") as (squares, mean, root, dve_chain), nc.Block() as block:
        @block.scalar
        def _(act):
            for t in range(TT):
                nc.scalar.activation(junk[:, t], y[:, t, :], ACT.Square, accum_out=ssq[:, t:t + 1]).then_inc(squares, 1)
            act.wait_ge(mean, 1)
            nc.scalar.activation(rstd, ssq, ACT.Sqrt).then_inc(root, 1)

        @block.vector
        def _(dve):
            link = chain(dve, dve_chain)
            V = nc.vector
            dve.wait_ge(squares, TT)
            V.tensor_scalar(ssq, ssq, 1.0 / D, EPS, ALU.mult, ALU.add).then_inc(mean, 1)
            dve.wait_ge(root, 1)
            link(V.reciprocal(rstd, rstd))
            for t in range(TT):
                last = V.scalar_tensor_tensor(y[:, t, :], y[:, t, :], rstd[:, t:t + 1], gain, ALU.mult, ALU.mult)
            link(last)
            for t in range(TT):
                V.scalar_tensor_tensor(m.x[:, t, :], y[:, t, :], factor, m.x[:, t, :], ALU.mult, ALU.add)


def project(nc, m, name, acts, weight, N, out, T=TT, features=False):
    G, RAW, SPLIT = 2, 3, 2
    NG = DK // G
    n_tok = T * P
    chunks = [(c, min(512, N - c)) for c in range(0, N, 512)]
    steps = [(c, g) for c in range(len(chunks)) for g in range(NG)]
    high, low = acts
    tiles = 4 if features else T

    with weight_ring(nc, raw=RAW, split=SPLIT) as (raw, parts), \
            stage(nc, name, "loaded0 loaded1 loaded2 rounded split used out_dve out_act") as \
            (loaded0, loaded1, loaded2, rounded, split, used, out_dve, out_act), nc.Block() as block:
        loaded = (loaded0, loaded1, loaded2)

        def bank(c, t):
            return m.PS[:, (c % 2) * 4 + t, 0:n_tok if features else chunks[c][1]]

        def target(c, t):
            at, w = chunks[c]
            return out[:, 4 * c + t, :] if features else out[:, t, at:at + w]

        @block.sync
        def _(sp):
            for i, (c, g) in enumerate(steps):
                at, w = chunks[c]
                if i >= RAW:
                    sp.wait_ge(split, i - RAW + 1)
                sp.dma_start(raw[i % RAW][:, :, 0:w],
                             weight[g * G * P:(g + 1) * G * P, at:at + w].rearrange("(k p) n -> p k n", p=P))\
                    .then_inc(loaded[i % RAW], 16)

        @block.tensor
        def _(pe):
            for i, (c, g) in enumerate(steps):
                w = chunks[c][1]
                w_high, w_low = parts[i % SPLIT]
                pe.wait_ge(split, i + 1)
                if g == 0 and c >= 2:
                    pe.wait_ge(out_dve, c - 1)
                    pe.wait_ge(out_act, c - 1)
                for t in range(tiles):
                    part = slice(t * P, t * P + P)
                    for kk in range(G):
                        k = g * G + kk
                        if features:
                            still, still_low = w_high[:, kk, part], w_low[:, kk, part]
                            move, move_low = high[:, k, :], low[:, k, :]
                        else:
                            still, still_low = high[:, k, part], low[:, k, part]
                            move, move_low = w_high[:, kk, 0:w], w_low[:, kk, 0:w]
                        nc.tensor.matmul(bank(c, t), still, move, start=(k == 0), stop=False)
                        nc.tensor.matmul(bank(c, t), still, move_low, start=False, stop=False)
                        last = nc.tensor.matmul(bank(c, t), still_low, move, start=False, stop=(k == DK - 1))
                last.then_inc(used, 1)

        @block.scalar
        def _(act):
            def copy_out(c):
                act.wait_ge(used, (c + 1) * NG)
                for t in range(1, tiles, 2):
                    last = nc.scalar.activation(target(c, t), bank(c, t), ACT.Copy)
                last.then_inc(out_act, 1)

            for i, (c, g) in enumerate(steps):
                act.wait_ge(loaded[i % RAW], 16 * (i // RAW + 1))
                if i >= SPLIT:
                    act.wait_ge(used, i - SPLIT + 1)
                w = chunks[c][1]
                nc.scalar.activation(parts[i % SPLIT][0][:, :, 0:w], raw[i % RAW][:, :, 0:w], ACT.Copy).then_inc(rounded, 1)
                if g == 1 and c >= 1:
                    copy_out(c - 1)
            copy_out(len(chunks) - 1)

        @block.vector
        def _(dve):
            def copy_out(c):
                dve.wait_ge(used, (c + 1) * NG)
                for t in range(0, tiles, 2):
                    last = nc.vector.tensor_copy(target(c, t), bank(c, t))
                last.then_inc(out_dve, 1)

            for i, (c, g) in enumerate(steps):
                dve.wait_ge(rounded, i + 1)
                w = chunks[c][1]
                w_high, w_low = parts[i % SPLIT]
                nc.vector.tensor_tensor(w_low[:, :, 0:w], raw[i % RAW][:, :, 0:w], w_high[:, :, 0:w].bitcast(F32),
                                        ALU.subtract).then_inc(split, 1)
                if g == 1 and c >= 1:
                    copy_out(c - 1)
            copy_out(len(chunks) - 1)


def project_model(nc, m, name, acts, K, weight, out):
    with weight_ring(nc, K=1, wide=D, raw=2) as (raw, parts), \
            region(nc, "a_high0", SEQ, dtype=F32R) as ah0, region(nc, "a_high1", SEQ, dtype=F32R) as ah1, \
            region(nc, "a_low0", SEQ, dtype=F32R) as al0, region(nc, "a_low1", SEQ, dtype=F32R) as al1, \
            stage(nc, name, "loaded_even loaded_odd rounded split used") as (loaded_even, loaded_odd, rounded, split, used), \
            nc.Block() as block:
        loaded, a_high, a_low = (loaded_even, loaded_odd), (ah0, ah1), (al0, al1)
        pairs = K // 2
        flat = lambda ap: ap.rearrange("p a n -> p (a n)")
        tile = lambda j: flat(acts[:, bass.ds(j, 1), :])

        @block.sync
        def _(sp):
            def load(j, s):
                sp.dma_start(flat(raw[s]), weight[bass.ds(j * P, P), :]).then_inc(loaded[s], 16)

            load(0, 0)
            load(1, 1)
            if pairs > 1:
                with sp.Fori(0, pairs - 1) as i:
                    for s in range(2):
                        sp.wait_ge(split, i * 2 + s + 1)
                        load(i * 2 + s + 2, s)

        def run(engine, pair):
            pair(0, True, pairs == 1)
            if pairs > 2:
                with engine.Fori(1, pairs - 1) as i:
                    pair(i, False, False)
            if pairs > 1:
                pair(pairs - 1, False, True)

        @block.tensor
        def _(pe):
            def products(s, first, final):
                w_high, w_low = (flat(x) for x in parts[s])
                for t in range(TT):
                    part = slice(t * P, t * P + P)
                    for half in range(2):
                        to, cols = m.PS[:, 2 * t + half, :], slice(half * 512, half * 512 + 512)
                        nc.tensor.matmul(to, a_high[s][:, part], w_high[:, cols], start=first, stop=False)
                        nc.tensor.matmul(to, a_high[s][:, part], w_low[:, cols], start=False, stop=False)
                        last = nc.tensor.matmul(to, a_low[s][:, part], w_high[:, cols], start=False, stop=final)
                last.then_inc(used, 1)

            def pair(i, first, final):
                for s in range(2):
                    pe.wait_ge(split, i * 2 + s + 1)
                    products(s, first and s == 0, final and s == 1)

            run(pe, pair)

        @block.scalar
        def _(act):
            def pair(i, first, final):
                for s in range(2):
                    act.wait_ge(loaded[s], (i + 1) * 16)
                    if not first:
                        act.wait_ge(used, i * 2 + s - 1)
                    nc.scalar.activation(flat(parts[s][0]), flat(raw[s]), ACT.Copy)
                    nc.scalar.activation(a_high[s], tile(i * 2 + s), ACT.Copy).then_inc(rounded, 1)

            run(act, pair)
            act.wait_ge(used, K)
            for t in range(1, TT, 2):
                nc.scalar.activation(out[:, t, :], m.PS[:, 2 * t:2 * t + 2, :].rearrange("p b n -> p (b n)"), ACT.Copy)

        @block.vector
        def _(dve):
            def pair(i, first, final):
                for s in range(2):
                    dve.wait_ge(rounded, i * 2 + s + 1)
                    w_high, w_low = (flat(x) for x in parts[s])
                    nc.vector.tensor_tensor(w_low, flat(raw[s]), w_high.bitcast(F32), ALU.subtract)
                    nc.vector.tensor_tensor(a_low[s], tile(i * 2 + s), a_high[s].bitcast(F32), ALU.subtract).then_inc(split, 1)

            run(dve, pair)
            dve.wait_ge(used, K)
            for t in range(0, TT, 2):
                nc.vector.tensor_copy(out[:, t, :], m.PS[:, 2 * t:2 * t + 2, :].rearrange("p b n -> p (b n)"))


def turn_tiles(nc, m, name, src_of, K, dst):
    with stage(nc, name, "turned") as (turned,), nc.Block() as block:
        @block.tensor
        def _(pe):
            for k in range(K):
                for t in range(TT):
                    last = nc.tensor.transpose(m.PS[:, k, t * P:t * P + P], src_of(t, k), m.ident)
                last.then_inc(turned, 1)

        @block.vector
        def _(dve):
            for k in range(0, K, 2):
                dve.wait_ge(turned, k + 1)
                nc.vector.tensor_copy(dst[:, k, :], m.PS[:, k, :])

        @block.scalar
        def _(act):
            for k in range(1, K, 2):
                act.wait_ge(turned, k + 1)
                nc.scalar.activation(dst[:, k, :], m.PS[:, k, :], ACT.Copy)


def swiglu_up(nc, m, name, weight, h, acts):
    cols = weight.rearrange("(k p) (g n) -> p k g n", p=P, g=2)
    high, low = h
    with weight_ring(nc, K=DK, wide=2 * P, raw=2) as (raw, parts), \
            region(nc, "silu0", SEQ) as silu0, region(nc, "silu1", SEQ) as silu1, \
            stage(nc, name, "loaded_even loaded_odd rounded split product silu gated") as \
            (loaded_even, loaded_odd, rounded, split, product, silu, gated), nc.Block() as block:
        loaded, silus = (loaded_even, loaded_odd), (silu0, silu1)
        gate_up = lambda ap: ap.rearrange("p k (g c) -> p k g c", g=2)

        @block.sync
        def _(sp):
            def load(j, s):
                for g in range(2):
                    sp.dma_start(gate_up(raw[s])[:, :, g, :], cols[:, :, g, bass.ds(j * P, P)]).then_inc(loaded[s], 16)

            load(0, 0)
            load(1, 1)
            with sp.Fori(0, FK // 2 - 1) as i:
                for s in range(2):
                    sp.wait_ge(split, i * 2 + s + 1)
                    load(i * 2 + s + 2, s)

        @block.tensor
        def _(pe):
            def pair(i, first):
                for s in range(2):
                    pe.wait_ge(split, i * 2 + s + 1)
                    if not first:
                        pe.wait_ge(gated, i * 2 + s - 1)
                    w_high, w_low = (gate_up(x) for x in parts[s])
                    for g in range(2):
                        to = m.PS[:, 2 * s + g, :]
                        for k in range(DK):
                            nc.tensor.matmul(to, w_high[:, k, g, :], high[:, k, :], start=(k == 0), stop=False)
                            nc.tensor.matmul(to, w_high[:, k, g, :], low[:, k, :], start=False, stop=False)
                            last = nc.tensor.matmul(to, w_low[:, k, g, :], high[:, k, :], start=False, stop=(k == DK - 1))
                    last.then_inc(product, 1)

            pair(0, True)
            with pe.Fori(1, FK // 2) as i:
                pair(i, False)

        @block.scalar
        def _(act):
            def rounding(i, s, first):
                act.wait_ge(loaded[s], (i + 1) * 32)
                if not first:
                    act.wait_ge(product, i * 2 + s - 1)
                nc.scalar.activation(parts[s][0], raw[s], ACT.Copy).then_inc(rounded, 1)

            def silu_of(i, s, first):
                act.wait_ge(product, i * 2 + s + 1)
                if not first:
                    act.wait_ge(gated, i * 2 + s - 1)
                nc.scalar.activation(silus[s], m.PS[:, 2 * s, :], ACT.Silu).then_inc(silu, 1)

            rounding(0, 0, True)
            rounding(0, 1, True)
            silu_of(0, 0, True)
            rounding(1, 0, False)
            silu_of(0, 1, True)
            rounding(1, 1, False)
            with act.Fori(1, FK // 2 - 1) as i:
                silu_of(i, 0, False)
                rounding(i + 1, 0, False)
                silu_of(i, 1, False)
                rounding(i + 1, 1, False)
            silu_of(FK // 2 - 1, 0, False)
            silu_of(FK // 2 - 1, 1, False)

        @block.vector
        def _(dve):
            def rest(i, s):
                dve.wait_ge(rounded, i * 2 + s + 1)
                nc.vector.tensor_tensor(parts[s][1], raw[s], parts[s][0].bitcast(F32), ALU.subtract).then_inc(split, 1)

            def gating(i, s):
                dve.wait_ge(silu, i * 2 + s + 1)
                to = acts[:, bass.ds(i * 2 + s, 1), :].rearrange("p a n -> p (a n)")
                nc.vector.tensor_tensor(to, silus[s], m.PS[:, 2 * s + 1, :], ALU.mult).then_inc(gated, 1)

            rest(0, 0)
            rest(0, 1)
            with dve.Fori(0, FK // 2 - 1) as i:
                gating(i, 0)
                rest(i + 1, 0)
                gating(i, 1)
                rest(i + 1, 1)
            gating(FK // 2 - 1, 0)
            gating(FK // 2 - 1, 1)


def feed_forward(nc, m, name, w_in, w_out, pre, post):
    with region(nc, "ffn_acts", FK, SEQ) as acts:
        with split_acts(nc, "h", DK, SEQ) as h:
            norm_transpose(nc, m, name + "_pre", m.x, TT, pre, h, Arena(acts.rearrange("p j n -> p (j n)")))
            swiglu_up(nc, m, name + "_up", w_in, h, acts)
        project_model(nc, m, name + "_down", acts, FK, w_out, m.y)
    with region(nc, "scratch", TT * D + 64) as scratch:
        post_norm_add(nc, m, name + "_post", m.y, post, 0.5, Arena(scratch))



def attention(nc, m, proj, y, A):
    qT = A.take(QH // 2, SEQ)
    kT = A.take(KVH, P + SEQ)
    vp = A.take(TT + 1, KVH * HD)
    kdup = A.take(TT, KVH, 2, HD)
    Ss = [A.take(QH, 2 * P) for _ in range(2)]
    pT = A.take(2 * QH, P)
    tmp = A.take(4, TT, 10, 8)
    mxs, ess, den = [A.take(QH) for _ in range(2)], [A.take(QH) for _ in range(2)], A.take(QH)
    kq = ATTN_COLS - 2 * KVH * HD
    with stage(nc, "attn", "keys_dup turned_q turned_k dve scored shifted probs_act probs_turned turned_act turned_dve summed stored ready taken") as \
            (keys_dup, turned_q, turned_k, dve_chain, scored, shifted, probs, probs_turned, turned_act, turned_dve, summed,
             stored, ready, taken), nc.Block() as block:
        by_parity = lambda ap: ap.rearrange("p (j a) -> p a j", a=2)
        in_order = lambda ap: ap.rearrange("p (a j) -> p a j", a=2)
        sinks = by_parity(m.row("sinks"))
        place = lambda h: (h % 2) * (QH // 2) + h // 2

        @block.vector
        def _(dve):
            link = chain(dve, dve_chain)
            V = nc.vector
            for t in range(TT):
                heads = proj[:, t, 0:10 * HD].rearrange("p (h d) -> p h d", d=HD)
                x1, x2 = heads[:, :, 0:8], heads[:, :, 8:16]
                cos, sin = spread(m.cos[:, t, :], 1, 10), spread(m.sin[:, t, :], 1, 10)
                V.tensor_tensor(tmp[:, 0, t], x1, cos, ALU.mult)
                V.tensor_tensor(tmp[:, 1, t], x2, sin, ALU.mult)
                V.tensor_tensor(tmp[:, 2, t], x2, cos, ALU.mult)
                link(V.tensor_tensor(tmp[:, 3, t], x1, sin, ALU.mult))
                V.tensor_tensor(x1, tmp[:, 0, t], tmp[:, 1, t], ALU.subtract)
                link(V.tensor_tensor(x2, tmp[:, 2, t], tmp[:, 3, t], ALU.add))
                for twice in range(2):
                    last = V.tensor_copy(kdup[:, t, :, twice, :],
                                         proj[:, t, kq:kq + KVH * HD].rearrange("p (h d) -> p h d", d=HD))
            last.then_inc(keys_dup, 1)
            V.memset(kT[:, :, 0:P], 0.0)
            V.memset(vp[:, 0, :], 0.0)
            V.tensor_copy(vp[:, 1:TT + 1, :], proj[:, :, kq + KVH * HD:ATTN_COLS])
            dve.wait_ge(turned_q, 1)
            V.tensor_scalar(qT, m.PS[:, 0:4, :], HD ** -0.5, None, ALU.mult)
            dve.wait_ge(turned_k, 1)
            V.tensor_copy(kT[:, :, P:P + SEQ], m.PS[:, 4:6, :]).then_inc(ready, 1)

            def shift(n):
                S, mx, es = Ss[n % 2], mxs[n % 2], ess[n % 2]
                dve.wait_ge(scored, n + 1)
                scores = m.PS[:, 0:4, :].rearrange("p b (h k) -> p (b h) k", h=2)
                V.tensor_tensor(S, scores, spread(m.window[:, min(n, 1), :], 1, QH), ALU.add).then_inc(taken, 1)
                dve.wait_ge(taken, n + 1)
                link(V.tensor_reduce(mx, S, AX.X, ALU.max))
                link(V.tensor_tensor(in_order(mx), in_order(mx), sinks, ALU.max))
                V.tensor_tensor(in_order(es), sinks, in_order(mx), ALU.subtract)
                V.tensor_tensor(S, S, spread(mx, 2, 2 * P), ALU.subtract).then_inc(shifted, 1)

            shift(0)
            for n in range(TT):
                if n + 1 < TT:
                    if n:
                        dve.wait_ge(probs_turned, n)
                    shift(n + 1)
                S, es = Ss[n % 2], ess[n % 2]
                dve.wait_ge(probs, n + 1)
                link(V.tensor_reduce(den, S, AX.X, ALU.add))
                link(V.tensor_tensor(den, den, es, ALU.add))
                link(V.reciprocal(den, den))
                dve.wait_ge(probs_turned, n + 1)
                V.tensor_copy(pT[:, 0:QH, :], m.PS[:, 4:6, :].rearrange("p b (h k) -> p (b h) k", h=4)).then_inc(turned_dve, 1)
                dve.wait_ge(summed, n + 1)
                for a in range(2):
                    last = V.tensor_tensor(y[:, n, 0:QH * HD].rearrange("p (j a d) -> p a j d", a=2, d=HD)[:, a],
                                           m.PS[:, 4, :].rearrange("p (j a d) -> p a j d", a=2, d=HD)[:, a],
                                           spread(in_order(den)[:, a], 2, HD), ALU.mult)
                last.then_inc(stored, 1)
                dve.wait_ge(stored, n + 1)

        @block.scalar
        def _(act):
            for n in range(TT):
                act.wait_ge(shifted, n + 1)
                nc.scalar.activation(ess[n % 2], ess[n % 2], ACT.Exp)
                nc.scalar.activation(Ss[n % 2], Ss[n % 2], ACT.Exp).then_inc(probs, 1)
                act.wait_ge(probs_turned, n + 1)
                nc.scalar.activation(pT[:, QH:2 * QH, :], m.PS[:, 6:8, :].rearrange("p b (h k) -> p (b h) k", h=4),
                                     ACT.Copy).then_inc(turned_act, 1)

        @block.tensor
        def _(pe):
            pe.wait_ge(keys_dup, 1)
            for j in range(QH // 2):
                for t in range(TT):
                    last = nc.tensor.transpose(m.PS[:, j, t * P:t * P + P], proj[:, t, j * P:j * P + P], m.ident)
            last.then_inc(turned_q, 1)
            for j in range(KVH):
                for t in range(TT):
                    last = nc.tensor.transpose(m.PS[:, 4 + j, t * P:t * P + P],
                                               kdup[:, t, j].rearrange("p a d -> p (a d)"), m.ident)
            last.then_inc(turned_k, 1)
            pe.wait_ge(ready, 1)

            def score(n):
                if n:
                    pe.wait_ge(taken, n)
                for h in range(QH):
                    at = (h % 2) * HD
                    last = nc.tensor.matmul(m.PS[:, place(h) // 2, (place(h) % 2) * 2 * P:(place(h) % 2 + 1) * 2 * P],
                                            qT[at:at + HD, h // 2, n * P:n * P + P],
                                            kT[at:at + HD, h // (QH // KVH), n * P:n * P + 2 * P], start=True, stop=True)
                last.then_inc(scored, 1)

            score(0)
            for n in range(TT):
                if n + 1 < TT:
                    score(n + 1)
                pe.wait_ge(probs, n + 1)
                if n:
                    pe.wait_ge(stored, n)
                for h in range(QH):
                    for b in range(2):
                        i = 2 * h + b
                        last = nc.tensor.transpose(m.PS[:, 4 + i // 4, (i % 4) * P:(i % 4 + 1) * P],
                                                   Ss[n % 2][:, place(h), b * P:b * P + P], m.ident)
                last.then_inc(probs_turned, 1)
                pe.wait_ge(turned_dve, n + 1)
                pe.wait_ge(turned_act, n + 1)
                for h in range(QH):
                    kv = h // (QH // KVH)
                    for b in range(2):
                        last = nc.tensor.matmul(m.PS[:, 4, h * HD:h * HD + HD], pT[:, 2 * h + b, :],
                                                vp[:, n + b, kv * HD:kv * HD + HD], start=(b == 0), stop=(b == 1))
                last.then_inc(summed, 1)



def log1p_series(link, V, e, z, z2, out):
    link(V.tensor_scalar(z2, e, 2.0, None, ALU.add))
    link(V.reciprocal(z2, z2))
    link(V.tensor_tensor(z, e, z2, ALU.mult))
    link(V.tensor_tensor(z2, z, z, ALU.mult))
    link(V.tensor_scalar(out, z2, 1.0 / 17, None, ALU.mult))
    for n in (15, 13, 11, 9, 7, 5, 3):
        link(V.scalar_tensor_tensor(out, out, 1.0 / n, z2, ALU.add, ALU.mult))
    link(V.tensor_scalar(out, out, 1.0, 2.0, ALU.add, ALU.mult))
    link(V.tensor_tensor(out, out, z, ALU.mult))


def mlstm(nc, m, proj, y, A):
    xc = A.take(4, 3 + SEQ)
    qk = A.take(4, SEQ)
    gates = A.take(11, SEQ, parts=4)
    I, F, E, Z, Z2, L, G, C, M, EM, ONE = (gates[:, j, :] for j in range(11))
    ccol, ecol = A.take(TT, MH), A.take(TT, MH)
    pairs = [(j, i) for j in range(TT) for i in range(j, TT)]
    start = [pairs.index((j, j)) for j in range(TT)]
    W = A.take(MH, len(pairs), P)
    va = A.take(TT, MH, HD + 1)
    num = A.take(TT, MH, HD)
    den, ms = A.take(TT, MH), A.take(TT, MH)
    og = A.take(TT, MH, HD)
    iT, fT = m.PS[0:4, 4, :], m.PS[0:4, 5, :]

    with stage(nc, "mlstm1", "turned tanh_in tanh_out abs_in exp_out dve conv rows cols bcast dist weights") as \
            (turned, tanh_in, tanh_out, abs_in, exp_out, dve_chain, conv_done, rows_done, cols_done, bcast, dist, weights), \
            nc.Block() as block:
        @block.tensor
        def _(pe):
            for t in range(TT):
                nc.tensor.transpose(m.PS[0:4, 4, t * P:t * P + P], proj[:, t, ML_I:ML_I + MH], m.ident)
            for t in range(TT):
                last = nc.tensor.transpose(m.PS[0:4, 5, t * P:t * P + P], proj[:, t, ML_F:ML_F + MH], m.ident)
            last.then_inc(turned, 1)
            for j in range(4):
                for t in range(TT):
                    last = nc.tensor.transpose(m.PS[:, j, t * P:t * P + P],
                                               proj[:, t, ATTN_COLS + j * P:ATTN_COLS + j * P + P], m.ident)
            last.then_inc(turned, 1)
            pe.wait_ge(rows_done, 1)
            for t in range(TT):
                nc.tensor.transpose(m.PS[:, 6, t * 4:t * 4 + 4], C[:, t * P:t * P + P], m.ident[0:4, 0:4])
            for t in range(TT):
                last = nc.tensor.transpose(m.PS[:, 7, t * 4:t * 4 + 4], EM[:, t * P:t * P + P], m.ident[0:4, 0:4])
            last.then_inc(cols_done, 1)
            pe.wait_ge(conv_done, 1)
            for h in range(MH):
                last = nc.tensor.matmul(m.PS[:, h, :], m.pick[:, h, :], M, start=True, stop=True)
            last.then_inc(bcast, 1)

        @block.scalar
        def _(act):
            act.wait_ge(tanh_in, 1)
            nc.scalar.activation(I, I, ACT.Tanh)
            nc.scalar.activation(F, F, ACT.Tanh).then_inc(tanh_out, 1)
            act.wait_ge(abs_in, 1)
            nc.scalar.activation(E, E, ACT.Exp, scale=-1.0).then_inc(exp_out, 1)
            act.wait_ge(abs_in, 2)
            nc.scalar.activation(EM, EM, ACT.Exp, scale=-1.0).then_inc(rows_done, 1)
            act.wait_ge(dist, 1)
            nc.scalar.activation(W, W, ACT.Exp, scale=-1.0).then_inc(weights, 1)
            act.wait_ge(conv_done, 2)
            nc.scalar.activation(qk, qk, ACT.Silu)
            nc.scalar.activation(og, proj[:, :, ML_O:ML_O + MH * HD].rearrange("p t (h d) -> p t h d", d=HD), ACT.Sigmoid)

        @block.vector
        def _(dve):
            link = chain(dve, dve_chain)
            V = nc.vector
            dve.wait_ge(turned, 1)
            V.tensor_scalar(I, iT, m.col("i_bias")[0:4], 1 / GATE_CAP, ALU.add, ALU.mult)
            V.tensor_scalar(F, fT, m.col("f_bias")[0:4], 1 / GATE_CAP, ALU.add, ALU.mult).then_inc(tanh_in, 1)
            V.memset(ONE, 1.0)
            V.memset(xc[:, :, 0:3], 0.0)
            V.memset(va[:, :, :, HD:HD + 1], 1.0)
            V.tensor_copy(va[:, :, :, 0:HD], proj[:, :, ML_V:ML_V + MH * HD].rearrange("p t (h d) -> p t h d", d=HD))
            dve.wait_ge(turned, 2)
            V.tensor_copy(xc[:, :, 3:3 + SEQ], m.PS[:, 0:4, :]).then_inc(conv_done, 1)
            dve.wait_ge(tanh_out, 1)
            V.tensor_scalar(I, I, GATE_CAP, None, ALU.mult)
            link(V.tensor_scalar(F, F, GATE_CAP, None, ALU.mult))
            V.scalar_tensor_tensor(E, F, -1.0, F, ALU.mult, ALU.max).then_inc(abs_in, 1)
            dve.wait_ge(exp_out, 1)
            log1p_series(link, V, E, Z, Z2, L)
            link(V.scalar_tensor_tensor(L, F, 0.0, L, ALU.min, ALU.subtract))
            link(V.tensor_tensor_scan(G, ONE, L, 0.0, ALU.mult, ALU.add))
            link(V.tensor_tensor(C, I, G, ALU.subtract))
            link(V.tensor_tensor_scan(M, ONE, C, NEG, ALU.mult, ALU.max))
            V.tensor_tensor(EM, G, M, ALU.add).then_inc(abs_in, 1)
            dve.wait_ge(cols_done, 1)
            V.tensor_copy(ecol, m.PS[:, 7, 0:TT * MH].rearrange("p (t h) -> p t h", h=MH))
            link(V.tensor_copy(ccol, m.PS[:, 6, 0:TT * MH].rearrange("p (t h) -> p t h", h=MH)))
            dve.wait_ge(bcast, 1)
            for h in range(MH):
                for j in range(TT):
                    n = TT - j
                    last = V.tensor_scalar(W[:, h, start[j]:start[j] + n, :],
                                           m.PS[:, h, j * P:].rearrange("p (n k) -> p n k", k=P),
                                           ccol[:, j, h:h + 1], 0.0, ALU.subtract, ALU.max)
            last.then_inc(dist, 1)
            taps = m.col("conv").rearrange("p (j w) -> p j w", w=4)
            for j in range(4):
                last = V.tensor_scalar(qk[:, j, :], xc[:, j, 0:SEQ], taps[:, j, 0:1], None, ALU.mult)
            link(last)
            for w in range(1, 4):
                for j in range(4):
                    last = V.scalar_tensor_tensor(qk[:, j, :], xc[:, j, w:w + SEQ], taps[:, j, w:w + 1], qk[:, j, :],
                                                  ALU.mult, ALU.add)
                if w < 3:
                    link(last)
            last.then_inc(conv_done, 1)
            dve.wait_ge(weights, 1)
            for j in range(TT):
                V.tensor_tensor(W[:, :, start[j], :], W[:, :, start[j], :], spread(m.upper, 1, MH), ALU.mult)

    with stage(nc, "mlstm2", "scored weighted summed squares root dve") as (scored, weighted, summed, squares, root, dve_chain), \
            nc.Block() as block:
        @block.tensor
        def _(pe):
            for j in range(TT):
                if j >= 2:
                    pe.wait_ge(weighted, j - 1)
                for h in range(MH):
                    at = (h % 2) * HD
                    last = nc.tensor.matmul(m.PS[:, 4 * (j % 2) + h, 0:SEQ - j * P],
                                            qk[at:at + HD, 2 + h // 2, j * P:j * P + P],
                                            qk[at:at + HD, h // 2, j * P:SEQ], start=True, stop=True)
                last.then_inc(scored, 1)
            pe.wait_ge(weighted, TT)
            for i in range(TT):
                for h in range(MH):
                    for j in range(i + 1):
                        last = nc.tensor.matmul(m.PS[:, i, h * (HD + 1):(h + 1) * (HD + 1)], W[:, h, start[j] + i - j, :],
                                                va[:, j, h, :], start=(j == 0), stop=(j == i))
            last.then_inc(summed, 1)

        @block.vector
        def _(dve):
            link = chain(dve, dve_chain)
            V = nc.vector
            for j in range(TT):
                dve.wait_ge(scored, j + 1)
                for h in range(MH):
                    part = W[:, h, start[j]:start[j] + TT - j, :].rearrange("p n k -> p (n k)")
                    last = V.scalar_tensor_tensor(part, m.PS[:, 4 * (j % 2) + h, 0:SEQ - j * P], HD ** -0.5, part,
                                                  ALU.mult, ALU.mult)
                last.then_inc(weighted, 1)
            dve.wait_ge(summed, 1)
            sums = m.PS[:, 0:TT, 0:MH * (HD + 1)].rearrange("p t (h d) -> p t h d", d=HD + 1)
            link(V.tensor_copy(den, sums[:, :, :, HD]))
            link(V.scalar_tensor_tensor(den, den, -1.0, den, ALU.mult, ALU.max))
            link(V.tensor_tensor(den, den, ecol, ALU.max))
            link(V.reciprocal(den, den))
            for t in range(TT):
                last = V.tensor_tensor(num[:, t], sums[:, t, :, 0:HD], spread(den[:, t], 2, HD), ALU.mult)
            link(last)
            link(V.tensor_tensor(va[:, :, :, 0:HD], num, num, ALU.mult))
            link(V.tensor_reduce(ms, va[:, :, :, 0:HD], AX.X, ALU.add))
            V.tensor_scalar(ms, ms, 1.0 / HD, EPS, ALU.mult, ALU.add).then_inc(squares, 1)
            norm = m.row("mlstm_norm").rearrange("p (h d) -> p h d", d=HD)
            link(V.tensor_tensor(og, og, spread(norm, 1, TT), ALU.mult))
            dve.wait_ge(root, 1)
            link(V.reciprocal(ms, ms))
            for t in range(TT):
                last = V.tensor_tensor(num[:, t], num[:, t], spread(ms[:, t], 2, HD), ALU.mult)
            link(last)
            V.tensor_tensor(y[:, :, QH * HD:(QH + MH) * HD].rearrange("p t (h d) -> p t h d", d=HD), num, og, ALU.mult)

        @block.scalar
        def _(act):
            act.wait_ge(squares, 1)
            nc.scalar.activation(ms, ms, ACT.Sqrt).then_inc(root, 1)



def invert(nc, m, name, AT, A0, levels, A):
    N = 4 * TT
    XT, X, A0T, A2, A2T = (A.take(N, P) for _ in range(5))
    IA, IAT = X, XT
    with stage(nc, name, "product0 product1 dve0 dve1 act0 act1 own") as (product0, product1, dve0, dve1, act0, act1, own), \
            nc.Block() as block:
        products, by_dve, by_act = (product0, product1), (dve0, dve1), (act0, act1)
        H = N // 2
        part = lambda ap, g: ap[:, g * H:(g + 1) * H, :]
        low, high = ([m.PS[:, 4 * g + s:4 * g + s + 2, :].rearrange("p b (h k) -> p (b h) k", h=4) for g in range(2)]
                     for s in (0, 2))
        mask = lambda ap: spread(ap, 1, H)
        C, T1 = A0, A0T
        last_level = len(levels) - 1

        @block.tensor
        def _(pe):
            def multiply(g, dve_at, act_at, lows, highs):
                pe.wait_ge(by_dve[g], dve_at)
                if act_at:
                    pe.wait_ge(by_act[g], act_at)
                for to, pair in ((low[g], lows), (high[g], highs)):
                    if pair:
                        left, right = (part(x, g) for x in pair)
                        for i in range(H):
                            last = nc.tensor.matmul(to[:, i, :], left[:, i, :], right[:, i, :], start=True, stop=True)
                last.then_inc(products[g], 1)

            for g in range(2):
                multiply(g, 1, 0, (A0T, A0), (A0, A0T))
            for g in range(2):
                multiply(g, 2, 1, (A2T, IA), (A2, IAT))
            for g in range(2):
                multiply(g, 3, 1, (A2T, A2), (A2, A2T))
            for g in range(2):
                multiply(g, 4, 2, (A0T, X), (A0, XT))
            for n in range(len(levels)):
                for g in range(2):
                    multiply(g, 6 + 2 * n, 0, (C, X), None)
                for g in range(2):
                    multiply(g, 6 + 2 * n, 3 + n, (XT, T1) if n < last_level else None, (T1, XT))

        @block.scalar
        def _(act):
            def copy(g, round_, to, of):
                act.wait_ge(products[g], round_)
                nc.scalar.activation(part(to, g), of[g], ACT.Copy).then_inc(by_act[g], 1)

            for g in range(2):
                copy(g, 1, A2T, high)
            for g in range(2):
                copy(g, 3, A0T, high)
            for n in range(len(levels)):
                for g in range(2):
                    copy(g, 5 + 2 * n, T1, low)

        @block.vector
        def _(dve):
            link = chain(dve, own)
            V = nc.vector

            def add_both(g, round_, low_too=True):
                dve.wait_ge(products[g], round_)
                if low_too:
                    V.tensor_tensor(part(X, g), low[g], part(X, g), ALU.add)
                V.tensor_tensor(part(XT, g), high[g], part(XT, g), ALU.add).then_inc(by_dve[g], 1)

            for g in range(2):
                link(V.tensor_tensor(part(A0T, g), part(AT, g), mask(m.upper8), ALU.mult))
                V.tensor_tensor(part(IAT, g), part(A0T, g), mask(m.ident), ALU.add)
                V.tensor_tensor(part(IA, g), part(A0, g), mask(m.ident), ALU.add).then_inc(by_dve[g], 1)
            for g in range(2):
                dve.wait_ge(products[g], 1)
                V.tensor_copy(part(A2, g), low[g]).then_inc(by_dve[g], 1)
            for g in range(2):
                add_both(g, 2)
            for g in range(2):
                dve.wait_ge(products[g], 3)
                V.tensor_copy(part(A0, g), low[g]).then_inc(by_dve[g], 1)
            for n, b in enumerate(levels):
                for g in range(2):
                    add_both(g, 4 + 2 * n)
                    V.tensor_tensor(part(C, g), part(AT, g), mask(m.merge[b]), ALU.mult).then_inc(by_dve[g], 1)
            for g in range(2):
                add_both(g, 4 + 2 * len(levels), False)
    return XT



def rwkv(nc, m, proj, y, A, w_up, a_up, g_up):
    LC = 64
    NC = SEQ // LC
    N = 4 * TT
    place = lambda t, h: (h % 2) * 8 + t * 2 + h // 2
    g = A.take(TT, 256)
    bonus = A.take(TT, RH)
    vtok = A.take(TT, 256)
    rt, at_, bt, kt, bh, kh = (A.take(2, SEQ) for _ in range(6))
    pend = A.take(2, NC)
    stay = A.at
    fm = A.take(DK, SEQ)
    r, k, v, lora, gx = fm[:, 0:2], fm[:, 2:4], fm[:, 4:6], fm[:, 6], fm[:, 7]
    upw, gw = A.take(256), A.take(256)
    raw = A.take(DK, 1 + SEQ)
    B = Arena(m.A)
    lw, a, kk, t1, t2, reset = (B.take(2, SEQ) for _ in range(6))

    with stage(nc, "rwkv1", "loaded turned moved mixed lora_in lora_out gates gate_out squares root norm_sum dve expd exp_in bonus_out heads_out") as \
            (loaded, turned, moved, mixed, lora_in, lora_out, gates, gate_out, squares, root, norm_sum, dve_chain, expd, exp_in,
             bonus_out, heads_out), nc.Block() as block:
        @block.sync
        def _(sp):
            sp.dma_start(upw[0:64], w_up).then_inc(loaded, 16)
            sp.dma_start(upw[64:128], a_up).then_inc(loaded, 16)
            sp.dma_start(gw, g_up).then_inc(loaded, 16)

        @block.tensor
        def _(pe):
            for j in range(DK):
                for t in range(TT):
                    last = nc.tensor.transpose(m.PS[:, j, t * P:t * P + P], proj[:, t, RW + j * P:RW + j * P + P], m.ident)
            last.then_inc(turned, 1)
            pe.wait_ge(moved, 1)
            pe.wait_ge(loaded, 48)
            pe.wait_ge(lora_in, 1)
            for j in range(2):
                nc.tensor.matmul(m.PS[:, j, :], upw[0:64, j * P:j * P + P], lora[0:64], start=True, stop=True)
                last = nc.tensor.matmul(m.PS[:, 2 + j, :], upw[64:128, j * P:j * P + P], lora[64:128], start=True, stop=True)
            last.then_inc(lora_out, 1)
            for t in range(TT):
                last = nc.tensor.matmul(m.PS[:, 4 + t // 2, (t % 2) * 256:(t % 2 + 1) * 256], gx[:, t * P:t * P + P], gw,
                                        start=True, stop=True)
            last.then_inc(gate_out, 1)
            pe.wait_ge(squares, 1)
            for j in range(2):
                last = nc.tensor.matmul(m.PS[:, 6 + j, :], m.same[64], t1[:, j], start=True, stop=True)
            last.then_inc(norm_sum, 1)
            pe.wait_ge(squares, 2)
            for t in range(TT):
                for j in range(2):
                    last = nc.tensor.matmul(m.PS[:, 4, t * 4 + 2 * j:t * 4 + 2 * j + 2], t1[:, j, t * P:t * P + P],
                                            m.same[64][:, 0:P:64], start=True, stop=True)
            for t in range(TT):
                for j in range(2):
                    last = nc.tensor.transpose(m.PS[:, t // 2, (t % 2) * 256 + j * P:(t % 2) * 256 + j * P + P],
                                               v[:, j, t * P:t * P + P], m.ident)
            last.then_inc(bonus_out, 1)

        @block.scalar
        def _(act):
            act.wait_ge(mixed, 1)
            nc.scalar.activation(lora[0:64], lora[0:64], ACT.Tanh)
            nc.scalar.activation(gx, gx, ACT.Sigmoid).then_inc(lora_in, 1)
            act.wait_ge(lora_out, 1)
            for j in range(2):
                nc.scalar.activation(lw[:, j], m.PS[:, j, :], ACT.Sigmoid, bias=m.col("w0")[:, j:j + 1])
                nc.scalar.activation(a[:, j], m.PS[:, 2 + j, :], ACT.Sigmoid, bias=m.col("a0")[:, j:j + 1])\
                    .then_inc(gates, 1)
            act.wait_ge(norm_sum, 2)
            nc.scalar.activation(t2, t2, ACT.Sqrt).then_inc(root, 1)
            for i in range(3):
                act.wait_ge(exp_in, i + 1)
                src, dst, sign = ((t1, rt, 1.0), (t2, at_, 1.0), (t1, bt, -1.0))[i]
                nc.scalar.activation(dst, src, ACT.Exp, scale=sign).then_inc(expd, 1)
            act.wait_ge(exp_in, 4)
            nc.scalar.activation(bh, bh, ACT.Exp)
            nc.scalar.activation(pend, t1.rearrange("p a (c l) -> p a c l", l=LC)[:, :, :, LC - 1], ACT.Exp).then_inc(expd, 1)

        @block.vector
        def _(dve):
            link = chain(dve, dve_chain)
            V = nc.vector
            link(V.memset(raw[:, :, 0:1], 0.0))
            dve.wait_ge(turned, 1)
            V.memset(reset, 1.0)
            link(V.tensor_copy(raw[:, :, 1:1 + SEQ], m.PS[:, :, :]))
            V.memset(reset.rearrange("p a (c l) -> p a c l", l=LC)[:, :, :, 0:1], 0.0)
            link(V.tensor_tensor(fm, raw[:, :, 0:SEQ], raw[:, :, 1:1 + SEQ], ALU.subtract))
            for j in (6, 7, 0, 1, 2, 3, 4, 5):
                last = V.scalar_tensor_tensor(fm[:, j], fm[:, j], m.col("mu")[:, j:j + 1], raw[:, j, 1:1 + SEQ],
                                              ALU.mult, ALU.add)
                if j == 7:
                    last.then_inc(mixed, 1)
            last.then_inc(moved, 1)
            dve.wait_ge(moved, 1)
            for j in range(2):
                last = V.tensor_scalar(kk[:, j], k[:, j], m.col("k_k")[:, j:j + 1], None, ALU.mult)
            link(last)
            V.tensor_tensor(t1, kk, kk, ALU.mult).then_inc(squares, 1)
            dve.wait_ge(norm_sum, 1)
            V.tensor_scalar(t2, m.PS[:, 6:8, :], 1e-24, None, ALU.max).then_inc(norm_sum, 1)
            dve.wait_ge(root, 1)
            link(V.reciprocal(t2, t2))
            link(V.tensor_tensor(kk, kk, t2, ALU.mult))
            dve.wait_ge(gates, 2)
            link(V.tensor_scalar(t2, a, 1.0, None, ALU.subtract))
            for j in range(2):
                last = V.tensor_scalar(t2[:, j], t2[:, j], m.col("k_a")[:, j:j + 1], 1.0, ALU.mult, ALU.add)
            link(last)
            link(V.tensor_tensor(k, k, t2, ALU.mult))
            dve.wait_ge(gate_out, 1)
            link(V.tensor_copy(g, m.PS[:, 4:6, :].rearrange("p b (t n) -> p (b t) n", t=2)))
            link(V.tensor_tensor(t1, r, k, ALU.mult))
            for j in range(2):
                last = V.tensor_scalar(t1[:, j], t1[:, j], m.col("r_k")[:, j:j + 1], None, ALU.mult)
            last.then_inc(squares, 1)
            dve.wait_ge(bonus_out, 1)
            V.tensor_copy(vtok, m.PS[:, 0:2, :].rearrange("p b (t n) -> p (b t) n", t=2))
            link(V.tensor_copy(bonus, m.PS[:, 4, 0:16].rearrange("p (t h) -> p t h", h=RH)))
            link(V.tensor_scalar(lw, lw, -math.exp(-0.5), None, ALU.mult))
            for j in range(2):
                last = V.tensor_tensor_scan(t1[:, j], reset[:, j], lw[:, j], 0.0, ALU.mult, ALU.add)
            last.then_inc(exp_in, 1)
            dve.wait_ge(exp_in, 1)
            V.tensor_tensor(t2, t1, lw, ALU.subtract).then_inc(exp_in, 2)
            cum = t1.rearrange("p a (c l) -> p a c l", l=LC)
            V.tensor_tensor(bh.rearrange("p a (c l) -> p a c l", l=LC), spread(cum[:, :, :, LC - 1], 3, LC), cum,
                            ALU.subtract).then_inc(exp_in, 1)
            dve.wait_ge(expd, 4)
            link(V.tensor_tensor(a, a, kk, ALU.mult))
            V.tensor_tensor(rt, rt, r, ALU.mult)
            V.scalar_tensor_tensor(at_, at_, -1.0, kk, ALU.mult, ALU.mult)
            V.tensor_tensor(kt, bt, k, ALU.mult)
            V.tensor_tensor(kh, bh, k, ALU.mult)
            dve.wait_ge(dve_chain, 1)
            link(V.tensor_tensor(bt, bt, a, ALU.mult))
            V.tensor_tensor(bh, bh, a, ALU.mult)

    A.at = stay
    AbT, A0, AkT, RbT, RkT = (A.take(N, P) for _ in range(5))
    abk = A.take(TT, 3, 256)
    with stage(nc, "rwkv2", "turned scored dve act") as (turned, scored, dve_chain, act_chain), nc.Block() as block:
        @block.tensor
        def _(pe):
            for i in range(3):
                src = (at_, bh, kh)[i]
                for t in range(TT):
                    for j in range(2):
                        last = nc.tensor.transpose(m.PS[:, 2 * i + t // 2, (t % 2) * 256 + j * P:(t % 2) * 256 + j * P + P],
                                                   src[:, j, t * P:t * P + P], m.ident)
            last.then_inc(turned, 1)
            n = 0
            for left, right in ((bt, at_), (at_, bt), (kt, at_), (bt, rt), (kt, rt)):
                pe.wait_ge(dve_chain, n + 1)
                for t in range(TT):
                    for h in range(RH):
                        po, j = (h % 2) * HD, h // 2
                        last = nc.tensor.matmul(m.PS[:, place(t, h) // 4, (place(t, h) % 4) * P:(place(t, h) % 4 + 1) * P], left[po:po + HD, j, t * P:t * P + P],
                                                right[po:po + HD, j, t * P:t * P + P], start=True, stop=True)
                last.then_inc(scored, 1)
                n += 1

        @block.vector
        def _(dve):
            V = nc.vector
            dve.wait_ge(turned, 1)
            for i in range(3):
                last = V.tensor_copy(abk[:, :, i, :], m.PS[:, 2 * i:2 * i + 2, :].rearrange("p b (t n) -> p (b t) n", t=2))
            last.then_inc(dve_chain, 1)
            for n, (to, mask) in enumerate(((AbT, m.strict_upper64), (A0, m.lower8), (AkT, m.strict_upper64),
                                            (RbT, m.upper64), (RkT, m.upper64))):
                dve.wait_ge(scored, n + 1)
                V.tensor_tensor(to, m.PS[:, 0:4, :].rearrange("p b (h k) -> p (b h) k", h=4), spread(mask, 1, N), ALU.mult)\
                    .then_inc(dve_chain, 1)

    B = Arena(m.A)
    XT = invert(nc, m, "rwkv_inv", AbT, A0, (8, 16, 32), B)
    B.at = N * P

    zin = A0
    WU = AbT
    TTm, Hm = B.take(2, 2, NC // 2, HD), B.take(2, 2, NC // 2, HD)
    QT = B.take(2, SEQ)
    Nst = B.take(2, NC + 1, HD)
    y0 = B.take(TT, 256)
    with stage(nc, "rwkv3", "product dve act") as (product, dve_chain, act_chain), nc.Block() as block:
        flat = lambda ap: ap.rearrange("p b (h k) -> p (b h) k", h=4)
        diag = m.ident

        @block.tensor
        def _(pe):
            for t in range(TT):
                for h in range(RH):
                    last = nc.tensor.matmul(m.PS[:, place(t, h) // 8, (place(t, h) % 8) * HD:(place(t, h) % 8 + 1) * HD], AkT[:, place(t, h), :], vtok[:, t, h * HD:h * HD + HD],
                                            start=True, stop=True)
            last.then_inc(product, 1)
            pe.wait_ge(dve_chain, 1)
            for t in range(TT):
                for h in range(RH):
                    last = nc.tensor.matmul(m.PS[:, 4 + place(t, h) // 4, (place(t, h) % 4) * P:(place(t, h) % 4 + 1) * P], XT[:, place(t, h), :], zin[:, place(t, h), :],
                                            start=True, stop=True)
            last.then_inc(product, 1)
            pe.wait_ge(dve_chain, 2)
            for t in range(TT):
                for h in range(RH):
                    po, j = (h % 2) * HD, h // 2
                    last = nc.tensor.matmul(m.PS[po:po + HD, j, t * P:t * P + P], WU[:, place(t, h), 0:HD], RbT[:, place(t, h), :],
                                            start=True, stop=True)
            for c in range(NC):
                t, q = c // 2, (c % 2) * LC
                for h in range(RH):
                    po, j = (h % 2) * HD, h // 2
                    wu = WU[q:q + LC, place(t, h), :]
                    bt_, kt_ = abk[q:q + LC, t, 1, h * HD:h * HD + HD], abk[q:q + LC, t, 2, h * HD:h * HD + HD]
                    at = (4 * j + c // 2) * HD
                    nc.tensor.matmul(m.PS[po:po + HD, 2 + c % 2, at:at + HD], wu[:, 0:HD], bt_, start=True, stop=True)
                    nc.tensor.matmul(m.PS[po:po + HD, 4 + c % 2, at:at + HD], bt_, wu[:, HD:P], start=True, stop=False)
                    last = nc.tensor.matmul(m.PS[po:po + HD, 4 + c % 2, at:at + HD], kt_,
                                            vtok[q:q + LC, t, h * HD:h * HD + HD], start=False, stop=True)
            for t in range(TT):
                for h in range(RH):
                    to = m.PS[:, 6 + t // 2, (t % 2) * 256 + h * HD:(t % 2) * 256 + h * HD + HD]
                    nc.tensor.matmul(to, RbT[:, place(t, h), :], WU[:, place(t, h), HD:P], start=True, stop=False)
                    last = nc.tensor.matmul(to, RkT[:, place(t, h), :], vtok[:, t, h * HD:h * HD + HD], start=False, stop=True)
            last.then_inc(product, 1)
            for c in range(NC - 1):
                pe.wait_ge(dve_chain, 3 + c)
                for h in range(RH):
                    po, j = (h % 2) * HD, h // 2
                    last = nc.tensor.matmul(m.PS[po:po + HD, 0, j * HD:j * HD + HD], TTm[po:po + HD, c % 2, j, c // 2, :],
                                            Nst[po:po + HD, j, c, :], start=True, stop=True)
                last.then_inc(product, 1)
            pe.wait_ge(dve_chain, 3 + NC - 1)
            for c in range(NC):
                t, q = c // 2, (c % 2) * LC
                for h in range(RH):
                    po, j = (h % 2) * HD, h // 2
                    last = nc.tensor.matmul(m.PS[q:q + LC, 4 + h % 2, (t * 2 + j) * HD:(t * 2 + j) * HD + HD],
                                            QT[po:po + HD, j, c * LC:c * LC + LC], Nst[po:po + HD, j, c, :],
                                            start=True, stop=True)
            last.then_inc(product, 1)

        @block.vector
        def _(dve):
            V = nc.vector
            for a in range(2):
                V.tensor_copy(zin.rearrange("p (a t j) n -> p a t j n", a=2, j=2)[:, a, :, :, 0:HD],
                              abk[:, :, 0, :].rearrange("p t (j a d) -> p a t j d", a=2, d=HD)[:, a])
            V.memset(Nst[:, :, 0, :], 0.0)
            dve.wait_ge(product, 1)
            V.tensor_copy(zin[:, :, HD:P], m.PS[:, 0:2, :].rearrange("p b (n d) -> p (b n) d", d=HD)).then_inc(dve_chain, 1)
            dve.wait_ge(product, 2)
            V.tensor_copy(WU, flat(m.PS[:, 4:8, :])).then_inc(dve_chain, 1)
            dve.wait_ge(product, 3)
            V.tensor_tensor(QT, m.PS[:, 0:2, :], rt, ALU.add)
            V.tensor_copy(Hm.rearrange("p a j c n -> p a (j c n)"), m.PS[:, 4:6, :])
            V.tensor_copy(y0, m.PS[:, 6:8, :].rearrange("p b (t n) -> p (b t) n", t=2))
            for po in (0, HD):
                for j in range(2):
                    for c in range(NC):
                        last = V.scalar_tensor_tensor(TTm[po:po + HD, c % 2, j, c // 2, :], diag[po:po + HD, po:po + HD],
                                                      pend[po:po + HD, j, c:c + 1], m.PS[po:po + HD, 2 + c % 2, (4 * j + c // 2) * HD:(4 * j + c // 2 + 1) * HD],
                                                      ALU.mult, ALU.add)
            last.then_inc(dve_chain, 1)
            for c in range(NC - 1):
                dve.wait_ge(product, 4 + c)
                V.tensor_tensor(Nst[:, :, c + 1, :], m.PS[:, 0, 0:2 * HD].rearrange("p (j n) -> p j n", j=2), Hm[:, c % 2, :, c // 2, :],
                                ALU.add).then_inc(dve_chain, 1)
            dve.wait_ge(product, 4 + NC - 1)
            for a in range(2):
                part = y0.rearrange("p t (j a d) -> p a t j d", a=2, d=HD)[:, a]
                V.tensor_tensor(part, part, m.PS[:, 4 + a, :].rearrange("p (t j d) -> p t j d", t=TT, d=HD), ALU.add)

    yv, sq = y0, B.take(TT, RH, HD)
    mean, var = B.take(TT, RH), B.take(TT, RH)
    with stage(nc, "rwkv4", "squares root dve") as (squares, root, dve_chain), nc.Block() as block:
        y4 = yv.rearrange("p t (h d) -> p t h d", d=HD)
        v4 = vtok.rearrange("p t (h d) -> p t h d", d=HD)

        @block.vector
        def _(dve):
            link = chain(dve, dve_chain)
            V = nc.vector
            link(V.tensor_reduce(mean, y4, AX.X, ALU.add))
            link(V.tensor_scalar(mean, mean, 1.0 / HD, None, ALU.mult))
            for t in range(TT):
                last = V.tensor_tensor(y4[:, t], y4[:, t], spread(mean[:, t], 2, HD), ALU.subtract)
            link(last)
            link(V.tensor_tensor(sq, y4, y4, ALU.mult))
            link(V.tensor_reduce(var, sq, AX.X, ALU.add))
            V.tensor_scalar(var, var, 1.0 / HD, 64e-5, ALU.mult, ALU.add).then_inc(squares, 1)
            for t in range(TT):
                last = V.tensor_tensor(v4[:, t], v4[:, t], spread(bonus[:, t], 2, HD), ALU.mult)
            link(last)
            link(V.tensor_tensor(vtok, vtok, spread(m.row("ln_b"), 1, TT), ALU.add))
            dve.wait_ge(root, 1)
            link(V.reciprocal(var, var))
            for t in range(TT):
                last = V.tensor_tensor(y4[:, t], y4[:, t], spread(var[:, t], 2, HD), ALU.mult)
            link(last)
            link(V.tensor_tensor(yv, yv, spread(m.row("ln_w"), 1, TT), ALU.mult))
            link(V.tensor_tensor(yv, yv, vtok, ALU.add))
            V.tensor_tensor(y[:, :, (QH + MH) * HD:D], yv, g, ALU.mult)

        @block.scalar
        def _(act):
            act.wait_ge(squares, 1)
            nc.scalar.activation(var, var, ACT.Sqrt).then_inc(root, 1)



def gated_embedding(nc, m, p, w_gate, w_proj):
    with region(nc, "ple", TT * (D + D_PLE) + D_PLE // P * SEQ) as ple, region(nc, "scratch", TT * D + 64) as scratch:
        A = Arena(ple)
        gate = A.take(TT, D)
        pt = A.take(TT, D_PLE)
        pT = A.take(D_PLE // P, SEQ)
        with split_acts(nc, "h", DK, SEQ) as h:
            norm_transpose(nc, m, "ple_pre", m.x, TT, m.col("ple_pre"), h, Arena(scratch))
            project(nc, m, "ple_gate", h, w_gate, D, gate)
        with stage(nc, "ple_load", "loaded") as (loaded,), nc.Block() as block:
            @block.sync
            def _(sp):
                sp.dma_start(pt, p.rearrange("(t p) n -> p t n", p=P)).then_inc(loaded, 16)
                sp.wait_ge(loaded, 16)

            @block.scalar
            def _(act):
                nc.scalar.activation(gate, gate, ACT.Sigmoid)
        turn_tiles(nc, m, "ple_turn", lambda t, k: pt[:, t, k * P:k * P + P], D_PLE // P, pT)
        project_model(nc, m, "ple_proj", pT, D_PLE // P, w_proj, m.y)
        with stage(nc, "ple_mul", "done") as (done,), nc.Block() as block:
            @block.vector
            def _(dve):
                nc.vector.tensor_tensor(m.y, m.y, gate, ALU.mult).then_inc(done, 1)
        post_norm_add(nc, m, "ple_post", m.y, m.row("ple_post"), 1.0, Arena(scratch))


def first_layer(nc, m, w, l):
    def at(name):
        ap = w[name]
        names = "abc"[:len(ap.shape) - 1]
        sub = ap[bass.ds(l, 1)]
        return sub.rearrange(f"z {' '.join(names)} -> (z {names[0]}) {' '.join(names[1:])}")

    load_layer(nc, m, at("cols"), w["rows"][bass.ds(l, 1)], NCOL, NROW)
    m.table = (COLS, ROWS)
    feed_forward(nc, m, "ffn1", at("w_ffn1_in"), at("w_ffn1_out"), m.col("ffn1_pre"), m.row("ffn1_post"))
    with region(nc, "mix", TT * D_IN) as m.A:
        with split_acts(nc, "h", DK, SEQ) as h:
            norm_transpose(nc, m, "mix_pre", m.x, TT, m.col("mix_pre"), h, Arena(m.A))
            proj = m.A.rearrange("p (t n) -> p t n", t=TT)
            project(nc, m, "mix_in", h, at("w_in"), D_IN, proj)
        with region(nc, "mix_scratch", 22600) as scratch:
            attention(nc, m, proj, m.y, Arena(scratch))
            mlstm(nc, m, proj, m.y, Arena(scratch))
            rwkv(nc, m, proj, m.y, Arena(scratch), at("rwkv_w_up"), at("rwkv_a_up"), at("rwkv_g_up"))
        yT = Arena(m.A).take(DK, SEQ)
        turn_tiles(nc, m, "mix_turn", lambda t, k: m.y[:, t, k * P:k * P + P], DK, yT)
        project_model(nc, m, "mix_out", yT, DK, at("w_out"), m.y)
        post_norm_add(nc, m, "mix_post", m.y, m.row("mix_post"), 1.0, Arena(m.A))
    feed_forward(nc, m, "ffn2", at("w_ffn2_in"), at("w_ffn2_out"), m.col("ffn2_pre"), m.row("ffn2_post"))
    gated_embedding(nc, m, at("p"), at("w_ple_gate"), at("w_ple_proj"))



def convolve(V, link, tiles, taps, src, dst, bias=None):
    for j in tiles:
        if bias is None:
            last = V.tensor_scalar(dst[:, j, :], src[:, j, :], taps[:, j, 3:4], None, ALU.mult)
        else:
            last = V.tensor_scalar(dst[:, j, :], src[:, j, :], taps[:, j, 3:4], bias[:, j:j + 1], ALU.mult, ALU.add)
    link(last)
    for back in range(1, 4):
        for j in tiles:
            last = V.scalar_tensor_tensor(dst[:, j, back:], src[:, j, 0:SEQ - back], taps[:, j, 3 - back:4 - back],
                                          dst[:, j, back:], ALU.mult, ALU.add)
        link(last)


def rg_lru(nc, m, feats, yT, A, weights):
    gw = A.take(2, 4, HD)
    c, r, i, a, sq = (A.take(4, SEQ) for _ in range(5))
    lam = m.col("lam")
    la, e, z, z2, sp = (A.take(4) for _ in range(5))
    xr, gate = feats[:, 0:4], feats[:, 4:8]
    with stage(nc, "lru", "loaded dve lam_in lam_out mixed product gates la_in act squares root gelu") as \
            (loaded, dve_chain, lam_in, lam_out, mixed, product, gates, la_in, act_out, squares, root, gelu), \
            nc.Block() as block:
        @block.sync
        def _(sp_):
            for which in range(2):
                sp_.dma_start(gw[:, which], weights[which].rearrange("j p n -> p j n")).then_inc(loaded, 16)

        @block.tensor
        def _(pe):
            pe.wait_ge(loaded, 32)
            pe.wait_ge(mixed, 1)
            for which in range(2):
                for j in range(4):
                    for po in (0, HD):
                        last = nc.tensor.matmul(m.PS[po:po + HD, 4 * which + j, :], gw[po:po + HD, which, j, :],
                                                c[po:po + HD, j, :], start=True, stop=True)
                last.then_inc(product, 1)

        @block.scalar
        def _(act):
            act.wait_ge(lam_in, 1)
            nc.scalar.activation(e, la, ACT.Exp, scale=-1.0).then_inc(lam_out, 1)
            for which, (to, bias) in enumerate(((r, "ba"), (i, "bx"))):
                act.wait_ge(product, which + 1)
                for j in range(4):
                    last = nc.scalar.activation(to[:, j], m.PS[:, 4 * which + j, :], ACT.Sigmoid, bias=m.col(bias)[:, j:j + 1])
                last.then_inc(gates, 1)
            act.wait_ge(la_in, 1)
            nc.scalar.activation(a, r, ACT.Exp)
            nc.scalar.activation(sq, r, ACT.Tanh, scale=-1.0).then_inc(act_out, 1)
            nc.scalar.activation(gate, gate, ACT.Gelu_apprx_tanh).then_inc(gelu, 1)
            act.wait_ge(squares, 1)
            nc.scalar.activation(sq, sq, ACT.Sqrt).then_inc(root, 1)

        @block.vector
        def _(dve):
            link = chain(dve, dve_chain)
            V = nc.vector
            V.scalar_tensor_tensor(la, lam, -1.0, lam, ALU.mult, ALU.max).then_inc(lam_in, 1)
            convolve(V, link, range(4), m.col("conv_lru").rearrange("p (j w) -> p j w", w=4), xr, c, m.col("conv_b"))
            V.memset(z, 0.0).then_inc(mixed, 1)
            dve.wait_ge(lam_out, 1)
            dve.wait_ge(mixed, 1)
            log1p_series(link, V, e, z, z2, sp)
            link(V.tensor_scalar(la, lam, -1.0, 0.0, ALU.mult, ALU.max))
            link(V.tensor_tensor(sp, sp, la, ALU.add))
            link(V.tensor_scalar(sp, sp, -8.0, None, ALU.mult))
            dve.wait_ge(gates, 2)
            for j in range(4):
                last = V.tensor_scalar(r[:, j], r[:, j], sp[:, j:j + 1], None, ALU.mult)
            last.then_inc(la_in, 1)
            link(V.tensor_tensor(i, i, c, ALU.mult))
            dve.wait_ge(act_out, 1)
            link(V.tensor_tensor(r, a, a, ALU.mult))
            V.scalar_tensor_tensor(sq, r, 1.0, sq, ALU.add, ALU.mult).then_inc(squares, 1)
            dve.wait_ge(root, 1)
            link(V.tensor_tensor(i, i, sq, ALU.mult))
            for j in range(4):
                last = V.tensor_tensor_scan(c[:, j], a[:, j], i[:, j], 0.0, ALU.mult, ALU.add)
            link(last)
            dve.wait_ge(gelu, 1)
            V.tensor_tensor(yT, c, gate, ALU.mult)


def delta_net(nc, m, f, zab, yT, A):
    N = 4 * TT
    araw, beta, g, e, z, z2, gcol, eg, kds, egl = (A.take(N) for _ in range(10))
    start = A.at
    cv, sq = A.take(12, SEQ), A.take(8, SEQ)
    taps = m.col("conv_qkv").rearrange("p (j w) -> p j w", w=4)
    th = lambda ap: ap.rearrange("p (t h) -> p t h", h=4)

    with stage(nc, "gdn1", "dve conv silu squared summed shifted root") as (dve_chain, conv, silu, squared, summed, shifted, root), \
            nc.Block() as block:
        @block.vector
        def _(dve):
            link = chain(dve, dve_chain)
            V = nc.vector
            for part in range(3):
                convolve(V, link, range(4 * part, 4 * part + 4), taps, f, cv)
                V.memset(e, 0.0).then_inc(conv, 1)
            for half in range(2):
                dve.wait_ge(summed, half + 1)
                V.tensor_scalar(sq[:, 4 * half:4 * half + 4], m.PS[:, 4 * half:4 * half + 4, :], EPS, None, ALU.add)\
                    .then_inc(shifted, 1)
            for half in range(2):
                dve.wait_ge(root, half + 1)
                part = slice(4 * half, 4 * half + 4)
                link(V.reciprocal(sq[:, part], sq[:, part]))
                V.scalar_tensor_tensor(f[:, part].rearrange("p a b -> p (a b)"), cv[:, part].rearrange("p a b -> p (a b)"),
                                       (P ** -0.5, 1.0)[half], sq[:, part].rearrange("p a b -> p (a b)"), ALU.mult, ALU.mult)

        @block.scalar
        def _(act):
            for part in range(3):
                act.wait_ge(conv, part + 1)
                tiles = slice(4 * part, 4 * part + 4)
                to = cv[:, tiles] if part < 2 else f[:, tiles]
                nc.scalar.activation(to, cv[:, tiles], ACT.Silu).then_inc(silu, 1)
                if part < 2:
                    act.wait_ge(silu, part + 1)
                    nc.scalar.activation(sq[:, tiles], cv[:, tiles], ACT.Square).then_inc(squared, 1)
            for half in range(2):
                act.wait_ge(shifted, half + 1)
                tiles = slice(4 * half, 4 * half + 4)
                nc.scalar.activation(sq[:, tiles], sq[:, tiles], ACT.Sqrt).then_inc(root, 1)

        @block.tensor
        def _(pe):
            for half in range(2):
                pe.wait_ge(squared, half + 1)
                for j in range(4 * half, 4 * half + 4):
                    last = nc.tensor.matmul(m.PS[:, j, :], m.ones, sq[:, j, :], start=True, stop=True)
                last.then_inc(summed, 1)

    A.at = start
    DT, D_, attnT, AT, QT = (A.take(N, P) for _ in range(5))
    zin = A.take(N, 2 * P)
    kd = A.take(N, P)
    kbT = A.take(N, P)
    bb, gb, A0 = AT, attnT, D_
    four = lambda ap, h0: ap[:, h0:h0 + 4, :].rearrange("p h (t k) -> p t h k", t=TT)
    banks = lambda b: m.PS[:, b:b + 4, :].rearrange("p b (h k) -> p (b h) k", h=4)
    banks4 = lambda b: m.PS[:, b:b + 4, :].rearrange("p b (h k) -> p b h k", h=4)
    view4 = lambda ap: ap.rearrange("p (t h) k -> p t h k", h=4)
    with stage(nc, "gdn2", "dve abs_in exp_out product copies dist act_out") as (dve_chain, abs_in, exp_out, product, copies, dist, act_out), \
            nc.Block() as block:
        @block.vector
        def _(dve):
            link = chain(dve, dve_chain)
            V = nc.vector
            link(V.tensor_tensor(th(araw), zab[:, :, 512:516], spread(m.row("dt_bias"), 1, TT), ALU.add))
            link(V.scalar_tensor_tensor(e, araw, -1.0, araw, ALU.mult, ALU.max))
            V.tensor_copy(th(beta), zab[:, :, 516:520]).then_inc(abs_in, 1)
            dve.wait_ge(exp_out, 1)
            log1p_series(link, V, e, z, z2, g)
            link(V.scalar_tensor_tensor(g, araw, 0.0, g, ALU.max, ALU.add))
            link(V.scalar_tensor_tensor(th(g), th(g), -1.0, spread(m.row("a_log"), 1, TT), ALU.mult, ALU.mult))
            V.tensor_copy(gb, spread(g, 2, P))
            V.tensor_copy(bb, spread(beta, 2, P)).then_inc(copies, 1)
            dve.wait_ge(product, 1)
            link(V.tensor_copy(gcol, m.PS[:, 4, 0:N]))
            V.tensor_copy(egl, banks(0)[:, :, P - 1])
            link(V.tensor_tensor(DT, banks(0), spread(gcol, 2, P), ALU.subtract))
            V.tensor_tensor(kds, egl, gcol, ALU.subtract)
            V.tensor_scalar(D_, DT, -1.0, 0.0, ALU.mult, ALU.min)
            link(V.tensor_scalar(DT, DT, 0.0, None, ALU.min))
            V.memset(z, 0.0).then_inc(dist, 1)
            dve.wait_ge(product, 2)
            V.tensor_tensor(view4(kbT), four(f, 4), banks4(4), ALU.mult)
            dve.wait_ge(act_out, 1)
            V.tensor_tensor(DT, DT, spread(m.upper, 1, N), ALU.mult)
            V.tensor_tensor(D_, D_, spread(m.lower8, 1, N), ALU.mult)
            V.tensor_tensor(view4(QT), four(f, 0), view4(QT), ALU.mult)

        @block.scalar
        def _(act):
            act.wait_ge(abs_in, 1)
            nc.scalar.activation(e, e, ACT.Exp, scale=-1.0)
            nc.scalar.activation(m.row("a_log"), m.row("a_log"), ACT.Exp)
            nc.scalar.activation(beta, beta, ACT.Sigmoid).then_inc(exp_out, 1)
            act.wait_ge(dist, 1)
            nc.scalar.activation(QT, banks(0), ACT.Exp)
            nc.scalar.activation(DT, DT, ACT.Exp)
            nc.scalar.activation(D_, D_, ACT.Exp)
            nc.scalar.activation(eg, gcol, ACT.Exp)
            nc.scalar.activation(kds, kds, ACT.Exp)
            nc.scalar.activation(egl, egl, ACT.Exp).then_inc(act_out, 1)

        @block.tensor
        def _(pe):
            pe.wait_ge(copies, 1)
            nc.tensor.matmul(m.PS[:, 4, 0:N], m.upper, g, start=True, stop=True)
            for n in range(N):
                last = nc.tensor.matmul(banks(0)[:, n, :], gb[:, n, :], m.upper, start=True, stop=True)
            last.then_inc(product, 1)
            pe.wait_ge(dist, 1)
            for n in range(N):
                last = nc.tensor.matmul(banks(4)[:, n, :], bb[:, n, :], m.ident, start=True, stop=True)
            last.then_inc(product, 1)

    with stage(nc, "gdn3", "product dve turned") as (product, dve_chain, turned), nc.Block() as block:
        @block.vector
        def _(dve):
            V = nc.vector
            link = chain(dve, dve_chain)
            dve.wait_ge(product, 1)
            link(V.scalar_tensor_tensor(AT, banks(0), -1.0, DT, ALU.mult, ALU.mult))
            V.tensor_tensor(AT, AT, spread(m.strict_upper, 1, N), ALU.mult)
            dve.wait_ge(product, 2)
            link(V.scalar_tensor_tensor(A0, banks(4), -1.0, D_, ALU.mult, ALU.mult))
            dve.wait_ge(product, 3)
            link(V.tensor_tensor(attnT, banks(0), DT, ALU.mult))
            dve.wait_ge(turned, 1)
            V.tensor_tensor(zin[:, :, 0:P], banks(4), spread(beta, 2, P), ALU.mult)
            link(V.tensor_tensor(eg, eg, beta, ALU.mult))
            dve.wait_ge(turned, 2)
            V.tensor_tensor(kd, banks(0), spread(kds, 2, P), ALU.mult)
            V.tensor_tensor(zin[:, :, P:2 * P], banks(0), spread(eg, 2, P), ALU.mult)

        @block.tensor
        def _(pe):
            def scores(b, left, right, lk, rk):
                for t in range(TT):
                    for h in range(4):
                        lo = left[:, t * 4 + h, :] if lk is None else left[:, lk + h, t * P:t * P + P]
                        hi = right[:, t * 4 + h, :] if rk is None else right[:, rk + h, t * P:t * P + P]
                        last = nc.tensor.matmul(banks(b)[:, t * 4 + h, :], lo, hi, start=True, stop=True)
                last.then_inc(product, 1)

            scores(0, f, kbT, 4, None)
            scores(4, kbT, f, None, 4)
            pe.wait_ge(dve_chain, 1)
            scores(0, f, f, 4, 0)
            pe.wait_ge(dve_chain, 2)
            for b, head0, after in ((4, 8, None), (0, 4, 3)):
                if after:
                    pe.wait_ge(dve_chain, after)
                for t in range(TT):
                    for h in range(4):
                        last = nc.tensor.transpose(banks(b)[:, t * 4 + h, :], f[:, head0 + h, t * P:t * P + P], m.ident)
                last.then_inc(turned, 1)

    B = Arena(m.A)
    XT = invert(nc, m, "gdn_inv", AT, A0, (8, 16, 32, 64), B)
    B.at = N * P
    UW = B.take(N, 2 * P)
    Nst = B.take(TT + 1, GH, P)
    TTm, Hm, y0 = AT, A0, DT
    with stage(nc, "gdn4", "product dve") as (product, dve_chain), nc.Block() as block:
        @block.tensor
        def _(pe):
            for n in range(N):
                last = nc.tensor.matmul(m.PS[:, n // 2, (n % 2) * 256:(n % 2 + 1) * 256], XT[:, n, :], zin[:, n, :],
                                        start=True, stop=True)
            last.then_inc(product, 1)
            pe.wait_ge(dve_chain, 1)
            for n in range(N):
                nc.tensor.matmul(banks(0)[:, n, :], UW[:, n, P:2 * P], attnT[:, n, :], start=True, stop=True)
            for n in range(N):
                last = nc.tensor.matmul(banks(4)[:, n, :], UW[:, n, P:2 * P], kd[:, n, :], start=True, stop=True)
            last.then_inc(product, 1)
            pe.wait_ge(dve_chain, 2)
            for n in range(N):
                nc.tensor.matmul(banks(0)[:, n, :], kd[:, n, :], UW[:, n, 0:P], start=True, stop=True)
            for n in range(N):
                last = nc.tensor.matmul(banks(4)[:, n, :], attnT[:, n, :], UW[:, n, 0:P], start=True, stop=True)
            last.then_inc(product, 1)
            for t in range(TT - 1):
                pe.wait_ge(dve_chain, 3 + t)
                for h in range(GH):
                    last = nc.tensor.matmul(m.PS[:, 0, h * P:h * P + P], TTm[:, t * 4 + h, :], Nst[:, t, h, :],
                                            start=True, stop=True)
                last.then_inc(product, 1)
            pe.wait_ge(dve_chain, 3 + TT - 1)
            for n in range(N):
                last = nc.tensor.matmul(banks(4)[:, n, :], QT[:, n, :], Nst[:, n // 4, n % 4, :], start=True, stop=True)
            last.then_inc(product, 1)

        @block.vector
        def _(dve):
            V = nc.vector
            V.memset(Nst[:, 0], 0.0)
            dve.wait_ge(product, 1)
            V.tensor_copy(UW, m.PS[:, :, :].rearrange("p b (n k) -> p (b n) k", n=2)).then_inc(dve_chain, 1)
            dve.wait_ge(product, 2)
            V.tensor_tensor(QT, QT, banks(0), ALU.subtract)
            for n in range(N):
                last = V.scalar_tensor_tensor(TTm[:, n, :], m.ident, egl[:, n:n + 1], banks(4)[:, n, :], ALU.mult, ALU.subtract)
            last.then_inc(dve_chain, 1)
            dve.wait_ge(product, 3)
            V.tensor_copy(y0, banks(4))
            V.tensor_copy(Hm, banks(0)).then_inc(dve_chain, 1)
            for t in range(TT - 1):
                dve.wait_ge(product, 4 + t)
                if t == 0:
                    dve.wait_ge(dve_chain, 3)
                V.tensor_tensor(Nst[:, t + 1], m.PS[:, 0, :].rearrange("p (h k) -> p h k", h=GH),
                                Hm[:, 4 * t:4 * t + 4, :], ALU.add).then_inc(dve_chain, 1)
            dve.wait_ge(product, 4 + TT - 1)
            V.tensor_tensor(y0, y0, banks(4), ALU.add)

    ms, o2 = z, QT
    with stage(nc, "gdn5", "squares root dve silu gated turned") as (squares, root, dve_chain, silu, gated, turned), \
            nc.Block() as block:
        zz = zab[:, :, 0:512].rearrange("p t (h k) -> p t h k", h=4)

        @block.vector
        def _(dve):
            link = chain(dve, dve_chain)
            V = nc.vector
            link(V.tensor_tensor(o2, y0, y0, ALU.mult))
            link(V.tensor_reduce(ms, o2, AX.X, ALU.add))
            V.tensor_scalar(ms, ms, 1.0 / P, EPS, ALU.mult, ALU.add).then_inc(squares, 1)
            dve.wait_ge(root, 1)
            link(V.reciprocal(ms, ms))
            link(V.tensor_tensor(y0, y0, spread(ms, 2, P), ALU.mult))
            link(V.tensor_tensor(y0, y0, spread(m.row("gdn_norm"), 1, N), ALU.mult))
            dve.wait_ge(silu, 1)
            V.tensor_tensor(view4(y0), view4(y0), zz, ALU.mult).then_inc(gated, 1)
            dve.wait_ge(turned, 1)
            V.tensor_copy(yT, m.PS[:, 0:4, :])

        @block.scalar
        def _(act):
            nc.scalar.activation(zz, zz, ACT.Silu).then_inc(silu, 1)
            act.wait_ge(squares, 1)
            nc.scalar.activation(ms, ms, ACT.Sqrt).then_inc(root, 1)

        @block.tensor
        def _(pe):
            pe.wait_ge(gated, 1)
            for h in range(4):
                for t in range(TT):
                    last = nc.tensor.transpose(m.PS[:, h, t * P:t * P + P], y0[:, t * 4 + h, :], m.ident)
            last.then_inc(turned, 1)


def add_to_x(nc, m, name, y):
    with stage(nc, name, "added") as (added,), nc.Block() as block:
        @block.vector
        def _(dve):
            nc.vector.tensor_tensor(m.x, m.x, y, ALU.add).then_inc(added, 1)


def hybrid_mixer(nc, m, w):
    w_in = w["w_in_2"]
    with region(nc, "hybrid", 22 * SEQ + 64) as m.A, region(nc, "zab", TT, 520) as zab:
        A = Arena(m.A)
        qkv = A.take(12, SEQ)
        lru_f = A.take(8, SEQ)
        with split_acts(nc, "h", DK, SEQ) as h:
            norm_transpose(nc, m, "hyb_pre", m.x, TT, m.col("mix"), h, Arena(m.A))
            project(nc, m, "hyb_qkv", h, w_in[:, 0:G_Z], 3 * GQK, qkv, features=True)
            project(nc, m, "hyb_lru", h, w_in[:, G_XR:IN2], 1024, lru_f, features=True)
            project(nc, m, "hyb_z", h, w_in[:, G_Z:G_XR], 520, zab)
        with region(nc, "hybrid_scratch", 18700) as scratch:
            rg_lru(nc, m, lru_f, m.hT[:, 4:8], Arena(scratch), w["lru_w_2"])
            delta_net(nc, m, qkv, zab, m.hT[:, 0:4], Arena(scratch))
    with region(nc, "mixed", TT, D) as y:
        project_model(nc, m, "hyb_out", m.hT, DK, w["w_out_2"], y)
        add_to_x(nc, m, "hyb_add", y)



def cross_attention(nc, m, w):
    with ExitStack() as room:
        kT = room.enter_context(region(nc, "xa_kT", DK, MEM))
        v = room.enter_context(region(nc, "xa_v", 2, D))
        big = room.enter_context(region(nc, "xa", DK * SEQ + 4 * TT * MEM + 64))
        B = Arena(big)
        qT = B.take(DK, SEQ)
        keep = B.at
        with stage(nc, "mem_in", "loaded") as (loaded,), nc.Block() as block:
            mem = B.take(2, D)

            @block.sync
            def _(sp):
                sp.dma_start(mem, w["mem_2"].rearrange("(t p) n -> p t n", p=P)).then_inc(loaded, 16)
                sp.wait_ge(loaded, 16)
        with split_acts(nc, "mem", DK, MEM) as h:
            norm_transpose(nc, m, "xa_mem", mem, 2, m.col("mem"), h, Arena(big))
            project(nc, m, "xa_k", h, w["xattn_wkv_2"][:, 0:D], D, kT, T=2, features=True)
            project(nc, m, "xa_v", h, w["xattn_wkv_2"][:, D:2 * D], D, v, T=2)
        with split_acts(nc, "h", DK, SEQ) as h:
            norm_transpose(nc, m, "xa_pre", m.x, TT, m.col("xattn"), h, Arena(big))
            project(nc, m, "xa_q", h, w["xattn_wq_2"], D, qT, features=True)
        B.at = keep
        attend_memory(nc, m, qT, kT, v, B)
    with region(nc, "attended", TT, D) as y:
        project_model(nc, m, "xa_out", m.hT, DK, w["xattn_wo_2"], y)
        add_to_x(nc, m, "xa_add", y)


def attend_memory(nc, m, qT, kT, v, B):
    N = TT * XH
    S = B.take(N, MEM)
    mx, den = B.take(N), B.take(N)
    pT = qT
    with stage(nc, "xa", "scored dve act probs turned copied product copied_act") as \
            (scored, dve_chain, act_out, probs, turned, copied, product, copied_act), nc.Block() as block:
        @block.tensor
        def _(pe):
            for t in range(TT):
                for h in range(XH):
                    for b in range(2):
                        last = nc.tensor.matmul(m.PS[:, 2 * t + h // 2, (h % 2) * MEM:(h % 2 + 1) * MEM],
                                                qT[:, 2 * h + b, t * P:t * P + P], kT[:, 2 * h + b, :],
                                                start=(b == 0), stop=(b == 1))
            last.then_inc(scored, 1)
            pe.wait_ge(probs, 1)
            for h in range(XH):
                for b in range(2):
                    for t in range(TT):
                        last = nc.tensor.transpose(m.PS[:, 2 * h + b, t * P:t * P + P], S[:, t * XH + h, b * P:b * P + P], m.ident)
            last.then_inc(turned, 1)
            pe.wait_ge(copied, 1)
            pe.wait_ge(copied_act, 1)
            for h in range(XH):
                for half in range(2):
                    for b in range(2):
                        last = nc.tensor.matmul(m.PS[:, 2 * h + half, :], v[:, b, h * 256 + half * P:h * 256 + half * P + P],
                                                pT[:, 2 * h + b, :], start=(b == 0), stop=(b == 1))
            last.then_inc(product, 1)

        @block.vector
        def _(dve):
            link = chain(dve, dve_chain)
            V = nc.vector
            dve.wait_ge(scored, 1)
            scores = m.PS[:, :, :].rearrange("p b (h k) -> p (b h) k", h=2)
            link(V.tensor_reduce(mx, scores, AX.X, ALU.max))
            link(V.tensor_tensor(S, scores, spread(mx, 2, MEM), ALU.subtract))
            dve.wait_ge(act_out, 1)
            link(V.tensor_reduce(den, S, AX.X, ALU.add))
            link(V.reciprocal(den, den))
            V.tensor_tensor(S, S, spread(den, 2, MEM), ALU.mult).then_inc(probs, 1)
            dve.wait_ge(turned, 1)
            V.tensor_copy(pT[:, 0:4], m.PS[:, 0:4, :]).then_inc(copied, 1)
            dve.wait_ge(product, 1)
            V.tensor_copy(m.hT[:, 0:4], m.PS[:, 0:4, :])

        @block.scalar
        def _(act):
            act.wait_ge(dve_chain, 2)
            nc.scalar.activation(S, S, ACT.Exp, scale=256 ** -0.5).then_inc(act_out, 1)
            act.wait_ge(turned, 1)
            nc.scalar.activation(pT[:, 4:8], m.PS[:, 4:8, :], ACT.Copy).then_inc(copied_act, 1)
            act.wait_ge(product, 1)
            nc.scalar.activation(m.hT[:, 4:8], m.PS[:, 4:8, :], ACT.Copy)



def peer(nc, m, w):
    with ExitStack() as room:
        keep = room.enter_context(region(nc, "peer_keep", TT * D + 4 * TT * PH * TOPK))
        B = Arena(keep)
        qT = room.enter_context(region(nc, "peer_q", 2 * PH, SEQ))
        sub = room.enter_context(region(nc, "subkeys", 2 * PH, NKEY))
        with split_acts(nc, "h", DK, SEQ) as h:
            norm_transpose(nc, m, "peer_pre", m.x, TT, m.col("ffn"), h, B)
            xn = keep[:, 8:8 + TT * D].rearrange("p (t n) -> p t n", t=TT)
            project(nc, m, "peer_q", h, w["peer_wq_2"], 2 * PH * P, qT, features=True)
        with region(nc, "peer_scratch", 10000) as m.R:
            idx, gate, dots = choose_experts(nc, m, w, B, qT, sub, xn)
        with region(nc, "peer_rows", 18 * D + 64) as m.R:
            gather(nc, m, "peer_u", w["peer_u_2"], idx, xn, dots, None)
            with stage(nc, "peer_act", "gelu done") as (gelu, done), nc.Block() as block:
                @block.scalar
                def _(act):
                    nc.scalar.activation(dots, dots, ACT.Gelu_apprx_tanh).then_inc(gelu, 1)

                @block.vector
                def _(dve):
                    dve.wait_ge(gelu, 1)
                    nc.vector.tensor_tensor(dots, dots, gate, ALU.mult).then_inc(done, 1)
            gather(nc, m, "peer_v", w["peer_v_2"], idx, None, dots, m.x)


def choose_experts(nc, m, w, B, qT, sub, xn):
    NE = PH * TOPK
    idx = B.take(TT, NE, dtype=U32)
    gate = B.take(TT, NE)
    dots = B.take(TT, NE)
    iota = B.take(TOPK)
    iota_i = B.take(TOPK, dtype=I32)
    R2 = Arena(m.R)
    sc = R2.take(2 * PH, NKEY)
    vals, ids_f = R2.take(2 * PH, TOPK), R2.take(2 * PH, TOPK)
    ids = R2.take(2 * PH, TOPK, dtype=U32)
    cand = R2.take(PH, TOPK, TOPK)
    best, pos = R2.take(PH, TOPK), R2.take(PH, TOPK, dtype=U32)
    half_u = R2.take(PH, TOPK, dtype=U32)
    half_f, e12 = R2.take(PH, TOPK), R2.take(2, NE)
    den = R2.take(PH)
    flatc = cand.rearrange("p h i j -> p h (i j)")
    with stage(nc, "peer_top", "loaded scored taken dve iota_done exp_in exp_out") as \
            (loaded, scored, taken, dve_chain, iota_done, exp_in, exp_out), nc.Block() as block:
        @block.sync
        def _(sp):
            sp.dma_start(sub, w["subkeys_2"]).then_inc(loaded, 16)

        @block.gpsimd
        def _(pool):
            nc.gpsimd.iota(iota_i, pattern=[[1, TOPK]], base=0, channel_multiplier=0).then_inc(iota_done, 1)

        @block.tensor
        def _(pe):
            pe.wait_ge(loaded, 16)
            for t in range(TT):
                if t >= 2:
                    pe.wait_ge(taken, t - 1)
                for n in range(2 * PH):
                    last = nc.tensor.matmul(m.PS[:, 4 * (t % 2) + n // 4, (n % 4) * P:(n % 4 + 1) * P],
                                            qT[:, n, t * P:t * P + P], sub[:, n, :], start=True, stop=True)
                last.then_inc(scored, 1)

        @block.scalar
        def _(act):
            for t in range(TT):
                act.wait_ge(exp_in, t + 1)
                nc.scalar.activation(best, best, ACT.Exp).then_inc(exp_out, 1)

        @block.vector
        def _(dve):
            link = chain(dve, dve_chain)
            V = nc.vector
            dve.wait_ge(iota_done, 1)
            link(V.tensor_copy(iota, iota_i))
            V.tensor_tensor(xn, xn, spread(m.row("ffn_row"), 1, TT), ALU.mult)

            def top16(values, indices, table, n):
                for part in (slice(0, 8), slice(8, 16)):
                    for r in range(n):
                        last = V.max(values[:, r, part], table[:, r, :])
                    link(last)
                    for r in range(n):
                        last = V.max_index(indices[:, r, part], values[:, r, part], table[:, r, :])
                    if part.start == 0:
                        link(last)
                        for r in range(n):
                            last = V.match_replace(table[:, r, :], values[:, r, part], table[:, r, :], -3.0e38)
                    link(last)

            for t in range(TT):
                dve.wait_ge(scored, t + 1)
                last = V.tensor_copy(sc, m.PS[:, 4 * (t % 2):4 * (t % 2) + 4, :].rearrange("p b (n k) -> p (b n) k", n=4))
                last.then_inc(taken, 1)
                dve.wait_ge(taken, t + 1)
                top16(vals, ids, sc, 2 * PH)
                link(V.tensor_copy(ids_f, ids))
                pairs = vals.rearrange("p (h s) k -> p h s k", s=2)
                ipairs = ids_f.rearrange("p (h s) k -> p h s k", s=2)
                link(V.tensor_tensor(cand, spread(pairs[:, :, 0, :], 3, TOPK), spread(pairs[:, :, 1, :], 2, TOPK), ALU.add))
                top16(best, pos, flatc, PH)
                for s in range(2):
                    if s == 0:
                        link(V.tensor_scalar(half_u, pos, 4, None, ALU.logical_shift_right))
                    else:
                        link(V.tensor_scalar(half_u, pos, 15, None, ALU.bitwise_and))
                    link(V.tensor_copy(half_f, half_u))
                    link(V.tensor_tensor(cand.rearrange("p h i j -> p (h i) j"),
                                         spread(half_f.rearrange("p h k -> p (h k)"), 2, TOPK), spread(iota, 1, NE), ALU.is_equal))
                    link(V.tensor_tensor(cand, cand, spread(ipairs[:, :, s, :], 2, TOPK), ALU.mult))
                    link(V.tensor_reduce(e12[:, s, :], cand.rearrange("p h i j -> p (h i) j"), AX.X, ALU.add))
                link(V.scalar_tensor_tensor(e12[:, 0, :], e12[:, 0, :], float(NKEY), e12[:, 1, :], ALU.mult, ALU.add))
                V.tensor_copy(idx[:, t, :], e12[:, 0, :])
                link(V.tensor_copy(den, best[:, :, 0]))
                V.tensor_tensor(best, best, spread(den, 2, TOPK), ALU.subtract).then_inc(exp_in, 1)
                dve.wait_ge(exp_out, t + 1)
                link(V.tensor_reduce(den, best, AX.X, ALU.add))
                link(V.reciprocal(den, den))
                last = V.tensor_tensor(gate[:, t, :].rearrange("p (h k) -> p h k", h=PH), best, spread(den, 2, TOPK), ALU.mult)
                link(last)

    return idx, gate, dots


def gather(nc, m, name, table, idx, tokens, dots, acc):
    SLOTS = 8
    turns = TT * PH * TOPK // SLOTS
    A = Arena(m.R)
    rows = [A.take(D) for _ in range(2 * SLOTS)]
    junk = A.take(2, D)
    flat_idx = idx.rearrange("p t n -> p (t n)")
    flat_dots = dots.rearrange("p t n -> p (t n)")
    now = [A.take(SLOTS, dtype=U32) for _ in range(2)]
    zero, spare = A.take(2), A.take(2)
    with stage(nc, name, "zeroed copied used " + " ".join(f"row{s}" for s in range(2 * SLOTS))) as (zeroed, copied, used, *row_in), \
            nc.Block() as block:
        @block.gpsimd
        def _(pool):
            def turn(i, parity, first):
                if not first:
                    pool.wait_ge(used, i * SLOTS - SLOTS)
                    pool.wait_ge(copied, 1)
                nc.gpsimd.tensor_copy(now[parity], flat_idx[:, bass.ds(i * SLOTS, SLOTS)]).then_inc(copied, 1)
                pool.wait_ge(copied, i * 2 + 1)
                nc.gpsimd.tensor_tensor(spare, zero, zero, ALU.add).then_inc(copied, 1)
                for s in range(SLOTS):
                    slot = parity * SLOTS + s
                    nc.gpsimd.indirect_dma_start(out=rows[slot], out_offset=None, in_=table,
                                                 in_offset=bass.IndirectOffsetOnAxis(ap=now[parity][:, s:s + 1], axis=0))\
                        .then_inc(row_in[slot], 16)

            nc.gpsimd.memset(zero, 0.0).then_inc(zeroed, 1)
            pool.wait_ge(zeroed, 1)
            turn(0, 0, True)
            turn(1, 1, True)
            with pool.Fori(1, turns // 2) as i:
                turn(i * 2, 0, False)
                turn(i * 2 + 1, 1, False)

        @block.vector
        def _(dve):
            per = turns // TT // 2
            V = nc.vector

            def turn(i, parity, t):
                for s in range(SLOTS):
                    slot = parity * SLOTS + s
                    n = i * 2 * SLOTS + slot
                    dve.wait_ge(row_in[slot], (i + 1) * 16)
                    one = flat_dots[:, bass.ds(n, 1)]
                    tile = (tokens if acc is None else acc)[:, t, :]
                    if acc is None:
                        V.scalar_tensor_tensor(junk[:, s % 2], rows[slot], 1.0, tile, ALU.mult, ALU.mult, accum_out=one)\
                            .then_inc(used, 1)
                    else:
                        V.scalar_tensor_tensor(tile, rows[slot], one, tile, ALU.mult, ALU.add).then_inc(used, 1)
                    dve.wait_ge(used, n + 1)

            for t in range(TT):
                with dve.Fori(t * per, (t + 1) * per) as i:
                    for parity in range(2):
                        turn(i, parity, t)


def final_norm(nc, m):
    with region(nc, "final_ssq", TT) as ssq, stage(nc, "final", "squares mean root dve") as (squares, mean, root, dve_chain), nc.Block() as block:
        @block.scalar
        def _(act):
            for t in range(TT):
                nc.scalar.activation(m.y[:, t, :], m.x[:, t, :], ACT.Square, accum_out=ssq[:, t:t + 1]).then_inc(squares, 1)
            act.wait_ge(mean, 1)
            nc.scalar.activation(ssq, ssq, ACT.Sqrt).then_inc(root, 1)

        @block.vector
        def _(dve):
            link = chain(dve, dve_chain)
            V = nc.vector
            dve.wait_ge(squares, TT)
            V.tensor_scalar(ssq, ssq, 1.0 / D, EPS, ALU.mult, ALU.add).then_inc(mean, 1)
            dve.wait_ge(root, 1)
            link(V.reciprocal(ssq, ssq))
            for t in range(TT):
                V.scalar_tensor_tensor(m.x[:, t, :], m.x[:, t, :], ssq[:, t:t + 1], m.row("final"), ALU.mult, ALU.mult)


def second_block(nc, m, w):
    load_layer(nc, m, w["cols_2"], w["rows_2"], NCOL2, NROW2)
    m.table = (COLS2, ROWS2)
    hybrid_mixer(nc, m, w)
    cross_attention(nc, m, w)
    peer(nc, m, w)
    final_norm(nc, m)


def build(nc, w, out):
    ctx = ExitStack()
    with ctx:
        def sb(name, n, parts=P):
            return ctx.enter_context(nc.sbuf_tensor(name, [parts, n], F32))[:, :]

        m = Memory()
        m.PS = ctx.enter_context(nc.psum_tensor("PS", [P, 8, 512], F32))[:, :, :]
        m.x = sb("x", TT * D).rearrange("p (t n) -> p t n", t=TT)
        m.H = sb("H", DK * SEQ)
        m.hT = m.H.rearrange("p (k n) -> p k n", k=DK)
        m.y = m.H.rearrange("p (t n) -> p t n", t=TT)
        m.cols = sb("cols", max(NCOL, NCOL2))
        m.rows = sb("rows", max(NROW, NROW2))
        m.ident, m.ones = sb("ident", P), sb("ones", P)
        m.upper, m.strict_upper, m.strict_lower = (sb(n, P) for n in ("upper", "strict_upper", "strict_lower"))
        m.upper8, m.lower8 = sb("upper8", P), sb("lower8", P)
        m.upper64, m.strict_upper64 = sb("upper64", P), sb("strict_upper64", P)
        m.same = {b: sb(f"same{b}", P) for b in (8, 16, 32, 64)}
        m.merge = {b: sb(f"merge{b}", P) for b in (8, 16, 32, 64)}
        m.window = sb("window", 4 * P).rearrange("p (n k) -> p n k", n=2)
        m.pick = sb("pick", 4 * P, parts=4).rearrange("p (h n) -> p h n", h=4)
        m.cos, m.sin = (sb(n, TT * 8).rearrange("p (t j) -> p t j", t=TT) for n in ("cos", "sin"))
        m.table = (COLS, ROWS)
        m.col = lambda name: m.cols[:, m.table[0][name][0]:m.table[0][name][1]]
        m.row = lambda name: m.rows[:, m.table[1][name][0]:m.table[1][name][1]]

        constants(nc, m)
        with stage(nc, "x_in", "loaded") as (loaded,), nc.Block() as block:
            @block.sync
            def _(sp):
                sp.dma_start(m.x, w["x"].rearrange("z (t p) n -> p (z t) n", p=P)).then_inc(loaded, 16)
                sp.wait_ge(loaded, 16)
        rope_tables(nc, m, w["positions"].rearrange("z (t p) -> p (z t)", p=P), Arena(m.H))
        with nc.Fori(0, DEPTH) as l:
            first_layer(nc, m, w, l)
        second_block(nc, m, w)
        with stage(nc, "x_out", "stored") as (stored,), nc.Block() as block:
            @block.sync
            def _(sp):
                sp.dma_start(out.rearrange("z (t p) n -> p (z t) n", p=P), m.x).then_inc(stored, 16)
                sp.wait_ge(stored, 16)



def columns(parts):
    import numpy as np
    out = []
    for a in parts:
        L = a.shape[0]
        out.append(a.reshape(L, -1, P).transpose(0, 2, 1) if a.shape[-1] >= P
                   else np.pad(a.reshape(L, -1, 1), ((0, 0), (0, P - a.shape[-1]), (0, 0))))
    return np.ascontiguousarray(np.concatenate(out, axis=2))


def taps_last(a):
    L, W, C = a.shape
    return a.reshape(L, W, C // P, P).transpose(0, 2, 1, 3).reshape(L, -1)


def layout(i):
    import numpy as np
    w = {n: i[n] for n in ("x", "positions", "w_ffn1_in", "w_ffn1_out", "w_in", "rwkv_w_up", "rwkv_a_up", "rwkv_g_up",
                           "w_out", "w_ffn2_in", "w_ffn2_out", "w_ple_gate", "w_ple_proj")}
    w["p"] = i["p"].reshape(DEPTH, SEQ, D_PLE)
    w["cols"] = columns([i["ln_ffn1_pre"], i["ln_mix_pre"], i["ln_ffn2_pre"], i["ln_ple_pre"], taps_last(i["mlstm_conv"]),
                         i["rwkv_mu"], i["rwkv_w0"], i["rwkv_a0"], i["rwkv_k_k"], i["rwkv_k_a"],
                         i["rwkv_r_k"].reshape(DEPTH, -1), i["mlstm_i_bias"], i["mlstm_f_bias"]])
    w["rows"] = np.concatenate([i["ln_ffn1_post"], i["ln_mix_post"], i["ln_ffn2_post"], i["ln_ple_post"], i["mlstm_norm"],
                                i["rwkv_ln_w"], i["rwkv_ln_b"], i["attn_sinks"]], axis=1)
    for n in ("w_in", "w_out", "xattn_wq", "xattn_wkv", "xattn_wo", "peer_wq", "peer_u", "peer_v"):
        w[n + "_2"] = i[n + "_2"][0]
    w["mem_2"] = i["mem_2"][0]
    w["lru_w_2"] = np.stack([i["lru_wa_2"][0], i["lru_wx_2"][0]]).reshape(2, 4, 2 * HD, HD)
    w["subkeys_2"] = np.ascontiguousarray(i["peer_subkeys_2"][0].reshape(16, NKEY, P).transpose(2, 0, 1))
    w["cols_2"] = columns([i["norm_mix_w_2"], i["norm_xattn_w_2"], i["norm_mem_w_2"], i["norm_ffn_w_2"],
                           taps_last(i["conv_qkv_w_2"]), taps_last(i["lru_conv_w_2"]), i["lru_conv_b_2"], i["lru_ba_2"],
                           i["lru_bx_2"], i["lru_lambda_2"]])[0]
    w["rows_2"] = np.concatenate([i["gdn_a_log_2"], i["gdn_dt_bias_2"], i["gdn_norm_w_2"], i["norm_ffn_w_2"], i["norm_final_w_2"].reshape(1, -1)],
                                 axis=1)
    return w


def kernel(**inputs):
    import numpy as np
    import concourse.bacc as bacc
    from concourse.bass_utils import run_bass_kernel_spmd

    nc = bacc.Bacc("TRN2", target_bir_lowering=False, num_devices=1)
    arrays, w = {}, {}
    for name, a in layout({n: np.asarray(a) for n, a in inputs.items()}).items():
        a = np.ascontiguousarray(a)
        arrays[f"in_{name}"] = a
        w[name] = nc.dram_tensor(f"in_{name}", a.shape, mybir.dt.from_np(a.dtype), kind="ExternalInput").ap()
    out = nc.dram_tensor("out_x", (1, SEQ, D), F32, kind="ExternalOutput").ap()
    build(nc, w, out)
    got = run_bass_kernel_spmd(nc, [arrays], core_ids=[0])
    return got.results[0]["out_x"]
```

```python
import math
from contextlib import ExitStack, contextmanager, nullcontext

import concourse.bass as bass
from concourse import mybir

F32 = mybir.dt.float32
F32R = mybir.dt.float32r
I32 = mybir.dt.int32
U32 = mybir.dt.uint32
ACT = mybir.ActivationFunctionType
ALU = mybir.AluOpType
AX = mybir.AxisListType

P = 128
D = 1024
DK = D // P
SEQ = 512
TT = SEQ // P
DEPTH = 2
EPS = 1e-6
NEG = -1e30

HD = 64
D_FF = 2816
FK = D_FF // P
D_PLE = 256
QH, KVH = 8, 2
ATTN_COLS = QH * HD + 2 * KVH * HD
MH, RH = 4, 4
ML_V = ATTN_COLS + 2 * MH * HD
ML_O = ML_V + MH * HD
ML_I = ML_O + MH * HD
ML_F = ML_I + MH
RW = ML_F + MH
D_IN = RW + 3 * RH * HD + 64 + 64 + 128
TOK_V = ATTN_COLS
TOK_O = TOK_V + MH * HD
TOK_I = TOK_O + MH * HD
TOK_F = TOK_I + MH
TOK = TOK_F + MH
GATE_CAP = 15.0

COLS = {}
ROWS = {}


def lay(table, names):
    at = 0
    for name, width in names:
        table[name] = (at, at + width)
        at += width
    return at


NCOL = lay(COLS, [("ffn1_pre", 8), ("mix_pre", 8), ("ffn2_pre", 8), ("ple_pre", 8), ("conv", 16), ("mu", 8), ("w0", 2),
                  ("a0", 2), ("k_k", 2), ("k_a", 2), ("r_k", 2)])
NROW = lay(ROWS, [("ffn1_post", D), ("mix_post", D), ("ffn2_post", D), ("ple_post", D), ("mlstm_norm", 256),
                  ("ln_w", 256), ("ln_b", 256), ("sinks", 8), ("gate_bias", 2 * MH)])

GH = 4
GQK = GH * P
G_Z = 3 * GQK
G_A = G_Z + GQK
G_B = G_A + GH
G_XR = G_B + GH
G_GATE = G_XR + 512
IN2 = G_GATE + 512
MEM = 256
XH = 4
PH = 8
NKEY = 128
TOPK = 16
COLS2 = {}
ROWS2 = {}
NCOL2 = lay(COLS2, [("mix", 8), ("xattn", 8), ("mem", 8), ("ffn", 8), ("conv_qkv", 48), ("conv_lru", 16), ("conv_b", 4),
                    ("ba", 4), ("bx", 4), ("lam", 4)])
NROW2 = lay(ROWS2, [("a_log", GH), ("dt_bias", GH), ("gdn_norm", P), ("ffn_row", D), ("final", D)])


def chain(engine, sem):
    done = [0]

    def link(instruction):
        done[0] += 1
        instruction.then_inc(sem, 1)
        engine.wait_ge(sem, done[0])

    return link


@contextmanager
def stage(nc, name, signals):
    with ExitStack() as s:
        sems = [s.enter_context(nc.semaphore(f"{name}_{x}")) for x in signals.split()]
        yield sems
        numbers = sorted(x.num for x in sems)
        first = numbers[0]
        for n, following in zip(numbers, numbers[1:] + [None]):
            if following != n + 1:
                nc.multi_engine_barrier(list(nc.engines), range(first, n + 1))
                first = following


class Arena:

    def __init__(self, region):
        self.region, self.at = region, 0

    def take(self, *shape, parts=P, dtype=F32):
        n = math.prod(shape)
        n += n % 2
        assert self.at + n <= self.region.shape[1], (self.at, n, self.region.shape)
        flat = self.region[0:parts, self.at:self.at + math.prod(shape)]
        self.at += n
        if dtype != F32:
            flat = flat.bitcast(dtype)
        if len(shape) == 1:
            return flat
        names = "abcde"[:len(shape)]
        return flat.rearrange(f"p ({' '.join(names)}) -> p {' '.join(names)}", **dict(zip(names, shape)))


def spread(ap, axis, n):
    v = ap.unsqueeze(axis)
    shape = list(v.shape)
    shape[axis] = n
    return v.broadcast_to(shape)


class Memory:
    pass



def constants(nc, m, x):
    def block_view(ap, b):
        return ap.rearrange("p (n b) -> p n b", b=b)

    with stage(nc, "const", "loaded pool dve") as (loaded, pool_chain, dve_chain), nc.Block() as block:
        @block.sync
        def _(sp):
            load_ahead(sp, [(m.x, x.rearrange("z (t p) n -> p (z t) n", p=P))], loaded)

        @block.gpsimd
        def _(pool):
            link = chain(pool, pool_chain)
            for ap in (m.ident, m.upper, m.strict_upper, m.strict_lower, *m.same.values(), m.ones):
                nc.gpsimd.memset(ap, 1.0)
            link(nc.gpsimd.memset(m.window, 0.0))

            def keep(ap, pattern, base, mult, fill=0.0, op=ALU.is_ge):
                link(nc.gpsimd.affine_select(out=ap, in_=ap, compare_op=op, fill=fill, base=base,
                                             pattern=pattern, channel_multiplier=mult))

            keep(m.ident, [[-1, P]], 0, 1, op=ALU.is_equal)
            keep(m.upper, [[1, P]], 0, -1)
            keep(m.strict_upper, [[1, P]], -1, -1)
            keep(m.strict_lower, [[-1, P]], -1, 1)
            for b, ap in m.same.items():
                keep(block_view(ap, b), [[-b, P // b], [0, b]], 0, 1)
                keep(block_view(ap, b), [[b, P // b], [0, b]], b - 1, -1)
            for n in range(2):
                keep(m.window[:, n, :], [[-1, 2 * P]], P, 1, fill=NEG)
                keep(m.window[:, n, :], [[1, 2 * P]], -1, -1, fill=NEG)
            keep(m.window[:, 0, :], [[1, 2 * P]], -P, 0, fill=NEG)
            link(nc.gpsimd.memset(m.pick, 1.0))
            keep(m.pick, [[-1, 4], [0, P]], 0, 1, op=ALU.is_equal)

        @block.vector
        def _(dve):
            dve.wait_ge(pool_chain, 6 + 2 * len(m.same) + 5 + 1)
            link = chain(dve, dve_chain)
            V = nc.vector
            for b, ap in m.merge.items():
                if 2 * b < P:
                    link(V.tensor_tensor(ap, m.same[2 * b], m.same[b], ALU.subtract))
                else:
                    link(V.tensor_scalar(ap, m.same[b], -1.0, 1.0, ALU.mult, ALU.add))
                link(V.tensor_tensor(ap, ap, m.strict_upper, ALU.mult))
            V.tensor_tensor(m.upper8, m.same[8], m.strict_upper, ALU.mult)
            V.tensor_tensor(m.lower8, m.same[8], m.strict_lower, ALU.mult)
            V.tensor_tensor(m.strict_upper64, m.same[64], m.strict_upper, ALU.mult)
            link(V.tensor_tensor(m.upper64, m.same[64], m.upper, ALU.mult))


def rope_tables(nc, m, positions, A):
    turn = [6.28125, 0.0019350051879882812, 3.019915981956753e-07]
    magic = 1.5 * 2.0 ** 23
    pos_i = A.take(TT, dtype=I32)
    pos, ang, k, mag = A.take(TT), A.take(TT, 8), A.take(TT, 8), A.take(TT, 8)
    with stage(nc, "rope", "loaded reduced dve") as (loaded, reduced, dve_chain), nc.Block() as block:
        @block.sync
        def _(sp):
            with nc.allow_non_contiguous_dma(reason="512 positions"):
                sp.dma_start(pos_i, positions).then_inc(loaded, 16)

        @block.vector
        def _(dve):
            link = chain(dve, dve_chain)
            V = nc.vector
            dve.wait_ge(loaded, 16)
            link(V.tensor_copy(pos, pos_i))
            for j in range(8):
                last = V.tensor_scalar(ang[:, :, j], pos, float(bass.np.float32(500000.0 ** (-j / 8))), None, ALU.mult)
            link(last)
            link(V.tensor_scalar(k, ang, 1.0 / (2 * math.pi), magic, ALU.mult, ALU.add))
            link(V.tensor_scalar(k, k, magic, None, ALU.subtract))
            for part in turn:
                link(V.scalar_tensor_tensor(ang, k, -part, ang, ALU.mult, ALU.add))
            link(V.tensor_scalar(ang, ang, 3.1415925, -3.1415925, ALU.min, ALU.max))
            link(V.scalar_tensor_tensor(mag, ang, -1.0, ang, ALU.mult, ALU.max))
            V.tensor_scalar(mag, mag, -1.0, math.pi / 2, ALU.mult, ALU.add).then_inc(reduced, 1)

        @block.scalar
        def _(act):
            act.wait_ge(reduced, 1)
            nc.scalar.activation(m.sin, ang, ACT.Sin)
            nc.scalar.activation(m.cos, mag, ACT.Sin)



def load_columns(nc, m, cols, ncol):
    with stage(nc, "vectors", "loaded") as (loaded,), nc.Block() as block:
        @block.sync
        def _(sp):
            sp.dma_start(m.cols[:, 0:ncol], cols).then_inc(loaded, 16)
            sp.wait_ge(loaded, 16)


@contextmanager
def region(nc, name, *shape, dtype=F32):
    USES[name] = USES.get(name, 0) + 1
    with nc.sbuf_tensor(f"{name}_{USES[name]}", [P, math.prod(shape)], dtype) as t:
        if len(shape) == 1:
            yield t[:, :]
        else:
            names = "abcde"[:len(shape)]
            yield t[:, :].rearrange(f"p ({' '.join(names)}) -> p {' '.join(names)}", **dict(zip(names, shape)))


USES = {}


@contextmanager
def split_acts(nc, name, K, n):
    with region(nc, name + "_high", K, n, dtype=F32R) as high, region(nc, name + "_low", K, n, dtype=F32R) as low:
        yield high, low


@contextmanager
def weight_ring(nc, K=2, wide=512, raw=3, split=2):
    with ExitStack() as s:
        yield ([s.enter_context(region(nc, "w_raw", K, wide)) for _ in range(raw)],
               [s.enter_context(split_acts(nc, "w", K, wide)) for _ in range(split)])


def norm_transpose(nc, m, name, src, T, gain, dst, A, ahead=()):
    ssq, rstd = A.take(T), A.take(T)
    xn = A.take(T, D)
    high, low = dst
    with stage(nc, name, "loaded squares mean root scaled turned rounded dve") as \
            (loaded, squares, mean, root, scaled, turned, rounded, dve_chain), nc.Block() as block:
        @block.sync
        def _(sp):
            load_ahead(sp, ahead, loaded)

        @block.scalar
        def _(act):
            def take_root(t):
                act.wait_ge(mean, t + 1)
                nc.scalar.activation(rstd[:, t:t + 1], ssq[:, t:t + 1], ACT.Sqrt).then_inc(root, 1)

            for t in range(T):
                if t % 2 == 0:
                    nc.scalar.activation(m.y[:, t, :], src[:, t, :], ACT.Square, accum_out=ssq[:, t:t + 1]).then_inc(squares, 1)
                else:
                    take_root(t - 1)
                    take_root(t)
            for k in range(DK):
                act.wait_ge(turned, k + 1)
                nc.scalar.activation(high[:, k, :], m.PS[:, k, 0:P * T], ACT.Copy, scale=gain[:, k:k + 1]).then_inc(rounded, 1)

        @block.vector
        def _(dve):
            link = chain(dve, dve_chain)
            V = nc.vector

            def take_mean(t):
                V.tensor_scalar(ssq[:, t:t + 1], ssq[:, t:t + 1], 1.0 / D, EPS, ALU.mult, ALU.add).then_inc(mean, 1)

            def scale(t):
                dve.wait_ge(root, t + 1)
                link(V.reciprocal(rstd[:, t:t + 1], rstd[:, t:t + 1]))
                V.tensor_scalar(xn[:, t, :], src[:, t, :], rstd[:, t:t + 1], None, ALU.mult).then_inc(scaled, 1)

            for t in range(0, T, 2):
                link(V.scalar_tensor_tensor(m.y[:, t + 1, :], src[:, t + 1, :], 1.0, src[:, t + 1, :], ALU.mult, ALU.mult,
                                            accum_out=ssq[:, t + 1:t + 2]))
                dve.wait_ge(squares, t // 2 + 1)
                take_mean(t)
                take_mean(t + 1)
                if t:
                    scale(t - 2)
                    scale(t - 1)
            scale(T - 2)
            scale(T - 1)
            for k in range(DK):
                dve.wait_ge(rounded, k + 1)
                V.scalar_tensor_tensor(low[:, k, :], m.PS[:, k, 0:P * T], gain[:, k:k + 1], high[:, k, :].bitcast(F32),
                                       ALU.mult, ALU.subtract)

        @block.tensor
        def _(pe):
            for k in range(DK):
                for t in range(T):
                    if k == 0:
                        pe.wait_ge(scaled, t + 1)
                    last = nc.tensor.transpose(m.PS[:, k, t * P:t * P + P], xn[:, t, k * P:k * P + P], m.ident)
                last.then_inc(turned, 1)


def feature_chunks(weight, tiles, target):
    return [(weight[:, c * P:(c + 4) * P], True, lambda t, c=c: target(c + t)) for c in range(0, tiles, 4)]


def token_chunks(weight, widths, out, at=0):
    chunks, first = [], 0
    for w in widths:
        chunks.append((weight[:, first:first + w], False, lambda t, first=first, w=w: out[:, t, at + first:at + first + w]))
        first += w
    return chunks


def step_weights(chunks, i):
    columns, g = chunks[i // (DK // 2)][0], i % (DK // 2)
    return columns[g * 2 * P:(g + 1) * 2 * P, :].rearrange("(k p) n -> p k n", p=P)


def project_slots(raw, chunks):
    return [(raw[i][:, :, 0:chunks[0][0].shape[1]], step_weights(chunks, i)) for i in range(3)]


def project(nc, m, name, acts, chunks, T=TT, ring=None, beside=None):
    G, RAW, SPLIT = 2, 3, 2
    NG = DK // G
    n_tok = T * P
    steps = [(c, g) for c in range(len(chunks)) for g in range(NG)]
    high, low = acts
    width = lambda c: chunks[c][0].shape[1]
    tiles = lambda c: width(c) // P if chunks[c][1] else T

    with (nullcontext(ring) if ring else weight_ring(nc, raw=RAW, split=SPLIT)) as (raw, parts), \
            stage(nc, name, "loaded0 loaded1 loaded2 rounded split used out_dve out_act beside") as \
            (loaded0, loaded1, loaded2, rounded, split, used, out_dve, out_act, beside_done), nc.Block() as block:
        loaded = (loaded0, loaded1, loaded2)

        def bank(c, t):
            return m.PS[:, (c % 2) * 4 + t, 0:n_tok if chunks[c][1] else width(c)]

        @block.sync
        def _(sp):
            for i, (c, g) in enumerate(steps):
                if i < RAW and ring:
                    continue
                if i >= RAW:
                    sp.wait_ge(split, i - RAW + 1)
                sp.dma_start(raw[i % RAW][:, :, 0:width(c)], step_weights(chunks, i)).then_inc(loaded[i % RAW], 16)

        @block.tensor
        def _(pe):
            for i, (c, g) in enumerate(steps):
                w = width(c)
                w_high, w_low = parts[i % SPLIT]
                pe.wait_ge(split, i + 1)
                if g == 0 and c >= 2:
                    pe.wait_ge(out_dve, c - 1)
                    pe.wait_ge(out_act, c - 1)
                for t in range(tiles(c)):
                    part = slice(t * P, t * P + P)
                    for kk in range(G):
                        k = g * G + kk
                        if chunks[c][1]:
                            still, still_low = w_high[:, kk, part], w_low[:, kk, part]
                            move, move_low = high[:, k, :], low[:, k, :]
                        else:
                            still, still_low = high[:, k, part], low[:, k, part]
                            move, move_low = w_high[:, kk, 0:w], w_low[:, kk, 0:w]
                        nc.tensor.matmul(bank(c, t), still, move, start=(k == 0), stop=False)
                        nc.tensor.matmul(bank(c, t), still, move_low, start=False, stop=False)
                        last = nc.tensor.matmul(bank(c, t), still_low, move, start=False, stop=(k == DK - 1))
                last.then_inc(used, 1)

        @block.scalar
        def _(act):
            def copy_out(c):
                act.wait_ge(used, (c + 1) * NG)
                for t in range(1, tiles(c), 2):
                    last = nc.scalar.activation(chunks[c][2](t), bank(c, t), ACT.Copy)
                last.then_inc(out_act, 1)

            for i, (c, g) in enumerate(steps):
                turn = i // RAW + (0 if ring else 1)
                if turn:
                    act.wait_ge(loaded[i % RAW], 16 * turn)
                if i >= SPLIT:
                    act.wait_ge(used, i - SPLIT + 1)
                w = width(c)
                nc.scalar.activation(parts[i % SPLIT][0][:, :, 0:w], raw[i % RAW][:, :, 0:w], ACT.Copy).then_inc(rounded, 1)
                if g == 1 and c >= 1:
                    copy_out(c - 1)
            copy_out(len(chunks) - 1)

        @block.vector
        def _(dve):
            def copy_out(c):
                dve.wait_ge(used, (c + 1) * NG)
                for t in range(0, tiles(c), 2):
                    last = nc.vector.tensor_copy(chunks[c][2](t), bank(c, t))
                last.then_inc(out_dve, 1)

            def stored(c):
                dve.wait_ge(out_dve, c + 1)
                dve.wait_ge(out_act, c + 1)

            link = chain(dve, beside_done)
            for i, (c, g) in enumerate(steps):
                dve.wait_ge(rounded, i + 1)
                w = width(c)
                w_high, w_low = parts[i % SPLIT]
                nc.vector.tensor_tensor(w_low[:, :, 0:w], raw[i % RAW][:, :, 0:w], w_high[:, :, 0:w].bitcast(F32),
                                        ALU.subtract).then_inc(split, 1)
                if g == 1 and c >= 1:
                    copy_out(c - 1)
                if beside:
                    beside(dve, link, i, stored)
            copy_out(len(chunks) - 1)


def model_loads(raw, weight):
    return [(raw[:, s], weight[s * P:s * P + P, :]) for s in range(2)]


def load_ahead(sp, loads, loaded):
    for to, weights in loads:
        sp.dma_start(to, weights).then_inc(loaded, 16)
    if loads:
        sp.wait_ge(loaded, 16 * len(loads))


def project_model(nc, m, name, acts, K, weight, raw, gain=None, factor=1.0, gate=None):
    with weight_ring(nc, K=1, wide=D, raw=0) as (_, parts), \
            region(nc, "a_high0", SEQ, dtype=F32R) as ah0, region(nc, "a_high1", SEQ, dtype=F32R) as ah1, \
            region(nc, "a_low0", SEQ, dtype=F32R) as al0, region(nc, "a_low1", SEQ, dtype=F32R) as al1, \
            region(nc, "norm", 2 * TT) as norm, \
            stage(nc, name, "loaded_even loaded_odd rounded split used finished opened gated squares mean root dve scaled added") as \
            (loaded_even, loaded_odd, rounded, split, used, finished, opened, gated, squares, mean, root, dve_chain, scaled, added), \
            nc.Block() as block:
        ssq, rstd = norm[:, 0:TT], norm[:, TT:2 * TT]
        product = [m.PS[:, 2 * t:2 * t + 2, :].rearrange("p b n -> p (b n)") for t in range(TT)]
        loaded, a_high, a_low = (loaded_even, loaded_odd), (ah0, ah1), (al0, al1)
        pairs = K // 2
        flat = lambda ap: ap.rearrange("p a n -> p (a n)")
        tile = lambda j: flat(acts[:, bass.ds(j, 1), :])

        @block.sync
        def _(sp):
            def load(j, s):
                sp.dma_start(raw[:, s], weight[bass.ds(j * P, P), :]).then_inc(loaded[s], 16)

            if pairs > 1:
                with sp.Fori(0, pairs - 1) as i:
                    for s in range(2):
                        sp.wait_ge(split, i * 2 + s + 1)
                        load(i * 2 + s + 2, s)

        def run(engine, pair):
            pair(0, True, pairs == 1)
            if pairs > 2:
                with engine.Fori(1, pairs - 1) as i:
                    pair(i, False, False)
            if pairs > 1:
                pair(pairs - 1, False, True)

        @block.tensor
        def _(pe):
            def products(s, first, final):
                w_high, w_low = (flat(x) for x in parts[s])
                for t in range(TT):
                    part = slice(t * P, t * P + P)
                    for half in range(2):
                        to, cols = m.PS[:, 2 * t + half, :], slice(half * 512, half * 512 + 512)
                        nc.tensor.matmul(to, a_high[s][:, part], w_high[:, cols], start=first, stop=False)
                        nc.tensor.matmul(to, a_high[s][:, part], w_low[:, cols], start=False, stop=False)
                        last = nc.tensor.matmul(to, a_low[s][:, part], w_high[:, cols], start=False, stop=final)
                    if final:
                        last.then_inc(finished, 1)
                if not final:
                    last.then_inc(used, 1)

            def pair(i, first, final):
                for s in range(2):
                    pe.wait_ge(split, i * 2 + s + 1)
                    products(s, first and s == 0, final and s == 1)

            run(pe, pair)

        @block.scalar
        def _(act):
            def pair(i, first, final):
                for s in range(2):
                    if not first:
                        act.wait_ge(loaded[s], i * 16)
                        act.wait_ge(used, i * 2 + s - 1)
                    nc.scalar.activation(flat(parts[s][0]), raw[:, s], ACT.Copy)
                    nc.scalar.activation(a_high[s], tile(i * 2 + s), ACT.Copy).then_inc(rounded, 1)

            run(act, pair)
            if gate is not None:
                nc.scalar.activation(gate, gate, ACT.Sigmoid).then_inc(opened, 1)
            if gain is None:
                return

            def take_root(t):
                act.wait_ge(mean, t + 1)
                nc.scalar.activation(rstd[:, t:t + 1], ssq[:, t:t + 1], ACT.Sqrt).then_inc(root, 1)

            for t in range(TT):
                if gate is None:
                    act.wait_ge(finished, t + 1)
                    src, junk = product[t], m.y[:, t, :]
                else:
                    act.wait_ge(gated, t + 1)
                    src, junk = m.y[:, t, :], product[t]
                nc.scalar.activation(junk, src, ACT.Square, accum_out=ssq[:, t:t + 1]).then_inc(squares, 1)
                if t:
                    take_root(t - 1)
            take_root(TT - 1)

        @block.vector
        def _(dve):
            def pair(i, first, final):
                for s in range(2):
                    dve.wait_ge(rounded, i * 2 + s + 1)
                    w_high, w_low = (flat(x) for x in parts[s])
                    nc.vector.tensor_tensor(w_low, raw[:, s], w_high.bitcast(F32), ALU.subtract)
                    nc.vector.tensor_tensor(a_low[s], tile(i * 2 + s), a_high[s].bitcast(F32), ALU.subtract).then_inc(split, 1)

            run(dve, pair)
            V = nc.vector
            if gain is None:
                for t in range(TT):
                    dve.wait_ge(finished, t + 1)
                    V.tensor_tensor(m.x[:, t, :], m.x[:, t, :], product[t], ALU.add)
                return
            link = chain(dve, dve_chain)

            def open_gate(t):
                if gate is not None:
                    dve.wait_ge(opened, 1)
                    dve.wait_ge(finished, t + 1)
                    V.tensor_tensor(m.y[:, t, :], product[t], gate[:, t, :], ALU.mult).then_inc(gated, 1)

            def scale(t):
                dve.wait_ge(root, t + 1)
                link(V.reciprocal(rstd[:, t:t + 1], rstd[:, t:t + 1]))
                src = product[t] if gate is None else m.y[:, t, :]
                V.scalar_tensor_tensor(m.y[:, t, :], src, rstd[:, t:t + 1], gain, ALU.mult, ALU.mult).then_inc(scaled, 1)
                if t % 2 == 0:
                    dve.wait_ge(scaled, t + 1)
                    V.tensor_tensor(m.x[:, t, :], m.x[:, t, :], m.y[:, t, :], ALU.add)

            open_gate(0)
            for t in range(TT):
                if t + 1 < TT:
                    open_gate(t + 1)
                dve.wait_ge(squares, t + 1)
                V.tensor_scalar(ssq[:, t:t + 1], ssq[:, t:t + 1], 1.0 / (D * factor ** 2), EPS / factor ** 2, ALU.mult, ALU.add)\
                    .then_inc(mean, 1)
                if t:
                    scale(t - 1)
            scale(TT - 1)

        @block.gpsimd
        def _(pool):
            if gain is not None:
                for t in range(1, TT, 2):
                    pool.wait_ge(scaled, t + 1)
                    nc.gpsimd.tensor_tensor(m.x[:, t, :], m.x[:, t, :], m.y[:, t, :], ALU.add).then_inc(added, 1)


def convolve(V, link, n, taps, src, dst, bias=None):
    tap = lambda back: taps[:, n, 3 - back:4 - back]
    if bias is None:
        link(V.tensor_scalar(dst, src, tap(0), None, ALU.mult))
    else:
        link(V.tensor_scalar(dst, src, tap(0), bias[:, n:n + 1], ALU.mult, ALU.add))
    for back in range(1, 4):
        link(V.scalar_tensor_tensor(dst[:, back:], src[:, 0:SEQ - back], tap(back), dst[:, back:], ALU.mult, ALU.add))


def turn_tiles(nc, m, name, src_of, K, dst, ahead):
    with stage(nc, name, "loaded turned") as (loaded, turned), nc.Block() as block:
        @block.sync
        def _(sp):
            load_ahead(sp, ahead, loaded)

        @block.tensor
        def _(pe):
            for k in range(K):
                for t in range(TT):
                    last = nc.tensor.transpose(m.PS[:, k, t * P:t * P + P], src_of(t, k), m.ident)
                last.then_inc(turned, 1)

        @block.vector
        def _(dve):
            for k in range(0, K, 2):
                dve.wait_ge(turned, k + 1)
                nc.vector.tensor_copy(dst[:, k, :], m.PS[:, k, :])

        @block.scalar
        def _(act):
            for k in range(1, K, 2):
                act.wait_ge(turned, k + 1)
                nc.scalar.activation(dst[:, k, :], m.PS[:, k, :], ACT.Copy)


def swiglu_loads(raw, weight, j, s):
    cols = weight.rearrange("(k p) (g n) -> p k g n", p=P, g=2)
    return [(raw[s].rearrange("p k (g c) -> p k g c", g=2)[:, :, g, :], cols[:, :, g, bass.ds(j * P, P)]) for g in range(2)]


def swiglu_up(nc, m, name, weight, h, acts, ring, ahead):
    raw, parts = ring
    high, low = h
    with region(nc, "silu0", SEQ) as silu0, region(nc, "silu1", SEQ) as silu1, \
            stage(nc, name, "loaded_next loaded_even loaded_odd rounded split product silu gated") as \
            (loaded_next, loaded_even, loaded_odd, rounded, split, product, silu, gated), nc.Block() as block:
        loaded, silus = (loaded_even, loaded_odd), (silu0, silu1)
        gate_up = lambda ap: ap.rearrange("p k (g c) -> p k g c", g=2)

        @block.sync
        def _(sp):
            with sp.Fori(0, FK // 2 - 1) as i:
                for s in range(2):
                    sp.wait_ge(split, i * 2 + s + 1)
                    for to, columns in swiglu_loads(raw, weight, i * 2 + s + 2, s):
                        sp.dma_start(to, columns).then_inc(loaded[s], 16)
            load_ahead(sp, ahead, loaded_next)

        @block.tensor
        def _(pe):
            def pair(i, first):
                for s in range(2):
                    pe.wait_ge(split, i * 2 + s + 1)
                    if not first:
                        pe.wait_ge(gated, i * 2 + s - 1)
                    w_high, w_low = (gate_up(x) for x in parts[s])
                    for g in range(2):
                        to = m.PS[:, 2 * s + g, :]
                        for k in range(DK):
                            nc.tensor.matmul(to, w_high[:, k, g, :], high[:, k, :], start=(k == 0), stop=False)
                            nc.tensor.matmul(to, w_high[:, k, g, :], low[:, k, :], start=False, stop=False)
                            last = nc.tensor.matmul(to, w_low[:, k, g, :], high[:, k, :], start=False, stop=(k == DK - 1))
                    last.then_inc(product, 1)

            pair(0, True)
            with pe.Fori(1, FK // 2) as i:
                pair(i, False)

        @block.scalar
        def _(act):
            def rounding(i, s, first):
                if not first:
                    act.wait_ge(loaded[s], i * 32)
                    act.wait_ge(product, i * 2 + s - 1)
                nc.scalar.activation(parts[s][0], raw[s], ACT.Copy).then_inc(rounded, 1)

            def silu_of(i, s, first):
                act.wait_ge(product, i * 2 + s + 1)
                if not first:
                    act.wait_ge(gated, i * 2 + s - 1)
                nc.scalar.activation(silus[s], m.PS[:, 2 * s, :], ACT.Silu).then_inc(silu, 1)

            rounding(0, 0, True)
            rounding(0, 1, True)
            silu_of(0, 0, True)
            rounding(1, 0, False)
            silu_of(0, 1, True)
            rounding(1, 1, False)
            with act.Fori(1, FK // 2 - 1) as i:
                silu_of(i, 0, False)
                rounding(i + 1, 0, False)
                silu_of(i, 1, False)
                rounding(i + 1, 1, False)
            silu_of(FK // 2 - 1, 0, False)
            silu_of(FK // 2 - 1, 1, False)

        @block.vector
        def _(dve):
            def rest(i, s):
                dve.wait_ge(rounded, i * 2 + s + 1)
                nc.vector.tensor_tensor(parts[s][1], raw[s], parts[s][0].bitcast(F32), ALU.subtract).then_inc(split, 1)

            def gating(i, s):
                dve.wait_ge(silu, i * 2 + s + 1)
                to = acts[:, bass.ds(i * 2 + s, 1), :].rearrange("p a n -> p (a n)")
                nc.vector.tensor_tensor(to, silus[s], m.PS[:, 2 * s + 1, :], ALU.mult).then_inc(gated, 1)

            rest(0, 0)
            rest(0, 1)
            with dve.Fori(0, FK // 2 - 1) as i:
                gating(i, 0)
                rest(i + 1, 0)
                gating(i, 1)
                rest(i + 1, 1)
            gating(FK // 2 - 1, 0)
            gating(FK // 2 - 1, 1)


def feed_forward(nc, m, name, w_in, w_out, pre, post, rows=()):
    with region(nc, "ffn_acts", FK, SEQ) as acts, region(nc, "m_raw", 2, D) as raw:
        with split_acts(nc, "h", DK, SEQ) as h, weight_ring(nc, K=DK, wide=2 * P, raw=2) as ring:
            norm_transpose(nc, m, name + "_pre", m.x, TT, pre, h, Arena(acts.rearrange("p j n -> p (j n)")),
                           swiglu_loads(ring[0], w_in, 0, 0) + swiglu_loads(ring[0], w_in, 1, 1) + list(rows))
            swiglu_up(nc, m, name + "_up", w_in, h, acts, ring, model_loads(raw, w_out))
        project_model(nc, m, name + "_down", acts, FK, w_out, raw, post, 0.5)



def rope(m, V, link, proj, t, tmp):
    heads = proj[:, t, 0:10 * HD].rearrange("p (h d) -> p h d", d=HD)
    x1, x2 = heads[:, :, 0:8], heads[:, :, 8:16]
    cos, sin = spread(m.cos[:, t, :], 1, 10), spread(m.sin[:, t, :], 1, 10)
    V.tensor_tensor(tmp[:, 0], x1, cos, ALU.mult)
    V.tensor_tensor(tmp[:, 1], x2, sin, ALU.mult)
    V.tensor_tensor(tmp[:, 2], x2, cos, ALU.mult)
    link(V.tensor_tensor(tmp[:, 3], x1, sin, ALU.mult))
    V.tensor_tensor(x1, tmp[:, 0], tmp[:, 1], ALU.subtract)
    link(V.tensor_tensor(x2, tmp[:, 2], tmp[:, 3], ALU.add))


def attention(nc, m, proj, y, A):
    qT = A.take(QH // 2, SEQ)
    kT = A.take(KVH, P + SEQ)
    vp = A.take(TT + 1, KVH * HD)
    kdup = A.take(TT, KVH, 2, HD)
    Ss = [A.take(QH, 2 * P) for _ in range(2)]
    pT = A.take(2 * QH, P)
    mxs, ess, dens = ([A.take(QH) for _ in range(2)] for _ in range(3))
    kq = ATTN_COLS - 2 * KVH * HD
    with stage(nc, "attn", "keys_dup turned_q turned_k dve scored shifted probs_act probs_turned turned_act turned_dve summed stored ready taken") as \
            (keys_dup, turned_q, turned_k, dve_chain, scored, shifted, probs, probs_turned, turned_act, turned_dve, summed,
             stored, ready, taken), nc.Block() as block:
        by_parity = lambda ap: ap.rearrange("p (j a) -> p a j", a=2)
        in_order = lambda ap: ap.rearrange("p (a j) -> p a j", a=2)
        sinks = by_parity(m.row("sinks"))
        place = lambda h: (h % 2) * (QH // 2) + h // 2

        @block.vector
        def _(dve):
            link = chain(dve, dve_chain)
            V = nc.vector
            for t in range(TT):
                for twice in range(2):
                    last = V.tensor_copy(kdup[:, t, :, twice, :],
                                         proj[:, t, kq:kq + KVH * HD].rearrange("p (h d) -> p h d", d=HD))
            last.then_inc(keys_dup, 1)
            V.memset(kT[:, :, 0:P], 0.0)
            V.memset(vp[:, 0, :], 0.0)
            V.tensor_copy(vp[:, 1:TT + 1, :], proj[:, :, kq + KVH * HD:ATTN_COLS])
            dve.wait_ge(turned_q, 1)
            V.tensor_scalar(qT, m.PS[:, 0:4, :], HD ** -0.5, None, ALU.mult)
            dve.wait_ge(turned_k, 1)
            V.tensor_copy(kT[:, :, P:P + SEQ], m.PS[:, 4:6, :]).then_inc(ready, 1)

            def shift(n):
                S, mx, es = Ss[n % 2], mxs[n % 2], ess[n % 2]
                dve.wait_ge(scored, n + 1)
                scores = m.PS[:, 0:4, :].rearrange("p b (h k) -> p (b h) k", h=2)
                V.tensor_tensor(S, scores, spread(m.window[:, min(n, 1), :], 1, QH), ALU.add).then_inc(taken, 1)
                dve.wait_ge(taken, n + 1)
                link(V.tensor_reduce(mx, S, AX.X, ALU.max))
                link(V.tensor_tensor(in_order(mx), in_order(mx), sinks, ALU.max))
                link(V.tensor_tensor(in_order(es), sinks, in_order(mx), ALU.subtract))
                V.tensor_scalar(mx, mx, -1.0, None, ALU.mult).then_inc(shifted, 1)

            shift(0)
            for n in range(TT):
                if n + 1 < TT:
                    if n:
                        dve.wait_ge(probs_turned, n)
                    shift(n + 1)
                es, den = ess[n % 2], dens[n % 2]
                dve.wait_ge(probs, n + 1)
                link(V.tensor_tensor(den, den, es, ALU.add))
                link(V.reciprocal(den, den))
                dve.wait_ge(probs_turned, n + 1)
                V.tensor_copy(pT[:, 0:QH, :], m.PS[:, 4:6, :].rearrange("p b (h k) -> p (b h) k", h=4)).then_inc(turned_dve, 1)
                dve.wait_ge(summed, n + 1)
                for a in range(2):
                    last = V.tensor_tensor(y[:, n, 0:QH * HD].rearrange("p (j a d) -> p a j d", a=2, d=HD)[:, a],
                                           m.PS[:, 4, :].rearrange("p (j a d) -> p a j d", a=2, d=HD)[:, a],
                                           spread(in_order(den)[:, a], 2, HD), ALU.mult)
                last.then_inc(stored, 1)
                dve.wait_ge(stored, n + 1)

        @block.scalar
        def _(act):
            for n in range(TT):
                act.wait_ge(shifted, n + 1)
                nc.scalar.activation(ess[n % 2], ess[n % 2], ACT.Exp)
                for i in range(QH):
                    S = Ss[n % 2][:, i, :]
                    last = nc.scalar.activation(S, S, ACT.Exp, bias=mxs[n % 2][:, i:i + 1], accum_out=dens[n % 2][:, i:i + 1])
                last.then_inc(probs, 1)
                act.wait_ge(probs_turned, n + 1)
                nc.scalar.activation(pT[:, QH:2 * QH, :], m.PS[:, 6:8, :].rearrange("p b (h k) -> p (b h) k", h=4),
                                     ACT.Copy).then_inc(turned_act, 1)

        @block.tensor
        def _(pe):
            for j in range(QH // 2):
                for t in range(TT):
                    last = nc.tensor.transpose(m.PS[:, j, t * P:t * P + P], proj[:, t, j * P:j * P + P], m.ident)
            last.then_inc(turned_q, 1)
            pe.wait_ge(keys_dup, 1)
            for j in range(KVH):
                for t in range(TT):
                    last = nc.tensor.transpose(m.PS[:, 4 + j, t * P:t * P + P],
                                               kdup[:, t, j].rearrange("p a d -> p (a d)"), m.ident)
            last.then_inc(turned_k, 1)
            pe.wait_ge(ready, 1)

            def score(n):
                if n:
                    pe.wait_ge(taken, n)
                for h in range(QH):
                    at = (h % 2) * HD
                    last = nc.tensor.matmul(m.PS[:, place(h) // 2, (place(h) % 2) * 2 * P:(place(h) % 2 + 1) * 2 * P],
                                            qT[at:at + HD, h // 2, n * P:n * P + P],
                                            kT[at:at + HD, h // (QH // KVH), n * P:n * P + 2 * P], start=True, stop=True)
                last.then_inc(scored, 1)

            score(0)
            for n in range(TT):
                if n + 1 < TT:
                    score(n + 1)
                pe.wait_ge(probs, n + 1)
                if n:
                    pe.wait_ge(stored, n)
                for h in range(QH):
                    for b in range(2):
                        i = 2 * h + b
                        last = nc.tensor.transpose(m.PS[:, 4 + i // 4, (i % 4) * P:(i % 4 + 1) * P],
                                                   Ss[n % 2][:, place(h), b * P:b * P + P], m.ident)
                last.then_inc(probs_turned, 1)
                pe.wait_ge(turned_dve, n + 1)
                pe.wait_ge(turned_act, n + 1)
                for h in range(QH):
                    kv = h // (QH // KVH)
                    for b in range(2):
                        last = nc.tensor.matmul(m.PS[:, 4, h * HD:h * HD + HD], pT[:, 2 * h + b, :],
                                                vp[:, n + b, kv * HD:kv * HD + HD], start=(b == 0), stop=(b == 1))
                last.then_inc(summed, 1)



def log1p_series(link, V, e, z, z2, out):
    link(V.tensor_scalar(z2, e, 2.0, None, ALU.add))
    link(V.reciprocal(z2, z2))
    link(V.tensor_tensor(z, e, z2, ALU.mult))
    link(V.tensor_tensor(z2, z, z, ALU.mult))
    link(V.tensor_scalar(out, z2, 1.0 / 17, None, ALU.mult))
    for n in (15, 13, 11, 9, 7, 5, 3):
        link(V.scalar_tensor_tensor(out, out, 1.0 / n, z2, ALU.add, ALU.mult))
    link(V.tensor_scalar(out, out, 1.0, 2.0, ALU.add, ALU.mult))
    link(V.tensor_tensor(out, out, z, ALU.mult))


def mlstm(nc, m, proj, qk, y, A):
    both = A.take(TT, 2 * MH)
    F = both[:, :, MH:2 * MH]
    E, Z, Z2, L = (A.take(TT, MH) for _ in range(4))
    lines = A.take(5, SEQ, parts=4)
    G, C, M, EM, ONE = (lines[:, j, :] for j in range(5))
    ccol, ecol = A.take(TT, MH), A.take(TT, MH)
    pairs = [(j, i) for j in range(TT) for i in range(j, TT)]
    start = [pairs.index((j, j)) for j in range(TT)]
    W = A.take(MH, len(pairs), P)
    va = A.take(TT, MH, HD + 1)
    num = A.take(TT, MH, HD)
    den, ms = A.take(TT, MH), A.take(TT, MH)
    og = A.take(TT, MH, HD)
    both_in = proj[:, :, TOK_I:TOK]
    iT, lT = m.PS[0:4, 4, :], m.PS[0:4, 5, :]

    with stage(nc, "mlstm1", "turned tanh_in tanh_out abs_in exp_out dve gates rows cols bcast dist weights") as \
            (turned, tanh_in, tanh_out, abs_in, exp_out, dve_chain, gates_done, rows_done, cols_done, bcast, dist, weights), \
            nc.Block() as block:
        @block.tensor
        def _(pe):
            pe.wait_ge(gates_done, 1)
            for t in range(TT):
                nc.tensor.transpose(m.PS[0:4, 4, t * P:t * P + P], both[:, t, 0:MH], m.ident)
            for t in range(TT):
                last = nc.tensor.transpose(m.PS[0:4, 5, t * P:t * P + P], both[:, t, MH:2 * MH], m.ident)
            last.then_inc(turned, 1)
            pe.wait_ge(rows_done, 1)
            for t in range(TT):
                nc.tensor.transpose(m.PS[:, 6, t * 4:t * 4 + 4], C[:, t * P:t * P + P], m.ident[0:4, 0:4])
            for t in range(TT):
                last = nc.tensor.transpose(m.PS[:, 7, t * 4:t * 4 + 4], EM[:, t * P:t * P + P], m.ident[0:4, 0:4])
            last.then_inc(cols_done, 1)
            for h in range(MH):
                last = nc.tensor.matmul(m.PS[:, h, :], m.pick[:, h, :], M, start=True, stop=True)
            last.then_inc(bcast, 1)

        @block.scalar
        def _(act):
            act.wait_ge(tanh_in, 1)
            nc.scalar.activation(both, both, ACT.Tanh, scale=1 / GATE_CAP).then_inc(tanh_out, 1)
            act.wait_ge(abs_in, 1)
            nc.scalar.activation(E, E, ACT.Exp, scale=-1.0).then_inc(exp_out, 1)
            nc.scalar.activation(qk, qk, ACT.Silu)
            nc.scalar.activation(og, proj[:, :, TOK_O:TOK_I].rearrange("p t (h d) -> p t h d", d=HD), ACT.Sigmoid)
            act.wait_ge(abs_in, 2)
            nc.scalar.activation(EM, EM, ACT.Exp, scale=-1.0).then_inc(rows_done, 1)
            for j in range(TT):
                act.wait_ge(dist, j + 1)
                part = W[:, :, start[j]:start[j] + TT - j, :]
                nc.scalar.activation(part, part, ACT.Exp, scale=-1.0).then_inc(weights, 1)

        @block.vector
        def _(dve):
            link = chain(dve, dve_chain)
            V = nc.vector
            V.tensor_tensor(both, both_in, spread(m.row("gate_bias"), 1, TT), ALU.add).then_inc(tanh_in, 1)
            V.memset(ONE, 1.0)
            V.memset(va[:, :, :, HD:HD + 1], 1.0)
            V.tensor_copy(va[:, :, :, 0:HD], proj[:, :, TOK_V:TOK_O].rearrange("p t (h d) -> p t h d", d=HD))
            dve.wait_ge(tanh_out, 1)
            link(V.tensor_scalar(both, both, GATE_CAP, None, ALU.mult))
            V.scalar_tensor_tensor(E, F, -1.0, F, ALU.mult, ALU.max).then_inc(abs_in, 1)
            dve.wait_ge(exp_out, 1)
            log1p_series(link, V, E, Z, Z2, L)
            V.scalar_tensor_tensor(F, F, 0.0, L, ALU.min, ALU.subtract).then_inc(gates_done, 1)
            dve.wait_ge(turned, 1)
            link(V.tensor_tensor_scan(G, ONE, lT, 0.0, ALU.mult, ALU.add))
            link(V.tensor_tensor(C, iT, G, ALU.subtract))
            link(V.tensor_tensor_scan(M, ONE, C, NEG, ALU.mult, ALU.max))
            V.tensor_tensor(EM, G, M, ALU.add).then_inc(abs_in, 1)
            dve.wait_ge(cols_done, 1)
            V.tensor_copy(ecol, m.PS[:, 7, 0:TT * MH].rearrange("p (t h) -> p t h", h=MH))
            link(V.tensor_copy(ccol, m.PS[:, 6, 0:TT * MH].rearrange("p (t h) -> p t h", h=MH)))
            dve.wait_ge(bcast, 1)
            for j in range(TT):
                for h in range(MH):
                    n = TT - j
                    last = V.tensor_scalar(W[:, h, start[j]:start[j] + n, :],
                                           m.PS[:, h, j * P:].rearrange("p (n k) -> p n k", k=P),
                                           ccol[:, j, h:h + 1], 0.0, ALU.subtract, ALU.max)
                last.then_inc(dist, 1)
            for j in range(TT):
                dve.wait_ge(weights, j + 1)
                V.tensor_tensor(W[:, :, start[j], :], W[:, :, start[j], :], spread(m.upper, 1, MH), ALU.mult)

    def scores(j, h):
        bank, at = ((h, 0), (4 + h, 0), (h % 2, h // 2 * 2 * P), (2 + h % 2, h // 2 * P))[j]
        return m.PS[:, bank, at:at + SEQ - j * P]

    sums = m.PS[:, 4:4 + TT, 0:MH * (HD + 1)].rearrange("p t (h d) -> p t h d", d=HD + 1)
    with stage(nc, "mlstm2", "scored weighted summed den_read squared squares root dve") as (scored, weighted, summed, den_read, squared, squares, root, dve_chain), \
            nc.Block() as block:
        @block.tensor
        def _(pe):
            for j in range(TT):
                if j == 2:
                    pe.wait_ge(weighted, 1)
                for h in range(MH):
                    at = (h % 2) * HD
                    last = nc.tensor.matmul(scores(j, h), qk[at:at + HD, 2 + h // 2, j * P:j * P + P],
                                            qk[at:at + HD, h // 2, j * P:SEQ], start=True, stop=True)
                last.then_inc(scored, 1)
            for i in range(TT):
                pe.wait_ge(weighted, max(i + 1, 2))
                for h in range(MH):
                    for j in range(i + 1):
                        last = nc.tensor.matmul(m.PS[:, 4 + i, h * (HD + 1):(h + 1) * (HD + 1)], W[:, h, start[j] + i - j, :],
                                                va[:, j, h, :], start=(j == 0), stop=(j == i))
            last.then_inc(summed, 1)

        @block.vector
        def _(dve):
            link = chain(dve, dve_chain)
            V = nc.vector
            for j in range(TT):
                dve.wait_ge(scored, j + 1)
                for h in range(MH):
                    part = W[:, h, start[j]:start[j] + TT - j, :].rearrange("p n k -> p (n k)")
                    last = V.scalar_tensor_tensor(part, scores(j, h), HD ** -0.5, part,
                                                  ALU.mult, ALU.mult)
                last.then_inc(weighted, 1)
            norm = m.row("mlstm_norm").rearrange("p (h d) -> p h d", d=HD)
            link(V.tensor_tensor(og, og, spread(norm, 1, TT), ALU.mult))
            dve.wait_ge(summed, 1)
            V.tensor_copy(den, sums[:, :, :, HD]).then_inc(den_read, 1)
            dve.wait_ge(den_read, 1)
            link(V.scalar_tensor_tensor(den, den, -1.0, den, ALU.mult, ALU.max))
            link(V.tensor_tensor(den, den, ecol, ALU.max))
            link(V.reciprocal(den, den))
            dve.wait_ge(squared, 1)
            link(V.tensor_reduce(ms, num, AX.X, ALU.add))
            link(V.tensor_tensor(ms, ms, den, ALU.mult))
            link(V.tensor_tensor(ms, ms, den, ALU.mult))
            V.tensor_scalar(ms, ms, 1.0 / HD, EPS, ALU.mult, ALU.add).then_inc(squares, 1)
            dve.wait_ge(root, 1)
            link(V.reciprocal(ms, ms))
            link(V.tensor_tensor(ms, ms, den, ALU.mult))
            for t in range(TT):
                last = V.tensor_tensor(num[:, t], sums[:, t, :, 0:HD], spread(ms[:, t], 2, HD), ALU.mult)
            link(last)
            V.tensor_tensor(y[:, :, QH * HD:(QH + MH) * HD].rearrange("p t (h d) -> p t h d", d=HD), num, og, ALU.mult)

        @block.scalar
        def _(act):
            act.wait_ge(den_read, 1)
            for t in range(TT):
                last = nc.scalar.activation(num[:, t], sums[:, t, :, 0:HD], ACT.Square)
            last.then_inc(squared, 1)
            act.wait_ge(squares, 1)
            nc.scalar.activation(ms, ms, ACT.Sqrt).then_inc(root, 1)



def invert(nc, m, name, AT, A0, levels, A):
    N = 4 * TT
    XT, X, A0T, A2, A2T = (A.take(N, P) for _ in range(5))
    IA, IAT = X, XT
    with stage(nc, name, "product0 product1 dve0 dve1 act0 act1 own") as (product0, product1, dve0, dve1, act0, act1, own), \
            nc.Block() as block:
        products, by_dve, by_act = (product0, product1), (dve0, dve1), (act0, act1)
        H = N // 2
        part = lambda ap, g: ap[:, g * H:(g + 1) * H, :]
        low, high = ([m.PS[:, 4 * g + s:4 * g + s + 2, :].rearrange("p b (h k) -> p (b h) k", h=4) for g in range(2)]
                     for s in (0, 2))
        mask = lambda ap: spread(ap, 1, H)
        C, T1 = A0, A0T
        last_level = len(levels) - 1

        @block.tensor
        def _(pe):
            def multiply(g, dve_at, act_at, lows, highs):
                pe.wait_ge(by_dve[g], dve_at)
                if act_at:
                    pe.wait_ge(by_act[g], act_at)
                for to, pair in ((low[g], lows), (high[g], highs)):
                    if pair:
                        left, right = (part(x, g) for x in pair)
                        for i in range(H):
                            last = nc.tensor.matmul(to[:, i, :], left[:, i, :], right[:, i, :], start=True, stop=True)
                last.then_inc(products[g], 1)

            for g in range(2):
                multiply(g, 1, 0, (A0T, A0), (A0, A0T))
            for g in range(2):
                multiply(g, 2, 1, (A2T, IA), (A2, IAT))
            for g in range(2):
                multiply(g, 3, 1, (A2T, A2), (A2, A2T))
            for g in range(2):
                multiply(g, 4, 2, (A0T, X), (A0, XT))
            for n in range(len(levels)):
                for g in range(2):
                    multiply(g, 6 + 2 * n, 0, (C, X), None)
                for g in range(2):
                    multiply(g, 6 + 2 * n, 3 + n, (XT, T1) if n < last_level else None, (T1, XT))

        @block.scalar
        def _(act):
            def copy(g, round_, to, of):
                act.wait_ge(products[g], round_)
                nc.scalar.activation(part(to, g), of[g], ACT.Copy).then_inc(by_act[g], 1)

            for g in range(2):
                copy(g, 1, A2T, high)
            for g in range(2):
                copy(g, 3, A0T, high)
            for n in range(len(levels)):
                for g in range(2):
                    copy(g, 5 + 2 * n, T1, low)

        @block.vector
        def _(dve):
            link = chain(dve, own)
            V = nc.vector

            def add_both(g, round_, low_too=True):
                dve.wait_ge(products[g], round_)
                if low_too:
                    V.tensor_tensor(part(X, g), low[g], part(X, g), ALU.add)
                V.tensor_tensor(part(XT, g), high[g], part(XT, g), ALU.add).then_inc(by_dve[g], 1)

            for g in range(2):
                link(V.tensor_tensor(part(A0T, g), part(AT, g), mask(m.upper8), ALU.mult))
                V.tensor_tensor(part(IAT, g), part(A0T, g), mask(m.ident), ALU.add)
                V.tensor_tensor(part(IA, g), part(A0, g), mask(m.ident), ALU.add).then_inc(by_dve[g], 1)
            for g in range(2):
                dve.wait_ge(products[g], 1)
                V.tensor_copy(part(A2, g), low[g]).then_inc(by_dve[g], 1)
            for g in range(2):
                add_both(g, 2)
            for g in range(2):
                dve.wait_ge(products[g], 3)
                V.tensor_copy(part(A0, g), low[g]).then_inc(by_dve[g], 1)
            for n, b in enumerate(levels):
                for g in range(2):
                    add_both(g, 4 + 2 * n)
                    V.tensor_tensor(part(C, g), part(AT, g), mask(m.merge[b]), ALU.mult).then_inc(by_dve[g], 1)
            for g in range(2):
                add_both(g, 4 + 2 * len(levels), False)
    return XT



def rwkv(nc, m, fm, y, A, w_up, a_up, g_up, yT, ahead):
    LC = 64
    NC = SEQ // LC
    N = 4 * TT
    place = lambda t, h: (h % 2) * 8 + t * 2 + h // 2
    g = A.take(TT, 256)
    bonus = A.take(TT, RH)
    vtok = A.take(TT, 256)
    rt, at_, bt, kt, bh, kh = (A.take(2, SEQ) for _ in range(6))
    pend = A.take(2, NC)
    stay = A.at
    r, k, v, lora, gx = fm[:, 0:2], fm[:, 2:4], fm[:, 4:6], fm[:, 6], fm[:, 7]
    upw, gw = A.take(256), A.take(256)
    cum, before = A.take(2, SEQ), A.take(2, SEQ)
    B = Arena(m.A)
    lw, a, kk, t1, t2, reset = (B.take(2, SEQ) for _ in range(6))

    with stage(nc, "rwkv1", "loaded lora_in lora_out gates gate_out squares root norm_sum dve expd exp_in bonus_out") as \
            (loaded, lora_in, lora_out, gates, gate_out, squares, root, norm_sum, dve_chain, expd, exp_in,
             bonus_out), nc.Block() as block:
        @block.sync
        def _(sp):
            sp.dma_start(upw[0:64], w_up).then_inc(loaded, 16)
            sp.dma_start(upw[64:128], a_up).then_inc(loaded, 16)
            sp.dma_start(gw, g_up).then_inc(loaded, 16)

        @block.tensor
        def _(pe):
            pe.wait_ge(loaded, 48)
            pe.wait_ge(lora_in, 1)
            for j in range(2):
                nc.tensor.matmul(m.PS[:, j, :], upw[0:64, j * P:j * P + P], lora[0:64], start=True, stop=True)
                last = nc.tensor.matmul(m.PS[:, 2 + j, :], upw[64:128, j * P:j * P + P], lora[64:128], start=True, stop=True)
            last.then_inc(lora_out, 1)
            for t in range(TT):
                last = nc.tensor.matmul(m.PS[:, 4 + t // 2, (t % 2) * 256:(t % 2 + 1) * 256], gx[:, t * P:t * P + P], gw,
                                        start=True, stop=True)
            last.then_inc(gate_out, 1)
            pe.wait_ge(squares, 1)
            for j in range(2):
                last = nc.tensor.matmul(m.PS[:, 6 + j, :], m.same[64], t1[:, j], start=True, stop=True)
            last.then_inc(norm_sum, 1)
            pe.wait_ge(squares, 2)
            for t in range(TT):
                for j in range(2):
                    last = nc.tensor.matmul(m.PS[:, 4, t * 4 + 2 * j:t * 4 + 2 * j + 2], t1[:, j, t * P:t * P + P],
                                            m.same[64][:, 0:P:64], start=True, stop=True)
            for t in range(TT):
                for j in range(2):
                    last = nc.tensor.transpose(m.PS[:, t // 2, (t % 2) * 256 + j * P:(t % 2) * 256 + j * P + P],
                                               v[:, j, t * P:t * P + P], m.ident)
            last.then_inc(bonus_out, 1)

        @block.scalar
        def _(act):
            nc.scalar.activation(lora[0:64], lora[0:64], ACT.Tanh)
            nc.scalar.activation(gx, gx, ACT.Sigmoid).then_inc(lora_in, 1)
            act.wait_ge(lora_out, 1)
            for j in range(2):
                nc.scalar.activation(lw[:, j], m.PS[:, j, :], ACT.Sigmoid, bias=m.col("w0")[:, j:j + 1])
                nc.scalar.activation(a[:, j], m.PS[:, 2 + j, :], ACT.Sigmoid, bias=m.col("a0")[:, j:j + 1])\
                    .then_inc(gates, 1)
            act.wait_ge(norm_sum, 2)
            nc.scalar.activation(t2, t2, ACT.Sqrt).then_inc(root, 1)
            for i in range(3):
                act.wait_ge(exp_in, i + 1)
                src, dst, sign = ((cum, rt, 1.0), (before, at_, 1.0), (cum, bt, -1.0))[i]
                nc.scalar.activation(dst, src, ACT.Exp, scale=sign).then_inc(expd, 1)
            act.wait_ge(exp_in, 4)
            nc.scalar.activation(bh, bh, ACT.Exp)
            nc.scalar.activation(pend, cum.rearrange("p a (c l) -> p a c l", l=LC)[:, :, :, LC - 1], ACT.Exp).then_inc(expd, 1)

        @block.vector
        def _(dve):
            link = chain(dve, dve_chain)
            V = nc.vector
            link(V.memset(reset, 1.0))
            V.memset(reset.rearrange("p a (c l) -> p a c l", l=LC)[:, :, :, 0:1], 0.0)
            for j in range(2):
                last = V.tensor_scalar(kk[:, j], k[:, j], m.col("k_k")[:, j:j + 1], None, ALU.mult)
            link(last)
            V.tensor_tensor(t1, kk, kk, ALU.mult).then_inc(squares, 1)
            dve.wait_ge(norm_sum, 1)
            V.tensor_scalar(t2, m.PS[:, 6:8, :], 1e-24, None, ALU.max).then_inc(norm_sum, 1)
            dve.wait_ge(gates, 2)
            link(V.tensor_scalar(lw, lw, -math.exp(-0.5), None, ALU.mult))
            for j in range(2):
                last = V.tensor_tensor_scan(cum[:, j], reset[:, j], lw[:, j], 0.0, ALU.mult, ALU.add)
            last.then_inc(exp_in, 1)
            dve.wait_ge(exp_in, 1)
            V.tensor_tensor(before, cum, lw, ALU.subtract).then_inc(exp_in, 2)
            in_chunks = cum.rearrange("p a (c l) -> p a c l", l=LC)
            V.tensor_tensor(bh.rearrange("p a (c l) -> p a c l", l=LC), spread(in_chunks[:, :, :, LC - 1], 3, LC), in_chunks,
                            ALU.subtract).then_inc(exp_in, 1)
            dve.wait_ge(root, 1)
            link(V.reciprocal(t2, t2))
            link(V.tensor_tensor(kk, kk, t2, ALU.mult))
            link(V.tensor_scalar(t2, a, 1.0, None, ALU.subtract))
            for j in range(2):
                last = V.tensor_scalar(t2[:, j], t2[:, j], m.col("k_a")[:, j:j + 1], 1.0, ALU.mult, ALU.add)
            link(last)
            link(V.tensor_tensor(k, k, t2, ALU.mult))
            dve.wait_ge(gate_out, 1)
            link(V.tensor_copy(g, m.PS[:, 4:6, :].rearrange("p b (t n) -> p (b t) n", t=2)))
            link(V.tensor_tensor(t1, r, k, ALU.mult))
            for j in range(2):
                last = V.tensor_scalar(t1[:, j], t1[:, j], m.col("r_k")[:, j:j + 1], None, ALU.mult)
            last.then_inc(squares, 1)
            dve.wait_ge(bonus_out, 1)
            V.tensor_copy(vtok, m.PS[:, 0:2, :].rearrange("p b (t n) -> p (b t) n", t=2))
            link(V.tensor_copy(bonus, m.PS[:, 4, 0:16].rearrange("p (t h) -> p t h", h=RH)))
            dve.wait_ge(expd, 4)
            link(V.tensor_tensor(a, a, kk, ALU.mult))
            V.tensor_tensor(rt, rt, r, ALU.mult)
            V.scalar_tensor_tensor(at_, at_, -1.0, kk, ALU.mult, ALU.mult)
            V.tensor_tensor(kt, bt, k, ALU.mult)
            V.tensor_tensor(kh, bh, k, ALU.mult)
            dve.wait_ge(dve_chain, 1)
            link(V.tensor_tensor(bt, bt, a, ALU.mult))
            V.tensor_tensor(bh, bh, a, ALU.mult)

    A.at = stay
    AbT, A0, AkT, RbT, RkT = (A.take(N, P) for _ in range(5))
    abk = A.take(TT, 3, 256)
    with stage(nc, "rwkv2", "turned scored dve act") as (turned, scored, dve_chain, act_chain), nc.Block() as block:
        @block.tensor
        def _(pe):
            for i in range(3):
                src = (at_, bh, kh)[i]
                for t in range(TT):
                    for j in range(2):
                        last = nc.tensor.transpose(m.PS[:, 2 * i + t // 2, (t % 2) * 256 + j * P:(t % 2) * 256 + j * P + P],
                                                   src[:, j, t * P:t * P + P], m.ident)
            last.then_inc(turned, 1)
            n = 0
            for left, right in ((bt, at_), (at_, bt), (kt, at_), (bt, rt), (kt, rt)):
                pe.wait_ge(dve_chain, n + 1)
                for t in range(TT):
                    for h in range(RH):
                        po, j = (h % 2) * HD, h // 2
                        last = nc.tensor.matmul(m.PS[:, 4 * (n % 2) + place(t, h) // 4, (place(t, h) % 4) * P:(place(t, h) % 4 + 1) * P], left[po:po + HD, j, t * P:t * P + P],
                                                right[po:po + HD, j, t * P:t * P + P], start=True, stop=True)
                last.then_inc(scored, 1)
                n += 1

        @block.vector
        def _(dve):
            V = nc.vector
            dve.wait_ge(turned, 1)
            for i in range(3):
                last = V.tensor_copy(abk[:, :, i, :], m.PS[:, 2 * i:2 * i + 2, :].rearrange("p b (t n) -> p (b t) n", t=2))
                if i > 0:
                    last.then_inc(dve_chain, 1)
            for n, (to, mask) in enumerate(((AbT, m.strict_upper64), (A0, m.lower8), (AkT, m.strict_upper64),
                                            (RbT, m.upper64), (RkT, m.upper64))):
                dve.wait_ge(scored, n + 1)
                half = m.PS[:, 4 * (n % 2):4 * (n % 2) + 4, :]
                V.tensor_tensor(to, half.rearrange("p b (h k) -> p (b h) k", h=4), spread(mask, 1, N), ALU.mult)\
                    .then_inc(dve_chain, 1)

    B = Arena(m.A)
    XT = invert(nc, m, "rwkv_inv", AbT, A0, (8, 16, 32), B)
    B.at = N * P

    zin = A0
    WU = AbT
    TTm, Hm = B.take(2, 2, NC // 2, HD), B.take(2, 2, NC // 2, HD)
    QT = B.take(2, SEQ)
    Nst = B.take(2, NC + 1, HD)
    y0 = B.take(TT, 256)
    with stage(nc, "rwkv3", "product within dve act decay") as (product, within, dve_chain, act_chain, decay), nc.Block() as block:
        flat = lambda ap: ap.rearrange("p b (h k) -> p (b h) k", h=4)
        diag = m.ident

        @block.tensor
        def _(pe):
            for t in range(TT):
                for h in range(RH):
                    last = nc.tensor.matmul(m.PS[:, place(t, h) // 8, (place(t, h) % 8) * HD:(place(t, h) % 8 + 1) * HD], AkT[:, place(t, h), :], vtok[:, t, h * HD:h * HD + HD],
                                            start=True, stop=True)
            last.then_inc(product, 1)
            pe.wait_ge(dve_chain, 1)
            for t in range(TT):
                for h in range(RH):
                    last = nc.tensor.matmul(m.PS[:, 4 + place(t, h) // 4, (place(t, h) % 4) * P:(place(t, h) % 4 + 1) * P], XT[:, place(t, h), :], zin[:, place(t, h), :],
                                            start=True, stop=True)
            last.then_inc(product, 1)
            pe.wait_ge(dve_chain, 2)
            pe.wait_ge(act_chain, 1)
            for c in range(NC):
                t, q = c // 2, (c % 2) * LC
                for h in range(RH):
                    po, j = (h % 2) * HD, h // 2
                    wu = WU[q:q + LC, place(t, h), :]
                    bt_, kt_ = abk[q:q + LC, t, 1, h * HD:h * HD + HD], abk[q:q + LC, t, 2, h * HD:h * HD + HD]
                    at = (4 * j + c // 2) * HD
                    nc.tensor.matmul(m.PS[po:po + HD, 2 + c % 2, at:at + HD], wu[:, 0:HD], bt_, start=True, stop=True)
                    nc.tensor.matmul(m.PS[po:po + HD, 4 + c % 2, at:at + HD], bt_, wu[:, HD:P], start=True, stop=False)
                    last = nc.tensor.matmul(m.PS[po:po + HD, 4 + c % 2, at:at + HD], kt_,
                                            vtok[q:q + LC, t, h * HD:h * HD + HD], start=False, stop=True)
            last.then_inc(product, 1)

            def queries_and_within(t, h):
                po, j = (h % 2) * HD, h // 2
                nc.tensor.matmul(m.PS[po:po + HD, j, t * P:t * P + P], WU[:, place(t, h), 0:HD], RbT[:, place(t, h), :],
                                 start=True, stop=True)
                to = m.PS[:, 6 + t // 2, (t % 2) * 256 + h * HD:(t % 2) * 256 + h * HD + HD]
                nc.tensor.matmul(to, RbT[:, place(t, h), :], WU[:, place(t, h), HD:P], start=True, stop=False)
                return nc.tensor.matmul(to, RkT[:, place(t, h), :], vtok[:, t, h * HD:h * HD + HD], start=False, stop=True)

            for c in range(NC - 1):
                pe.wait_ge(dve_chain, 3 + c)
                for h in range(RH):
                    po, j = (h % 2) * HD, h // 2
                    last = nc.tensor.matmul(m.PS[po:po + HD, 2, j * HD:j * HD + HD], TTm[po:po + HD, c % 2, j, c // 2, :],
                                            Nst[po:po + HD, j, c, :], start=True, stop=True)
                last.then_inc(product, 1)
                for i in range(3 * c, min(3 * c + 3, N)):
                    last = queries_and_within(i // RH, i % RH)
                    if i == N - 1:
                        last.then_inc(within, 1)
            pe.wait_ge(dve_chain, 3 + NC)
            for c in range(NC):
                t, q = c // 2, (c % 2) * LC
                for h in range(RH):
                    po, j = (h % 2) * HD, h // 2
                    last = nc.tensor.matmul(m.PS[q:q + LC, 4 + h % 2, (t * 2 + j) * HD:(t * 2 + j) * HD + HD],
                                            QT[po:po + HD, j, c * LC:c * LC + LC], Nst[po:po + HD, j, c, :],
                                            start=True, stop=True)
            last.then_inc(product, 1)

        @block.vector
        def _(dve):
            V = nc.vector
            for a in range(2):
                V.tensor_copy(zin.rearrange("p (a t j) n -> p a t j n", a=2, j=2)[:, a, :, :, 0:HD],
                              abk[:, :, 0, :].rearrange("p t (j a d) -> p a t j d", a=2, d=HD)[:, a])
            V.memset(Nst[:, :, 0, :], 0.0)
            by_parity = pend.rearrange("p j (c a) -> p a j c", a=2)
            for po in (0, HD):
                on_diagonal = spread(spread(diag[po:po + HD, po:po + HD], 1, NC // 2), 1, 2)
                for a in range(2):
                    last = V.tensor_tensor(TTm[po:po + HD, a], on_diagonal, spread(by_parity[po:po + HD, a], 3, HD), ALU.mult)
            last.then_inc(decay, 1)
            dve.wait_ge(product, 1)
            V.tensor_copy(zin[:, :, HD:P], m.PS[:, 0:2, :].rearrange("p b (n d) -> p (b n) d", d=HD)).then_inc(dve_chain, 1)
            dve.wait_ge(product, 2)
            V.tensor_copy(WU[:, 0:N // 2], flat(m.PS[:, 4:6, :])).then_inc(dve_chain, 1)
            dve.wait_ge(product, 3)
            dve.wait_ge(decay, 1)
            flat_T = TTm.rearrange("p a j c n -> p a (j c n)")
            V.tensor_tensor(flat_T, flat_T, m.PS[:, 2:4, :], ALU.add).then_inc(dve_chain, 1)
            dve.wait_ge(act_chain, 2)
            for c in range(NC - 1):
                dve.wait_ge(product, 4 + c)
                V.tensor_tensor(Nst[:, :, c + 1, :], m.PS[:, 2, 0:2 * HD].rearrange("p (j n) -> p j n", j=2), Hm[:, c % 2, :, c // 2, :],
                                ALU.add).then_inc(dve_chain, 1)
            dve.wait_ge(within, 1)
            V.tensor_tensor(QT, m.PS[:, 0:2, :], rt, ALU.add).then_inc(dve_chain, 1)
            dve.wait_ge(act_chain, 3)
            dve.wait_ge(product, 4 + NC - 1)
            for a in range(2):
                part = y0.rearrange("p t (j a d) -> p a t j d", a=2, d=HD)[:, a]
                V.tensor_tensor(part, part, m.PS[:, 4 + a, :].rearrange("p (t j d) -> p t j d", t=TT, d=HD), ALU.add)

        @block.scalar
        def _(act):
            act.wait_ge(product, 2)
            nc.scalar.activation(WU[:, N // 2:N], flat(m.PS[:, 6:8, :]), ACT.Copy).then_inc(act_chain, 1)
            act.wait_ge(product, 3)
            nc.scalar.activation(Hm.rearrange("p a j c n -> p a (j c n)"), m.PS[:, 4:6, :], ACT.Copy).then_inc(act_chain, 1)
            act.wait_ge(within, 1)
            nc.scalar.activation(y0, m.PS[:, 6:8, :].rearrange("p b (t n) -> p (b t) n", t=2), ACT.Copy).then_inc(act_chain, 1)

    yv, sq = y0, B.take(TT, RH, HD)
    mean, var = B.take(TT, RH), B.take(TT, RH)
    assert B.at <= m.A.shape[1] - 2 * D
    with stage(nc, "rwkv4", "loaded squares root turned gated stored dve") as (loaded, squares, root, turned, gated, stored, dve_chain), \
            nc.Block() as block:
        @block.sync
        def _(sp):
            load_ahead(sp, ahead, loaded)

        @block.tensor
        def _(pe):
            for k in range(DK):
                if k == (QH + MH) * HD // P:
                    pe.wait_ge(gated, 1)
                for t in range(TT):
                    last = nc.tensor.transpose(m.PS[:, k, t * P:t * P + P], y[:, t, k * P:k * P + P], m.ident)
                last.then_inc(turned, 1)

        y4 = yv.rearrange("p t (h d) -> p t h d", d=HD)
        v4 = vtok.rearrange("p t (h d) -> p t h d", d=HD)

        @block.vector
        def _(dve):
            link = chain(dve, dve_chain)
            V = nc.vector
            link(V.tensor_reduce(mean, y4, AX.X, ALU.add))
            link(V.tensor_scalar(mean, mean, 1.0 / HD, None, ALU.mult))
            for t in range(TT):
                last = V.tensor_tensor(y4[:, t], y4[:, t], spread(mean[:, t], 2, HD), ALU.subtract)
            link(last)
            link(V.tensor_tensor(sq, y4, y4, ALU.mult))
            link(V.tensor_reduce(var, sq, AX.X, ALU.add))
            V.tensor_scalar(var, var, 1.0 / HD, 64e-5, ALU.mult, ALU.add).then_inc(squares, 1)
            for t in range(TT):
                last = V.tensor_tensor(v4[:, t], v4[:, t], spread(bonus[:, t], 2, HD), ALU.mult)
            link(last)
            link(V.tensor_tensor(vtok, vtok, spread(m.row("ln_b"), 1, TT), ALU.add))
            dve.wait_ge(root, 1)
            link(V.reciprocal(var, var))
            for t in range(TT):
                last = V.tensor_tensor(y4[:, t], y4[:, t], spread(var[:, t], 2, HD), ALU.mult)
            link(last)
            link(V.tensor_tensor(yv, yv, spread(m.row("ln_w"), 1, TT), ALU.mult))
            link(V.tensor_tensor(yv, yv, vtok, ALU.add))
            V.tensor_tensor(y[:, :, (QH + MH) * HD:D], yv, g, ALU.mult).then_inc(gated, 1)
            dve.wait_ge(turned, DK - 1)
            V.tensor_copy(yT[:, DK - 2, :], m.PS[:, DK - 2, :]).then_inc(stored, 1)

        @block.scalar
        def _(act):
            act.wait_ge(squares, 1)
            nc.scalar.activation(var, var, ACT.Sqrt).then_inc(root, 1)
            for k in (*range(DK - 2), DK - 1):
                act.wait_ge(turned, k + 1)
                nc.scalar.activation(yT[:, k, :], m.PS[:, k, :], ACT.Copy).then_inc(stored, 1)



def gated_embedding(nc, m, pt, w_gate, w_proj):
    with region(nc, "ple", TT * D + D_PLE // P * SEQ) as ple, region(nc, "scratch", TT * D + 64) as scratch:
        A = Arena(ple)
        gate = A.take(TT, D)
        pT = A.take(D_PLE // P, SEQ)
        with split_acts(nc, "h", DK, SEQ) as h:
            chunks = token_chunks(w_gate, (512, 512), gate)
            with weight_ring(nc) as ring:
                norm_transpose(nc, m, "ple_pre", m.x, TT, m.col("ple_pre"), h, Arena(scratch), project_slots(ring[0], chunks))
                project(nc, m, "ple_gate", h, chunks, ring=ring)
        with region(nc, "m_raw", 2, D) as raw:
            turn_tiles(nc, m, "ple_turn", lambda t, k: pt[:, t, k * P:k * P + P], D_PLE // P, pT, model_loads(raw, w_proj))
            project_model(nc, m, "ple_proj", pT, D_PLE // P, w_proj, raw, m.row("ple_post"), 1.0, gate)


def first_layer(nc, m, w, l, pt):
    def at(name):
        ap = w[name]
        names = "abc"[:len(ap.shape) - 1]
        sub = ap[bass.ds(l, 1)]
        return sub.rearrange(f"z {' '.join(names)} -> (z {names[0]}) {' '.join(names[1:])}")

    load_columns(nc, m, at("cols"), NCOL)
    rows = [(m.rows[:, 0:NROW], w["rows"][bass.ds(l, 1)].broadcast_to([P, NROW])), (pt, at("p").rearrange("(t p) n -> p t n", p=P))]
    m.table = (COLS, ROWS)
    feed_forward(nc, m, "ffn1", at("w_ffn1_in"), at("w_ffn1_out"), m.col("ffn1_pre"), m.row("ffn1_post"), rows)
    with region(nc, "mix", TT * TOK + 5 * (3 + SEQ) + DK * (1 + SEQ) + 8) as m.A:
        B = Arena(m.A)
        proj = B.take(TT, TOK)
        conv_slots = B.take(5, 3 + SEQ)
        qk = conv_slots[:, 0:4, 0:SEQ]
        raw = B.take(DK, 1 + SEQ)
        fm = raw[:, :, 1:1 + SEQ]
        with split_acts(nc, "h", DK, SEQ) as h, region(nc, "shift", SEQ) as shift:
            w_in = at("w_in")
            chunks = feature_chunks(w_in[:, RW:D_IN], DK, lambda j: fm[:, j, :])
            chunks += feature_chunks(w_in[:, ATTN_COLS:ML_V], 4, lambda j: conv_slots[:, j + 1, 3:3 + SEQ])
            chunks += token_chunks(w_in[:, 0:ATTN_COLS], (512, 256), proj)
            chunks += token_chunks(w_in[:, ML_V:RW], (264, 256), proj, TOK_V)

            def beside(dve, link, step, stored):
                V = nc.vector
                if step == 0:
                    V.memset(raw[:, :, 0:1], 0.0)
                    link(V.memset(conv_slots[:, 1:5, 0:3], 0.0))
                if step in (6, 10, 14):
                    stored((step - 6) // 4)
                if 6 <= step < 14:
                    j = step - 6
                    link(V.tensor_tensor(shift, raw[:, j, 0:SEQ], fm[:, j, :], ALU.subtract))
                    link(V.scalar_tensor_tensor(fm[:, j, :], shift, m.col("mu")[:, j:j + 1], fm[:, j, :], ALU.mult, ALU.add))
                if 14 <= step < 18:
                    j = step - 14
                    taps = m.col("conv")[:, 4 * j:4 * j + 4]
                    x = conv_slots[:, j + 1, :]
                    link(V.tensor_scalar(qk[:, j, :], x[:, 0:SEQ], taps[:, 0:1], None, ALU.mult))
                    for w in range(1, 4):
                        link(V.scalar_tensor_tensor(qk[:, j, :], x[:, w:w + SEQ], taps[:, w:w + 1], qk[:, j, :], ALU.mult, ALU.add))

                if step >= 22 and step < 26:
                    if step == 22:
                        stored(4)
                    rope(m, V, link, proj, step - 22, shift[:, 0:320].rearrange("p (a h d) -> p a h d", a=4, d=8))

            with weight_ring(nc) as ring:
                norm_transpose(nc, m, "mix_pre", m.x, TT, m.col("mix_pre"), h, Arena(m.A), project_slots(ring[0], chunks))
                project(nc, m, "mix_in", h, chunks, ring=ring, beside=beside)
        with region(nc, "mix_scratch", 22600) as scratch:
            attention(nc, m, proj, m.y, Arena(scratch))
            mlstm(nc, m, proj, qk, m.y, Arena(scratch))
            yT = m.A[:, 0:DK * SEQ].rearrange("p (k n) -> p k n", k=DK)
            w_raw = m.A[:, m.A.shape[1] - 2 * D:m.A.shape[1]].rearrange("p (s n) -> p s n", s=2)
            rwkv(nc, m, fm, m.y, Arena(scratch), at("rwkv_w_up"), at("rwkv_a_up"), at("rwkv_g_up"), yT,
                 model_loads(w_raw, at("w_out")))
        project_model(nc, m, "mix_out", yT, DK, at("w_out"), w_raw, m.row("mix_post"))
    feed_forward(nc, m, "ffn2", at("w_ffn2_in"), at("w_ffn2_out"), m.col("ffn2_pre"), m.row("ffn2_post"))
    gated_embedding(nc, m, pt, at("w_ple_gate"), at("w_ple_proj"))



def rg_lru(nc, m, c, gate, yT, A, weights):
    gw = A.take(2, 4, HD)
    r, i, a, asq, sq = (A.take(4, SEQ) for _ in range(5))
    lam = m.col("lam")
    la, e, z, z2, sp = (A.take(4) for _ in range(5))
    with stage(nc, "lru", "loaded dve lam_in lam_out product gates la_in act squares root gelu") as \
            (loaded, dve_chain, lam_in, lam_out, product, gates, la_in, act_out, squares, root, gelu), \
            nc.Block() as block:
        @block.sync
        def _(sp_):
            for which in range(2):
                sp_.dma_start(gw[:, which], weights[which].rearrange("j p n -> p j n")).then_inc(loaded, 16)

        @block.tensor
        def _(pe):
            pe.wait_ge(loaded, 32)
            for which in range(2):
                for j in range(4):
                    for po in (0, HD):
                        last = nc.tensor.matmul(m.PS[po:po + HD, 4 * which + j, :], gw[po:po + HD, which, j, :],
                                                c[po:po + HD, j, :], start=True, stop=True)
                last.then_inc(product, 1)

        @block.scalar
        def _(act):
            act.wait_ge(lam_in, 1)
            nc.scalar.activation(e, la, ACT.Exp, scale=-1.0).then_inc(lam_out, 1)
            def gate_of(which, to, bias):
                act.wait_ge(product, which + 1)
                for j in range(4):
                    last = nc.scalar.activation(to[:, j], m.PS[:, 4 * which + j, :], ACT.Sigmoid, bias=m.col(bias)[:, j:j + 1])
                last.then_inc(gates, 1)

            gate_of(0, r, "ba")
            act.wait_ge(la_in, 1)
            act.wait_ge(gates, 1)
            for j in range(4):
                last = nc.scalar.activation(a[:, j], r[:, j], ACT.Exp, scale=sp[:, j:j + 1])
            last.then_inc(act_out, 1)
            for j in range(4):
                last = nc.scalar.activation(sq[:, j], r[:, j], ACT.Tanh, scale=la[:, j:j + 1])
            last.then_inc(act_out, 1)
            gate_of(1, i, "bx")
            act.wait_ge(squares, 1)
            nc.scalar.activation(sq, sq, ACT.Sqrt).then_inc(root, 1)
            nc.scalar.activation(gate, gate, ACT.Gelu_apprx_tanh).then_inc(gelu, 1)

        @block.vector
        def _(dve):
            link = chain(dve, dve_chain)
            V = nc.vector
            V.scalar_tensor_tensor(la, lam, -1.0, lam, ALU.mult, ALU.max).then_inc(lam_in, 1)
            dve.wait_ge(lam_out, 1)
            log1p_series(link, V, e, z, z2, sp)
            link(V.tensor_scalar(la, lam, -1.0, 0.0, ALU.mult, ALU.max))
            link(V.tensor_tensor(sp, sp, la, ALU.add))
            link(V.tensor_scalar(la, sp, 8.0, None, ALU.mult))
            V.tensor_scalar(sp, sp, -8.0, None, ALU.mult).then_inc(la_in, 1)
            dve.wait_ge(act_out, 1)
            link(V.tensor_tensor(asq, a, a, ALU.mult))
            dve.wait_ge(act_out, 2)
            V.scalar_tensor_tensor(sq, asq, 1.0, sq, ALU.add, ALU.mult).then_inc(squares, 1)
            dve.wait_ge(gates, 2)
            link(V.tensor_tensor(i, i, c, ALU.mult))
            dve.wait_ge(root, 1)
            link(V.tensor_tensor(i, i, sq, ALU.mult))
            for j in range(4):
                last = V.tensor_tensor_scan(c[:, j], a[:, j], i[:, j], 0.0, ALU.mult, ALU.add)
            link(last)
            dve.wait_ge(gelu, 1)
            V.tensor_tensor(yT, c, gate, ALU.mult)


def delta_net(nc, m, f, zab, yT, A, ahead):
    N = 4 * TT
    araw, beta, g, e, z, z2, gcol, eg, kds, egl = (A.take(N) for _ in range(10))
    start = A.at
    sq = A.take(8, SEQ)
    th = lambda ap: ap.rearrange("p (t h) -> p t h", h=4)

    select, root_of = A.take(7), A.take(2, SEQ, parts=4)
    with stage(nc, "gdn1", "silu squared select summed shifted root inverse spread dve") as \
            (silu, squared, selected, summed, shifted, root, inverse, spread_out, dve_chain), nc.Block() as block:
        group = lambda part: slice(4 * part, 4 * part + 4)
        inverses = lambda part: m.PS[:, 4 - 4 * part:8 - 4 * part, :].rearrange("p b n -> p (b n)")

        @block.vector
        def _(dve):
            V = nc.vector
            link = chain(dve, dve_chain)
            link(V.memset(select, 0.0))
            V.memset(select[:, 3:4], 1.0).then_inc(selected, 1)
            for part in range(2):
                dve.wait_ge(summed, part + 1)
                V.tensor_scalar(root_of[:, part], m.PS[0:4, part, :], EPS, None, ALU.add).then_inc(shifted, 1)
            for part in range(2):
                dve.wait_ge(root, part + 1)
                V.reciprocal(root_of[:, part], root_of[:, part]).then_inc(inverse, 1)
            for part in range(2):
                dve.wait_ge(spread_out, part + 1)
                V.scalar_tensor_tensor(f[:, group(part)].rearrange("p a b -> p (a b)"), f[:, group(part)].rearrange("p a b -> p (a b)"),
                                       (P ** -0.5, 1.0)[part], inverses(part), ALU.mult, ALU.mult)

        @block.scalar
        def _(act):
            for part in range(2):
                nc.scalar.activation(f[:, group(part)], f[:, group(part)], ACT.Silu).then_inc(silu, 1)
                act.wait_ge(silu, part + 1)
                nc.scalar.activation(sq[:, group(part)], f[:, group(part)], ACT.Square).then_inc(squared, 1)
            for part in range(2):
                act.wait_ge(shifted, part + 1)
                nc.scalar.activation(root_of[:, part], root_of[:, part], ACT.Sqrt).then_inc(root, 1)
            nc.scalar.activation(f[:, group(2)], f[:, group(2)], ACT.Silu).then_inc(silu, 1)

        @block.tensor
        def _(pe):
            pe.wait_ge(selected, 1)
            for part in range(2):
                pe.wait_ge(squared, part + 1)
                for h in range(4):
                    last = nc.tensor.matmul(m.PS[0:4, part, :], select[:, 3 - h:7 - h], sq[:, 4 * part + h, :],
                                            start=(h == 0), stop=(h == 3))
                last.then_inc(summed, 1)
            for part in range(2):
                pe.wait_ge(inverse, part + 1)
                for h in range(4):
                    last = nc.tensor.matmul(m.PS[:, 4 - 4 * part + h, :], m.pick[:, h, :], root_of[:, part], start=True, stop=True)
                last.then_inc(spread_out, 1)

    A.at = start
    DT, D_, attnT, AT, QT = (A.take(N, P) for _ in range(5))
    zin = A.take(N, 2 * P)
    kd = A.take(N, P)
    kbT = A.take(N, P)
    bb, gb, A0 = AT, attnT, D_
    four = lambda ap, h0: ap[:, h0:h0 + 4, :].rearrange("p h (t k) -> p t h k", t=TT)
    banks = lambda b: m.PS[:, b:b + 4, :].rearrange("p b (h k) -> p (b h) k", h=4)
    banks4 = lambda b: m.PS[:, b:b + 4, :].rearrange("p b (h k) -> p b h k", h=4)
    view4 = lambda ap: ap.rearrange("p (t h) k -> p t h k", h=4)
    with stage(nc, "gdn2", "dve abs_in exp_out product copies dist act_out") as (dve_chain, abs_in, exp_out, product, copies, dist, act_out), \
            nc.Block() as block:
        @block.vector
        def _(dve):
            link = chain(dve, dve_chain)
            V = nc.vector
            link(V.tensor_tensor(th(araw), zab[:, :, 512:516], spread(m.row("dt_bias"), 1, TT), ALU.add))
            link(V.scalar_tensor_tensor(e, araw, -1.0, araw, ALU.mult, ALU.max))
            V.tensor_copy(th(beta), zab[:, :, 516:520]).then_inc(abs_in, 1)
            dve.wait_ge(exp_out, 1)
            log1p_series(link, V, e, z, z2, g)
            link(V.scalar_tensor_tensor(g, araw, 0.0, g, ALU.max, ALU.add))
            link(V.scalar_tensor_tensor(th(g), th(g), -1.0, spread(m.row("a_log"), 1, TT), ALU.mult, ALU.mult))
            V.tensor_copy(gb, spread(g, 2, P))
            V.tensor_copy(bb, spread(beta, 2, P)).then_inc(copies, 1)
            dve.wait_ge(product, 1)
            link(V.tensor_copy(gcol, m.PS[:, 4, 0:N]))
            V.tensor_copy(egl, banks(0)[:, :, P - 1])
            link(V.tensor_tensor(DT, banks(0), spread(gcol, 2, P), ALU.subtract))
            V.tensor_tensor(kds, egl, gcol, ALU.subtract)
            V.tensor_scalar(D_, DT, -1.0, 0.0, ALU.mult, ALU.min)
            link(V.tensor_scalar(DT, DT, 0.0, None, ALU.min))
            V.memset(z, 0.0).then_inc(dist, 1)
            dve.wait_ge(product, 2)
            V.tensor_tensor(view4(kbT), four(f, 4), banks4(4), ALU.mult)
            dve.wait_ge(act_out, 1)
            V.tensor_tensor(DT, DT, spread(m.upper, 1, N), ALU.mult)
            V.tensor_tensor(D_, D_, spread(m.lower8, 1, N), ALU.mult)
            V.tensor_tensor(view4(QT), four(f, 0), view4(QT), ALU.mult)

        @block.scalar
        def _(act):
            act.wait_ge(abs_in, 1)
            nc.scalar.activation(e, e, ACT.Exp, scale=-1.0)
            nc.scalar.activation(m.row("a_log"), m.row("a_log"), ACT.Exp)
            nc.scalar.activation(beta, beta, ACT.Sigmoid).then_inc(exp_out, 1)
            act.wait_ge(dist, 1)
            nc.scalar.activation(QT, banks(0), ACT.Exp)
            nc.scalar.activation(DT, DT, ACT.Exp)
            nc.scalar.activation(D_, D_, ACT.Exp)
            nc.scalar.activation(eg, gcol, ACT.Exp)
            nc.scalar.activation(kds, kds, ACT.Exp)
            nc.scalar.activation(egl, egl, ACT.Exp).then_inc(act_out, 1)

        @block.tensor
        def _(pe):
            pe.wait_ge(copies, 1)
            nc.tensor.matmul(m.PS[:, 4, 0:N], m.upper, g, start=True, stop=True)
            for n in range(N):
                last = nc.tensor.matmul(banks(0)[:, n, :], gb[:, n, :], m.upper, start=True, stop=True)
            last.then_inc(product, 1)
            pe.wait_ge(dist, 1)
            for n in range(N):
                last = nc.tensor.matmul(banks(4)[:, n, :], bb[:, n, :], m.ident, start=True, stop=True)
            last.then_inc(product, 1)

    with stage(nc, "gdn3", "product dve turned") as (product, dve_chain, turned), nc.Block() as block:
        @block.vector
        def _(dve):
            V = nc.vector
            link = chain(dve, dve_chain)
            dve.wait_ge(product, 1)
            link(V.scalar_tensor_tensor(AT, banks(0), -1.0, DT, ALU.mult, ALU.mult))
            V.tensor_tensor(AT, AT, spread(m.strict_upper, 1, N), ALU.mult)
            dve.wait_ge(product, 2)
            link(V.scalar_tensor_tensor(A0, banks(4), -1.0, D_, ALU.mult, ALU.mult))
            dve.wait_ge(product, 3)
            link(V.tensor_tensor(attnT, banks(0), DT, ALU.mult))
            dve.wait_ge(turned, 1)
            V.tensor_tensor(zin[:, :, 0:P], banks(4), spread(beta, 2, P), ALU.mult)
            link(V.tensor_tensor(eg, eg, beta, ALU.mult))
            dve.wait_ge(turned, 2)
            V.tensor_tensor(kd, banks(0), spread(kds, 2, P), ALU.mult)
            V.tensor_tensor(zin[:, :, P:2 * P], banks(0), spread(eg, 2, P), ALU.mult)

        @block.tensor
        def _(pe):
            def scores(b, left, right, lk, rk):
                for t in range(TT):
                    for h in range(4):
                        lo = left[:, t * 4 + h, :] if lk is None else left[:, lk + h, t * P:t * P + P]
                        hi = right[:, t * 4 + h, :] if rk is None else right[:, rk + h, t * P:t * P + P]
                        last = nc.tensor.matmul(banks(b)[:, t * 4 + h, :], lo, hi, start=True, stop=True)
                last.then_inc(product, 1)

            scores(0, f, kbT, 4, None)
            scores(4, kbT, f, None, 4)
            pe.wait_ge(dve_chain, 1)
            scores(0, f, f, 4, 0)
            pe.wait_ge(dve_chain, 2)
            for b, head0, after in ((4, 8, None), (0, 4, 3)):
                if after:
                    pe.wait_ge(dve_chain, after)
                for t in range(TT):
                    for h in range(4):
                        last = nc.tensor.transpose(banks(b)[:, t * 4 + h, :], f[:, head0 + h, t * P:t * P + P], m.ident)
                last.then_inc(turned, 1)

    B = Arena(m.A)
    XT = invert(nc, m, "gdn_inv", AT, A0, (8, 16, 32, 64), B)
    B.at = N * P
    UW = B.take(N, 2 * P)
    Nst = B.take(TT + 1, GH, P)
    TTm, Hm, y0 = AT, A0, DT
    with stage(nc, "gdn4", "product minus dve act") as (product, minus, dve_chain, act_chain), nc.Block() as block:
        state = lambda t: m.PS[:, 0, :] if t % 2 == 0 else m.PS[:, 1, :]

        @block.tensor
        def _(pe):
            for n in range(N):
                last = nc.tensor.matmul(m.PS[:, n // 2, (n % 2) * 256:(n % 2 + 1) * 256], XT[:, n, :], zin[:, n, :],
                                        start=True, stop=True)
                if n == N // 2 - 1:
                    last.then_inc(product, 1)
            last.then_inc(product, 1)
            pe.wait_ge(dve_chain, 1)
            pe.wait_ge(act_chain, 1)
            for n in range(N):
                last = nc.tensor.matmul(banks(4)[:, n, :], UW[:, n, P:2 * P], kd[:, n, :], start=True, stop=True)
            last.then_inc(product, 1)
            for n in range(N):
                last = nc.tensor.matmul(banks(0)[:, n, :], kd[:, n, :], UW[:, n, 0:P], start=True, stop=True)
            last.then_inc(product, 1)
            for t in range(TT - 1):
                pe.wait_ge(dve_chain, 2 + t)
                if t == 0:
                    pe.wait_ge(act_chain, 2)
                for h in range(GH):
                    last = nc.tensor.matmul(state(t)[:, h * P:h * P + P], TTm[:, t * 4 + h, :], Nst[:, t, h, :],
                                            start=True, stop=True)
                last.then_inc(product, 1)
                if t == 0:
                    for n in range(N):
                        last = nc.tensor.matmul(banks(4)[:, n, :], UW[:, n, P:2 * P], attnT[:, n, :], start=True, stop=True)
                    last.then_inc(minus, 1)
            pe.wait_ge(dve_chain, 2 + TT)
            for n in range(N):
                nc.tensor.matmul(banks(0)[:, n, :], attnT[:, n, :], UW[:, n, 0:P], start=True, stop=False)
                last = nc.tensor.matmul(banks(0)[:, n, :], QT[:, n, :], Nst[:, n // 4, n % 4, :], start=False, stop=True)
            last.then_inc(product, 1)

        @block.scalar
        def _(act):
            act.wait_ge(product, 2)
            nc.scalar.activation(UW[:, N // 2:], m.PS[:, 4:8, :].rearrange("p b (n k) -> p (b n) k", n=2), ACT.Copy)\
                .then_inc(act_chain, 1)
            act.wait_ge(product, 4)
            nc.scalar.activation(Hm, banks(0), ACT.Copy).then_inc(act_chain, 1)

        @block.vector
        def _(dve):
            V = nc.vector
            V.memset(Nst[:, 0], 0.0)
            dve.wait_ge(product, 1)
            V.tensor_copy(UW[:, 0:N // 2], m.PS[:, 0:4, :].rearrange("p b (n k) -> p (b n) k", n=2)).then_inc(dve_chain, 1)
            dve.wait_ge(product, 3)
            for n in range(N):
                last = V.scalar_tensor_tensor(TTm[:, n, :], m.ident, egl[:, n:n + 1], banks(4)[:, n, :], ALU.mult, ALU.subtract)
            last.then_inc(dve_chain, 1)
            dve.wait_ge(act_chain, 2)
            for t in range(TT - 1):
                dve.wait_ge(product, 5 + t)
                V.tensor_tensor(Nst[:, t + 1], state(t).rearrange("p (h k) -> p h k", h=GH),
                                Hm[:, 4 * t:4 * t + 4, :], ALU.add).then_inc(dve_chain, 1)
            dve.wait_ge(minus, 1)
            V.tensor_tensor(QT, QT, banks(4), ALU.subtract).then_inc(dve_chain, 1)
            dve.wait_ge(product, 5 + TT - 1)
            V.tensor_copy(y0, banks(0))

    ms, o2 = z, QT
    with stage(nc, "gdn5", "loaded squares root dve silu gated turned") as \
            (loaded, squares, root, dve_chain, silu, gated, turned), nc.Block() as block:
        @block.sync
        def _(sp):
            load_ahead(sp, ahead, loaded)

        zz = zab[:, :, 0:512].rearrange("p t (h k) -> p t h k", h=4)

        @block.vector
        def _(dve):
            link = chain(dve, dve_chain)
            V = nc.vector
            link(V.tensor_tensor(o2, y0, y0, ALU.mult))
            link(V.tensor_reduce(ms, o2, AX.X, ALU.add))
            V.tensor_scalar(ms, ms, 1.0 / P, EPS, ALU.mult, ALU.add).then_inc(squares, 1)
            dve.wait_ge(root, 1)
            link(V.reciprocal(ms, ms))
            link(V.tensor_tensor(y0, y0, spread(ms, 2, P), ALU.mult))
            link(V.tensor_tensor(y0, y0, spread(m.row("gdn_norm"), 1, N), ALU.mult))
            dve.wait_ge(silu, 1)
            V.tensor_tensor(view4(y0), view4(y0), zz, ALU.mult).then_inc(gated, 1)
            dve.wait_ge(turned, 1)
            V.tensor_copy(yT, m.PS[:, 0:4, :])

        @block.scalar
        def _(act):
            nc.scalar.activation(zz, zz, ACT.Silu).then_inc(silu, 1)
            act.wait_ge(squares, 1)
            nc.scalar.activation(ms, ms, ACT.Sqrt).then_inc(root, 1)

        @block.tensor
        def _(pe):
            pe.wait_ge(gated, 1)
            for h in range(4):
                for t in range(TT):
                    last = nc.tensor.transpose(m.PS[:, h, t * P:t * P + P], y0[:, t * 4 + h, :], m.ident)
            last.then_inc(turned, 1)


def hybrid_mixer(nc, m, w, mem):
    w_in = w["w_in_2"]
    with region(nc, "m_raw", 2, D) as raw, region(nc, "hybrid", 21 * SEQ) as m.A, region(nc, "zab", TT, 520) as zab:
        slots = Arena(m.A).take(21, SEQ)
        XR, QKV, GATE = 1, 5, 17
        with split_acts(nc, "h", DK, SEQ) as h:
            chunks = feature_chunks(w_in[:, G_XR:G_GATE], 4, lambda j: slots[:, XR + j, :])
            chunks += feature_chunks(w_in[:, G_GATE:IN2], 4, lambda j: slots[:, GATE + j, :])
            chunks += feature_chunks(w_in[:, 0:G_Z], 12, lambda j: slots[:, QKV + j, :])
            chunks += token_chunks(w_in[:, G_Z:G_XR], (264, 256), zab)

            def beside(dve, link, step, stored):
                if 6 <= step < 10:
                    if step == 6:
                        stored(0)
                    n = step - 6
                    convolve(nc.vector, link, n, m.col("conv_lru").rearrange("p (j w) -> p j w", w=4),
                             slots[:, XR + n, :], slots[:, XR + n - 1, :], m.col("conv_b"))
                if 14 <= step < 26:
                    n = step - 14
                    if n % 4 == 0:
                        stored(2 + n // 4)
                    convolve(nc.vector, link, n, m.col("conv_qkv").rearrange("p (j w) -> p j w", w=4),
                             slots[:, QKV + n, :], slots[:, QKV + n - 1, :])

            with weight_ring(nc) as ring:
                norm_transpose(nc, m, "hyb_pre", m.x, TT, m.col("mix"), h, Arena(m.A),
                               project_slots(ring[0], chunks) + [(m.rows[:, 0:NROW2], w["rows_2"].broadcast_to([P, NROW2])),
                                                                 (mem, w["mem_2"].rearrange("(t p) n -> p t n", p=P))])
                project(nc, m, "hyb_in", h, chunks, ring=ring, beside=beside)
        with region(nc, "hybrid_scratch", 18700) as scratch:
            rg_lru(nc, m, slots[:, XR - 1:XR + 3], slots[:, GATE:GATE + 4], m.hT[:, 4:8], Arena(scratch), w["lru_w_2"])
            delta_net(nc, m, slots[:, QKV - 1:QKV + 11], zab, m.hT[:, 0:4], Arena(scratch), model_loads(raw, w["w_out_2"]))
        project_model(nc, m, "hyb_out", m.hT, DK, w["w_out_2"], raw)



def cross_attention(nc, m, w, mem):
    with ExitStack() as room:
        raw = room.enter_context(region(nc, "m_raw", 2, D))
        kT = room.enter_context(region(nc, "xa_kT", DK, MEM))
        v = room.enter_context(region(nc, "xa_v", 2, D))
        big = room.enter_context(region(nc, "xa", DK * SEQ + 4 * TT * MEM + 64))
        B = Arena(big)
        qT = B.take(DK, SEQ)
        keep = B.at
        with split_acts(nc, "mem", DK, MEM) as h:
            chunks = feature_chunks(w["xattn_wkv_2"][:, 0:D], DK, lambda j: kT[:, j, :])
            chunks += token_chunks(w["xattn_wkv_2"][:, D:2 * D], (512, 512), v)
            with weight_ring(nc) as ring:
                norm_transpose(nc, m, "xa_mem", mem, 2, m.col("mem"), h, Arena(big), project_slots(ring[0], chunks))
                project(nc, m, "xa_kv", h, chunks, T=2, ring=ring)
        with split_acts(nc, "h", DK, SEQ) as h:
            chunks = feature_chunks(w["xattn_wq_2"], DK, lambda j: qT[:, j, :])
            with weight_ring(nc) as ring:
                norm_transpose(nc, m, "xa_pre", m.x, TT, m.col("xattn"), h, Arena(big), project_slots(ring[0], chunks))
                project(nc, m, "xa_q", h, chunks, ring=ring)
        B.at = keep
        attend_memory(nc, m, qT, kT, v, B, model_loads(raw, w["xattn_wo_2"]))
        project_model(nc, m, "xa_out", m.hT, DK, w["xattn_wo_2"], raw)


def attend_memory(nc, m, qT, kT, v, B, ahead):
    S = B.take(TT, XH, MEM)
    mx, den = B.take(TT, XH), B.take(TT, XH)
    pT = qT
    with stage(nc, "xa", "loaded scored dve shifted act probs turned copied product stored") as \
            (loaded, scored, dve_chain, shifted, act_out, probs, turned, copied, product, stored), nc.Block() as block:
        banks = lambda t, n: m.PS[:, 2 * t:2 * t + 2, :].rearrange("p b (i k) -> p (b i) k", i=n // 2)
        tokens = lambda t: slice(t * P, t * P + P)

        @block.sync
        def _(sp):
            load_ahead(sp, ahead, loaded)

        @block.tensor
        def _(pe):
            def result(t):
                pe.wait_ge(copied, t + 1)
                for h in range(XH):
                    for half in range(2):
                        for b in range(2):
                            last = nc.tensor.matmul(banks(t, DK)[:, 2 * h + half, :], v[:, b, h * 256 + half * P:h * 256 + half * P + P],
                                                    pT[:, 2 * h + b, tokens(t)], start=(b == 0), stop=(b == 1))
                last.then_inc(product, 1)

            for t in range(TT):
                for h in range(XH):
                    for b in range(2):
                        last = nc.tensor.matmul(banks(t, XH)[:, h, :], qT[:, 2 * h + b, tokens(t)], kT[:, 2 * h + b, :],
                                                start=(b == 0), stop=(b == 1))
                last.then_inc(scored, 1)
            for t in range(TT):
                pe.wait_ge(probs, t + 1)
                for h in range(XH):
                    for b in range(2):
                        last = nc.tensor.transpose(banks(t, DK)[:, 2 * h + b, :], S[:, t, h, b * P:b * P + P], m.ident)
                last.then_inc(turned, 1)
                if t:
                    result(t - 1)
            result(TT - 1)

        @block.vector
        def _(dve):
            link = chain(dve, dve_chain)
            V = nc.vector

            def normalise(t):
                dve.wait_ge(act_out, t + 1)
                link(V.tensor_reduce(den[:, t], S[:, t], AX.X, ALU.add))
                link(V.reciprocal(den[:, t], den[:, t]))
                V.tensor_tensor(S[:, t], S[:, t], spread(den[:, t], 2, MEM), ALU.mult).then_inc(probs, 1)

            for t in range(TT):
                dve.wait_ge(scored, t + 1)
                link(V.tensor_reduce(mx[:, t], banks(t, XH), AX.X, ALU.max))
                V.tensor_tensor(S[:, t], banks(t, XH), spread(mx[:, t], 2, MEM), ALU.subtract).then_inc(shifted, 1)
                if t:
                    normalise(t - 1)
            normalise(TT - 1)
            for t in range(TT):
                dve.wait_ge(product, t + 1)
                V.tensor_copy(m.hT[:, :, tokens(t)], banks(t, DK)).then_inc(stored, 1)

        @block.scalar
        def _(act):
            def copy_turned(t):
                act.wait_ge(turned, t + 1)
                nc.scalar.activation(pT[:, :, tokens(t)], banks(t, DK), ACT.Copy).then_inc(copied, 1)

            for t in range(TT):
                act.wait_ge(shifted, t + 1)
                nc.scalar.activation(S[:, t], S[:, t], ACT.Exp, scale=256 ** -0.5).then_inc(act_out, 1)
                if t:
                    copy_turned(t - 1)
            copy_turned(TT - 1)



def peer(nc, m, w):
    with ExitStack() as room:
        keep = room.enter_context(region(nc, "peer_keep", TT * D + 4 * TT * PH * TOPK))
        qT = room.enter_context(region(nc, "peer_q", 2 * PH, SEQ))
        sub = room.enter_context(region(nc, "subkeys", 2 * PH, NKEY))
        with split_acts(nc, "h", DK, SEQ) as h:
            chunks = feature_chunks(w["peer_wq_2"], 2 * PH, lambda j: qT[:, j, :])
            with weight_ring(nc) as ring:
                norm_transpose(nc, m, "peer_pre", m.x, TT, m.col("ffn"), h, Arena(keep),
                               project_slots(ring[0], chunks) + [(sub, w["subkeys_2"])])
                project(nc, m, "peer_q", h, chunks, ring=ring)
        with region(nc, "peer_rows", 17 * D + 1200) as m.R:
            retrieve(nc, m, w, qT, sub, keep)


def retrieve(nc, m, w, qT, sub, keep):
    SLOTS = 8
    NE = PH * TOPK
    PAIRS = NE // (2 * SLOTS)
    STEPS = 29
    K = Arena(keep)
    K.take(2 * TT)
    xn = K.take(TT, D)
    idx = K.take(TT * NE, dtype=U32)
    gate, dots = K.take(TT * NE), K.take(TT * NE)
    R = Arena(m.R)
    rows = [R.take(D) for _ in range(2 * SLOTS)]
    sc, vals, ids_f = R.take(2, NKEY), R.take(2, TOPK), R.take(2, TOPK)
    ids = R.take(2, TOPK, dtype=U32)
    cand = R.take(2, TOPK, TOPK)
    best, pos = R.take(TOPK), R.take(TOPK, dtype=U32)
    half_u, half_f, e12 = R.take(2, TOPK, dtype=U32), R.take(2, TOPK), R.take(2, TOPK)
    den = R.take(2)
    iota, iota_i = R.take(TOPK), R.take(TOPK, dtype=I32)
    diagonal = R.take(SLOTS, P)
    now = [R.take(SLOTS, dtype=U32) for _ in range(2)]
    zero, spare, dve_zero, dve_spare = (R.take(2) for _ in range(4))
    score_columns = m.PS.rearrange("p b n -> p (b n)")
    with stage(nc, "peer", "iota_done zeroed ready scored taken steps exp_in exp_out chosen copied used0 used1 gelu gated diagonal_in added "
               + " ".join(f"row{s}" for s in range(2 * SLOTS))) as \
            (iota_done, zeroed, ready, scored, taken, steps, exp_in, exp_out, chosen, copied, used0, used1, gelu, gated, diagonal_in, added, *row_in), \
            nc.Block() as block:
        @block.tensor
        def _(pe):
            def score(t):
                for n in range(2 * PH):
                    last = nc.tensor.matmul(m.PS[:, n // 4, (n % 4) * P:(n % 4 + 1) * P],
                                            qT[:, n, t * P:t * P + P], sub[:, n, :], start=True, stop=True)
                last.then_inc(scored, 1)

            def add_rows(t, pair, first, last):
                for s in range(SLOTS):
                    slot = SLOTS + s
                    pe.wait_ge(diagonal_in, (pair + t * PAIRS) * SLOTS + (s + 1))
                    pe.wait_ge(row_in[slot], (pair + (2 * t + 1) * PAIRS + 1) * 16)
                    for half in range(2):
                        done = nc.tensor.matmul(m.PS[:, 4 + half, :], diagonal[:, s, :], rows[slot][:, half * 512:half * 512 + 512],
                                                start=first and s == 0, stop=last and s == SLOTS - 1)
                    done.then_inc(used1, 1)

            score(0)
            for t in range(TT):
                if t + 1 < TT:
                    pe.wait_ge(taken, (t + 1) * PH)
                    score(t + 1)
                if t > 0:
                    pe.wait_ge(added, t)
                add_rows(t, 0, True, False)
                with pe.Fori(1, PAIRS - 1) as pair:
                    add_rows(t, pair, False, False)
                add_rows(t, PAIRS - 1, False, True)

        @block.scalar
        def _(act):
            def exp(head):
                act.wait_ge(exp_in, head + 1)
                nc.scalar.activation(best, best, ACT.Exp).then_inc(exp_out, 1)

            with act.Fori(0, PH) as head:
                exp(head)
            for t in range(TT):
                act.wait_ge(used0, (2 * t + 1) * PAIRS * SLOTS)
                act.wait_ge(used1, (2 * t + 1) * PAIRS * SLOTS)
                mine = dots[:, t * NE:t * NE + NE]
                nc.scalar.activation(mine, mine, ACT.Gelu_apprx_tanh).then_inc(gelu, 1)
                act.wait_ge(gated, t + 1)
                with act.Fori(0, PAIRS) as pair:
                    for s in range(SLOTS):
                        act.wait_ge(used1, (pair + (2 * t + 1) * PAIRS) * SLOTS - SLOTS + (s + 1))
                        nc.scalar.activation(diagonal[:, s, :], m.ident, ACT.Copy,
                                             scale=dots[:, bass.ds(pair * (2 * SLOTS) + (t * NE + SLOTS + s), 1)]).then_inc(diagonal_in, 1)
                    if t + 1 < TT:
                        exp(pair + (t + 1) * PH)

        @block.gpsimd
        def _(pool):
            used = (used0, used1)

            def turn(table, t, number, column, parity, first):
                if not first:
                    pool.wait_ge(used[parity], number * SLOTS)
                nc.gpsimd.tensor_copy(now[parity], idx[:, bass.ds(column + t * NE, SLOTS)]).then_inc(copied, 1)
                pool.wait_ge(copied, (number * 2 + parity) * 2 + 1)
                nc.gpsimd.tensor_tensor(spare, zero, zero, ALU.add).then_inc(copied, 1)
                for s in range(SLOTS):
                    slot = parity * SLOTS + s
                    nc.gpsimd.indirect_dma_start(out=rows[slot], out_offset=None, in_=table,
                                                 in_offset=bass.IndirectOffsetOnAxis(ap=now[parity][:, s:s + 1], axis=0))\
                        .then_inc(row_in[slot], 16)

            nc.gpsimd.iota(iota_i, pattern=[[1, TOPK]], base=0, channel_multiplier=0).then_inc(iota_done, 1)
            nc.gpsimd.memset(zero, 0.0).then_inc(zeroed, 1)
            pool.wait_ge(zeroed, 1)
            pool.wait_ge(chosen, 1)
            turn(w["peer_u_2"], 0, 0, 0, 0, True)
            turn(w["peer_u_2"], 0, 0, SLOTS, 1, True)
            for t in range(TT):
                with pool.Fori(1 if t == 0 else 0, PAIRS) as pair:
                    pool.wait_ge(chosen, pair + t * PH + 1)
                    for parity in range(2):
                        turn(w["peer_u_2"], t, pair + 2 * t * PAIRS, (pair * 2 + parity) * SLOTS, parity, False)
                with pool.Fori(0, PAIRS) as pair:
                    for parity in range(2):
                        turn(w["peer_v_2"], t, pair + (2 * t + 1) * PAIRS, (pair * 2 + parity) * SLOTS, parity, False)

        @block.vector
        def _(dve):
            V = nc.vector
            dve.wait_ge(iota_done, 1)
            V.tensor_copy(iota, iota_i).then_inc(ready, 1)
            V.memset(dve_zero, 0.0).then_inc(ready, 1)
            V.tensor_tensor(xn, xn, spread(m.row("ffn_row"), 1, TT), ALU.mult).then_inc(ready, 1)
            dve.wait_ge(ready, 3)

            class Head:

                def __init__(self, t, head, between=lambda: None):
                    self.t, self.head, self.step, self.between = t, head, 0, between
                    self.before = head * STEPS + t * PH * STEPS
                    self.column = head * TOPK + t * NE

                def link(self, instruction):
                    self.step += 1
                    instruction.then_inc(steps, 1)
                    self.between()
                    dve.wait_ge(steps, self.before + self.step)

                def settle(self, instruction):
                    self.link(instruction)
                    self.step += 1
                    V.tensor_tensor(dve_spare, dve_zero, dve_zero, ALU.add).then_inc(steps, 1)

                def largest8(self, values, indices, table, part, spend):
                    for v, x in zip(values, table):
                        last = V.max(v[:, part], x)
                    self.settle(last)
                    for v, i, x in zip(values, indices, table):
                        last = V.max_index(i[:, part], v[:, part], x)
                    if not spend:
                        self.link(last)
                    else:
                        self.settle(last)
                        for v, x in zip(values, table):
                            last = V.match_replace(x, v[:, part], x, -3.0e38)
                        self.settle(last)

                def halves(self):
                    return [vals[:, s, :] for s in range(2)], [ids[:, s, :] for s in range(2)], [sc[:, s, :] for s in range(2)]

                def first_halves(self):
                    dve.wait_ge(scored, self.t + 1)
                    V.tensor_copy(sc.rearrange("p s k -> p (s k)"), score_columns[
                        :, bass.ds(self.head * (2 * NKEY), 2 * NKEY)]).then_inc(taken, 1)
                    dve.wait_ge(taken, self.head + self.t * PH + 1)
                    self.step += 1
                    V.tensor_tensor(dve_spare, dve_zero, dve_zero, ALU.add).then_inc(steps, 1)
                    self.largest8(*self.halves(), slice(0, 8), True)

                def sums(self):
                    self.largest8(*self.halves(), slice(8, 16), False)
                    V.tensor_copy(ids_f, ids)
                    self.settle(V.tensor_tensor(cand[:, 0], spread(vals[:, 0, :], 2, TOPK), spread(vals[:, 1, :], 1, TOPK), ALU.add))

                def best_sums(self):
                    table = cand[:, 0].rearrange("p i j -> p (i j)")
                    self.largest8([best], [pos], [table], slice(0, 8), True)
                    self.largest8([best], [pos], [table], slice(8, 16), False)
                    self.link(V.tensor_copy(den[:, 0:1], best[:, 0:1]))
                    V.tensor_scalar(best, best, den[:, 0:1], None, ALU.subtract).then_inc(exp_in, 1)

                def experts_and_gates(self):
                    V.tensor_scalar(half_u[:, 0, :], pos, 4, None, ALU.logical_shift_right)
                    self.link(V.tensor_scalar(half_u[:, 1, :], pos, 15, None, ALU.bitwise_and))
                    self.link(V.tensor_copy(half_f, half_u))
                    onehot = cand.rearrange("p s i j -> p (s i) j")
                    self.link(V.tensor_tensor(onehot, spread(half_f.rearrange("p s k -> p (s k)"), 2, TOPK),
                                              spread(iota, 1, 2 * TOPK), ALU.is_equal))
                    self.link(V.tensor_tensor(cand, cand, spread(ids_f, 2, TOPK), ALU.mult))
                    self.link(V.tensor_reduce(e12.rearrange("p s k -> p (s k)"), onehot, AX.X, ALU.add))
                    dve.wait_ge(exp_out, self.head + self.t * PH + 1)
                    V.scalar_tensor_tensor(idx[:, bass.ds(self.column, TOPK)], e12[:, 0, :], float(NKEY), e12[:, 1, :], ALU.mult, ALU.add)
                    self.link(V.tensor_reduce(den[:, 0:1], best, AX.X, ALU.add))
                    self.link(V.reciprocal(den[:, 0:1], den[:, 0:1]))
                    V.tensor_scalar(gate[:, bass.ds(self.column, TOPK)], best, den[:, 0:1], None, ALU.mult).then_inc(chosen, 1)
                    dve.wait_ge(chosen, self.head + self.t * PH + 1)
                    assert self.step == STEPS, self.step

            def multiply_u(t, pair, slot):
                dve.wait_ge(row_in[slot], (pair + 2 * t * PAIRS + 1) * 16)
                one = dots[:, bass.ds(pair * (2 * SLOTS) + (slot + t * NE), 1)]
                V.scalar_tensor_tensor(rows[slot], rows[slot], 1.0, xn[:, t, :], ALU.mult, ALU.mult, accum_out=one)\
                    .then_inc((used0, used1)[slot // SLOTS], 1)

            def add_v(t, pair, quarter):
                for s in (quarter * 2, quarter * 2 + 1):
                    dve.wait_ge(row_in[s], (pair + (2 * t + 1) * PAIRS + 1) * 16)
                    dve.wait_ge(used0, (pair + (2 * t + 1) * PAIRS) * SLOTS + s)
                    x = m.x[:, t, :]
                    V.scalar_tensor_tensor(x, rows[s], dots[:, bass.ds(pair * (2 * SLOTS) + (s + t * NE), 1)], x, ALU.mult, ALU.add)\
                        .then_inc(used0, 1)

            LEAD = 2
            for head in range(LEAD):
                h = Head(0, head)
                h.first_halves()
                h.sums()
                h.best_sums()
                h.experts_and_gates()
            for t in range(TT):
                heads_left = PAIRS - LEAD if t == 0 else 0
                if t == 0:
                    with dve.Fori(0, heads_left) as pair:
                        slots = list(range(2 * SLOTS))
                        h = Head(0, pair + LEAD, lambda: slots and multiply_u(0, pair, slots.pop(0)))
                        h.first_halves()
                        h.sums()
                        h.best_sums()
                        h.experts_and_gates()
                        for slot in slots:
                            multiply_u(0, pair, slot)
                with dve.Fori(heads_left, PAIRS) as pair:
                    for slot in range(2 * SLOTS):
                        multiply_u(t, pair, slot)
                dve.wait_ge(gelu, t + 1)
                mine = slice(t * NE, t * NE + NE)
                V.tensor_tensor(dots[:, mine], dots[:, mine], gate[:, mine], ALU.mult).then_inc(gated, 1)
                dve.wait_ge(gated, t + 1)
                with dve.Fori(0, PAIRS) as pair:
                    h = Head(t + 1, pair)
                    add_v(t, pair, 0)
                    if t + 1 < TT:
                        h.first_halves()
                    add_v(t, pair, 1)
                    if t + 1 < TT:
                        h.sums()
                    add_v(t, pair, 2)
                    if t + 1 < TT:
                        h.best_sums()
                    add_v(t, pair, 3)
                    if t + 1 < TT:
                        h.experts_and_gates()
                dve.wait_ge(used0, (2 * t + 2) * PAIRS * SLOTS)
                dve.wait_ge(used1, (2 * t + 2) * PAIRS * SLOTS)
                V.tensor_tensor(m.x[:, t, :].rearrange("p (b n) -> p b n", b=2), m.x[:, t, :].rearrange("p (b n) -> p b n", b=2),
                                m.PS[:, 4:6, :], ALU.add).then_inc(added, 1)


def final_norm(nc, m, out):
    with region(nc, "final_ssq", TT) as ssq, stage(nc, "final", "squares mean root normed stored dve") as \
            (squares, mean, root, normed, stored, dve_chain), nc.Block() as block:
        @block.scalar
        def _(act):
            for t in range(TT):
                nc.scalar.activation(m.y[:, t, :], m.x[:, t, :], ACT.Square, accum_out=ssq[:, t:t + 1]).then_inc(squares, 1)
            act.wait_ge(mean, 1)
            nc.scalar.activation(ssq, ssq, ACT.Sqrt).then_inc(root, 1)

        @block.vector
        def _(dve):
            link = chain(dve, dve_chain)
            V = nc.vector
            dve.wait_ge(squares, TT)
            V.tensor_scalar(ssq, ssq, 1.0 / D, EPS, ALU.mult, ALU.add).then_inc(mean, 1)
            dve.wait_ge(root, 1)
            link(V.reciprocal(ssq, ssq))
            for t in range(TT):
                V.scalar_tensor_tensor(m.x[:, t, :], m.x[:, t, :], ssq[:, t:t + 1], m.row("final"), ALU.mult, ALU.mult)\
                    .then_inc(normed, 1)

        @block.sync
        def _(sp):
            for t in range(TT):
                sp.wait_ge(normed, t + 1)
                sp.dma_start(out[0, t * P:t * P + P, :], m.x[:, t, :]).then_inc(stored, 16)
            sp.wait_ge(stored, 16 * TT)


def second_block(nc, m, w, out):
    load_columns(nc, m, w["cols_2"], NCOL2)
    m.table = (COLS2, ROWS2)
    with region(nc, "mem", 2, D) as mem:
        hybrid_mixer(nc, m, w, mem)
        cross_attention(nc, m, w, mem)
    peer(nc, m, w)
    final_norm(nc, m, out)


def build(nc, w, out):
    ctx = ExitStack()
    with ctx:
        def sb(name, n, parts=P):
            return ctx.enter_context(nc.sbuf_tensor(name, [parts, n], F32))[:, :]

        m = Memory()
        m.PS = ctx.enter_context(nc.psum_tensor("PS", [P, 8, 512], F32))[:, :, :]
        m.x = sb("x", TT * D).rearrange("p (t n) -> p t n", t=TT)
        m.H = sb("H", DK * SEQ)
        m.hT = m.H.rearrange("p (k n) -> p k n", k=DK)
        m.y = m.H.rearrange("p (t n) -> p t n", t=TT)
        m.cols = sb("cols", max(NCOL, NCOL2))
        m.rows = sb("rows", max(NROW, NROW2))
        m.ident, m.ones = sb("ident", P), sb("ones", P)
        m.upper, m.strict_upper, m.strict_lower = (sb(n, P) for n in ("upper", "strict_upper", "strict_lower"))
        m.upper8, m.lower8 = sb("upper8", P), sb("lower8", P)
        m.upper64, m.strict_upper64 = sb("upper64", P), sb("strict_upper64", P)
        m.same = {b: sb(f"same{b}", P) for b in (8, 16, 32, 64)}
        m.merge = {b: sb(f"merge{b}", P) for b in (8, 16, 32, 64)}
        m.window = sb("window", 4 * P).rearrange("p (n k) -> p n k", n=2)
        m.pick = sb("pick", 4 * P, parts=4).rearrange("p (h n) -> p h n", h=4)
        m.cos, m.sin = (sb(n, TT * 8).rearrange("p (t j) -> p t j", t=TT) for n in ("cos", "sin"))
        m.table = (COLS, ROWS)
        m.col = lambda name: m.cols[:, m.table[0][name][0]:m.table[0][name][1]]
        m.row = lambda name: m.rows[:, m.table[1][name][0]:m.table[1][name][1]]

        constants(nc, m, w["x"])
        rope_tables(nc, m, w["positions"].rearrange("z (t p) -> p (z t)", p=P), Arena(m.H))
        with region(nc, "p", TT, D_PLE) as pt, nc.Fori(0, DEPTH) as l:
            first_layer(nc, m, w, l, pt)
        second_block(nc, m, w, out)





def columns(parts):
    import numpy as np
    out = []
    for a in parts:
        L = a.shape[0]
        out.append(a.reshape(L, -1, P).transpose(0, 2, 1) if a.shape[-1] >= P
                   else np.pad(a.reshape(L, -1, 1), ((0, 0), (0, P - a.shape[-1]), (0, 0))))
    return np.ascontiguousarray(np.concatenate(out, axis=2))


def taps_last(a):
    L, W, C = a.shape
    return a.reshape(L, W, C // P, P).transpose(0, 2, 1, 3).reshape(L, -1)


def layout(i):
    import numpy as np
    w = {n: i[n] for n in ("x", "positions", "w_ffn1_in", "w_ffn1_out", "w_in", "rwkv_w_up", "rwkv_a_up", "rwkv_g_up",
                           "w_out", "w_ffn2_in", "w_ffn2_out", "w_ple_gate", "w_ple_proj")}
    w["p"] = i["p"].reshape(DEPTH, SEQ, D_PLE)
    w["cols"] = columns([i["ln_ffn1_pre"], i["ln_mix_pre"], i["ln_ffn2_pre"], i["ln_ple_pre"], taps_last(i["mlstm_conv"]),
                         i["rwkv_mu"], i["rwkv_w0"], i["rwkv_a0"], i["rwkv_k_k"], i["rwkv_k_a"],
                         i["rwkv_r_k"].reshape(DEPTH, -1)])
    w["rows"] = np.concatenate([i["ln_ffn1_post"], i["ln_mix_post"], i["ln_ffn2_post"], i["ln_ple_post"], i["mlstm_norm"],
                                i["rwkv_ln_w"], i["rwkv_ln_b"], i["attn_sinks"], i["mlstm_i_bias"], i["mlstm_f_bias"]], axis=1)
    for n in ("w_in", "w_out", "xattn_wq", "xattn_wkv", "xattn_wo", "peer_wq", "peer_u", "peer_v"):
        w[n + "_2"] = i[n + "_2"][0]
    w["mem_2"] = i["mem_2"][0]
    w["lru_w_2"] = np.stack([i["lru_wa_2"][0], i["lru_wx_2"][0]]).reshape(2, 4, 2 * HD, HD)
    w["subkeys_2"] = np.ascontiguousarray(i["peer_subkeys_2"][0].reshape(16, NKEY, P).transpose(2, 0, 1))
    w["cols_2"] = columns([i["norm_mix_w_2"], i["norm_xattn_w_2"], i["norm_mem_w_2"], i["norm_ffn_w_2"],
                           taps_last(i["conv_qkv_w_2"]), taps_last(i["lru_conv_w_2"]), i["lru_conv_b_2"], i["lru_ba_2"],
                           i["lru_bx_2"], i["lru_lambda_2"]])[0]
    w["rows_2"] = np.concatenate([i["gdn_a_log_2"], i["gdn_dt_bias_2"], i["gdn_norm_w_2"], i["norm_ffn_w_2"], i["norm_final_w_2"].reshape(1, -1)],
                                 axis=1)
    return w


def kernel(**inputs):
    import numpy as np
    import concourse.bacc as bacc
    from concourse.bass_utils import run_bass_kernel_spmd

    nc = bacc.Bacc("TRN2", target_bir_lowering=False, num_devices=1)
    arrays, w = {}, {}
    for name, a in layout({n: np.asarray(a) for n, a in inputs.items()}).items():
        a = np.ascontiguousarray(a)
        arrays[f"in_{name}"] = a
        w[name] = nc.dram_tensor(f"in_{name}", a.shape, mybir.dt.from_np(a.dtype), kind="ExternalInput").ap()
    out = nc.dram_tensor("out_x", (1, SEQ, D), F32, kind="ExternalOutput").ap()
    build(nc, w, out)
    got = run_bass_kernel_spmd(nc, [arrays], core_ids=[0])
    return got.results[0]["out_x"]
```
